# Optimizing a Trainium2 kernel written in Bass

```python
import jax, jax.numpy as jnp
from jax import lax
import numpy as np

D_MODEL = 1024
BATCH = 1
SEQ = 2048
DEPTH = 1
DEC_BATCH = 1
DEC_SEQ = 64
PAST_LEN = 4096

CHUNK = 64
MIX_DIM = D_MODEL
POOL_DIM = MIX_DIM // 4
POOL_WINDOWS = (2, 4, 8, 16)
POOL_GROUPS = len(POOL_WINDOWS)
POOL_GC = POOL_DIM // POOL_GROUPS
POOL_HIST = max(POOL_WINDOWS) - 1
ATTN_DIM = MIX_DIM - POOL_DIM
HEAD_DIM = 64
N_HEADS = ATTN_DIM // HEAD_DIM
GQA = 4
N_KV = N_HEADS // GQA
KV_DIM = N_KV * HEAD_DIM
IN_DIM = POOL_DIM + ATTN_DIM + 2 * KV_DIM
WINDOW = 128
N_BAND = WINDOW // CHUNK + 1
ALIBI_MAX = 8.0
D_FF = -(-8 * D_MODEL // (3 * 256)) * 256
EPS = 1e-6
NEG = -1e30

kernel_name = 'hybrid_pool_swa_stream_step'

def rms_norm(x, g):
    xf = x.astype(jnp.float32)
    y = xf * lax.rsqrt(jnp.mean(xf * xf, axis=-1, keepdims=True) + EPS)
    return (y * g.astype(jnp.float32)).astype(x.dtype)

def alibi_slopes():
    h = jnp.arange(N_HEADS, dtype=jnp.float32) + 1.0
    return (2.0 ** (-ALIBI_MAX * h / N_HEADS)).reshape(N_KV, GQA)

def mixer_inputs(x, norm_g, w_in, q_norm, k_norm):
    B, L, _ = x.shape
    z = rms_norm(x, norm_g) @ w_in
    u = z[..., :POOL_DIM]
    q = z[..., POOL_DIM:POOL_DIM + ATTN_DIM].reshape(B, L, N_KV, GQA, HEAD_DIM)
    k = z[..., POOL_DIM + ATTN_DIM:POOL_DIM + ATTN_DIM + KV_DIM].reshape(B, L, N_KV, HEAD_DIM)
    v = z[..., POOL_DIM + ATTN_DIM + KV_DIM:].reshape(B, L, N_KV, HEAD_DIM)
    return u, rms_norm(q, q_norm), rms_norm(k, k_norm), v

def pool_mix(u, prev, pos0, w_pool, pool_scale):
    B, L, C = u.shape
    ext = jnp.concatenate([prev.astype(u.dtype), u], axis=1)
    pos_ext = pos0 - POOL_HIST + jnp.arange(L + POOL_HIST)
    ext_f = ext.astype(jnp.float32) * (pos_ext >= 0).astype(jnp.float32)[None, :, None]
    cs = jnp.concatenate([jnp.zeros((B, 1, C), jnp.float32), jnp.cumsum(ext_f, axis=1)], axis=1)
    pos = pos0 + jnp.arange(L)
    base = POOL_HIST + 1
    parts = []
    for g, w in enumerate(POOL_WINDOWS):
        sl = slice(g * POOL_GC, (g + 1) * POOL_GC)
        win = cs[:, base:base + L, sl] - cs[:, base - w:base - w + L, sl]
        cnt = jnp.minimum(pos + 1, w).astype(jnp.float32)
        parts.append(win / cnt[None, :, None])
    d = (jnp.concatenate(parts, axis=-1) - u.astype(jnp.float32)).reshape(B, L, POOL_GROUPS, POOL_GC)
    out = jnp.einsum('blgc,gce->blge', d, w_pool.astype(jnp.float32)).reshape(B, L, C)
    out = out * pool_scale.astype(jnp.float32)
    return out.astype(u.dtype), ext[:, -POOL_HIST:]

def band_attention(q, k, v, q_pos, k_pos, sinks):
    s = jnp.einsum('bnqkgd,bnskd->bnkgqs', q.astype(jnp.float32), k.astype(jnp.float32)) * (HEAD_DIM ** -0.5)
    dist = jnp.abs(q_pos[:, :, None] - k_pos[:, None, :]).astype(jnp.float32)
    s = s - alibi_slopes()[None, None, :, :, None, None] * dist[None, :, None, None]
    q_start = (q_pos // CHUNK) * CHUNK
    kp = k_pos[:, None, :]
    valid = (kp >= 0) & (kp >= q_start[:, :, None] - WINDOW) & (kp < q_start[:, :, None] + CHUNK)
    s = jnp.where(valid[None, :, None, None], s, NEG)
    sink = sinks.astype(jnp.float32).reshape(N_KV, GQA)[None, None, :, :, None, None]
    m = jnp.maximum(jnp.max(s, axis=-1, keepdims=True), sink)
    p = jnp.exp(s - m)
    denom = jnp.sum(p, axis=-1, keepdims=True) + jnp.exp(sink - m)
    o = jnp.einsum('bnkgqs,bnskd->bnqkgd', p / denom, v.astype(jnp.float32))
    return o.astype(q.dtype)

def attn_prompt(q, k, v, sinks):
    B, L = q.shape[:2]
    nc = L // CHUNK
    qb = q.reshape(B, nc, CHUNK, N_KV, GQA, HEAD_DIM)
    pad = jnp.zeros((B, WINDOW, N_KV, HEAD_DIM), k.dtype)
    kc = jnp.concatenate([pad, k], axis=1).reshape(B, nc + N_BAND - 1, CHUNK, N_KV, HEAD_DIM)
    vc = jnp.concatenate([pad.astype(v.dtype), v], axis=1).reshape(B, nc + N_BAND - 1, CHUNK, N_KV, HEAD_DIM)
    kb = jnp.concatenate([kc[:, i:i + nc] for i in range(N_BAND)], axis=2)
    vb = jnp.concatenate([vc[:, i:i + nc] for i in range(N_BAND)], axis=2)
    starts = jnp.arange(nc)[:, None] * CHUNK
    q_pos = starts + jnp.arange(CHUNK)[None, :]
    k_pos = starts - WINDOW + jnp.arange(N_BAND * CHUNK)[None, :]
    o = band_attention(qb, kb, vb, q_pos, k_pos, sinks).reshape(B, L, ATTN_DIM)
    return o, k[:, -WINDOW:], v[:, -WINDOW:]

def attn_sample(q, k, v, cache_k, cache_v, sinks):
    B, L = q.shape[:2]
    kall = jnp.concatenate([cache_k.astype(k.dtype), k], axis=1)
    vall = jnp.concatenate([cache_v.astype(v.dtype), v], axis=1)
    q_pos = PAST_LEN + jnp.arange(L)
    k_pos = jnp.concatenate([PAST_LEN - WINDOW + jnp.arange(WINDOW), q_pos])
    o = band_attention(q[:, None], kall[:, None], vall[:, None], q_pos[None], k_pos[None], sinks)
    return o.reshape(B, L, ATTN_DIM), kall[:, -WINDOW:], vall[:, -WINDOW:]

def block_out(x, pool_o, attn_o, w_out, norm_ffn, w_gate, w_up, w_down):
    h = x + jnp.concatenate([pool_o, attn_o], axis=-1) @ w_out
    hn = rms_norm(h, norm_ffn)
    return h + (jax.nn.silu(hn @ w_gate) * (hn @ w_up)) @ w_down

def setup_inputs(seed: int = 0) -> dict:
    key = jax.random.key(seed)
    ks = jax.random.split(key, 20)
    n = jax.random.normal
    f = jnp.float32
    return {
        'x_prompt': n(ks[0], (BATCH, SEQ, D_MODEL), f),
        'x_sample': n(ks[1], (DEC_BATCH, DEC_SEQ, D_MODEL), f),
        'cache_pool': n(ks[2], (DEPTH, DEC_BATCH, POOL_HIST, POOL_DIM), f),
        'cache_k': n(ks[3], (DEPTH, DEC_BATCH, WINDOW, N_KV, HEAD_DIM), f),
        'cache_v': n(ks[4], (DEPTH, DEC_BATCH, WINDOW, N_KV, HEAD_DIM), f),
        'norm_mix': 1.0 + 0.05 * n(ks[5], (DEPTH, D_MODEL), f),
        'w_in': n(ks[6], (DEPTH, D_MODEL, IN_DIM), f) * D_MODEL ** -0.5,
        'w_pool': n(ks[7], (DEPTH, POOL_GROUPS, POOL_GC, POOL_GC), f) * POOL_GC ** -0.5,
        'pool_scale': 1.0 + 0.05 * n(ks[8], (DEPTH, POOL_DIM), f),
        'q_norm': 1.0 + 0.05 * n(ks[9], (DEPTH, HEAD_DIM), f),
        'k_norm': 1.0 + 0.05 * n(ks[10], (DEPTH, HEAD_DIM), f),
        'sinks': 0.5 * n(ks[11], (DEPTH, N_HEADS), f),
        'w_out': n(ks[12], (DEPTH, MIX_DIM, D_MODEL), f) * MIX_DIM ** -0.5,
        'norm_ffn': 1.0 + 0.05 * n(ks[13], (DEPTH, D_MODEL), f),
        'w_gate': n(ks[14], (DEPTH, D_MODEL, D_FF), f) * D_MODEL ** -0.5,
        'w_up': n(ks[15], (DEPTH, D_MODEL, D_FF), f) * D_MODEL ** -0.5,
        'w_down': n(ks[16], (DEPTH, D_FF, D_MODEL), f) * D_FF ** -0.5,
    }

def reference(x_prompt, x_sample, cache_pool, cache_k, cache_v, norm_mix, w_in, w_pool, pool_scale,
              q_norm, k_norm, sinks, w_out, norm_ffn, w_gate, w_up, w_down):
    hp, hs = x_prompt, x_sample
    pp_l, kp_l, vp_l, ps_l, ks_l, vs_l = [], [], [], [], [], []
    for l in range(DEPTH):
        u, q, k, v = mixer_inputs(hp, norm_mix[l], w_in[l], q_norm[l], k_norm[l])
        prev0 = jnp.zeros((hp.shape[0], POOL_HIST, POOL_DIM), u.dtype)
        pool_o, pool_st = pool_mix(u, prev0, 0, w_pool[l], pool_scale[l])
        attn_o, k_st, v_st = attn_prompt(q, k, v, sinks[l])
        hp = block_out(hp, pool_o, attn_o, w_out[l], norm_ffn[l], w_gate[l], w_up[l], w_down[l])
        pp_l.append(pool_st); kp_l.append(k_st); vp_l.append(v_st)
        u, q, k, v = mixer_inputs(hs, norm_mix[l], w_in[l], q_norm[l], k_norm[l])
        pool_o, pool_st = pool_mix(u, cache_pool[l], PAST_LEN, w_pool[l], pool_scale[l])
        attn_o, k_st, v_st = attn_sample(q, k, v, cache_k[l], cache_v[l], sinks[l])
        hs = block_out(hs, pool_o, attn_o, w_out[l], norm_ffn[l], w_gate[l], w_up[l], w_down[l])
        ps_l.append(pool_st); ks_l.append(k_st); vs_l.append(v_st)
    return (hp, hs, jnp.stack(pp_l), jnp.stack(kp_l), jnp.stack(vp_l),
            jnp.stack(ps_l), jnp.stack(ks_l), jnp.stack(vs_l))


_drawn_inputs = setup_inputs


def setup_inputs(seed=0):
    import zlib

    import numpy as np

    out = dict(_drawn_inputs(seed))
    spreads = {}
    factors = {'q_norm': 5.909, 'sinks': 45.84, 'pool_scale': 3.103}
    for name, (base, spread) in spreads.items():
        noise = np.random.default_rng([zlib.crc32(name.encode()), seed]).standard_normal(out[name].shape)
        drawn = base * np.exp(spread * noise) if base else spread * noise
        out[name] = __import__('jax').numpy.asarray(drawn.astype(out[name].dtype))
    for name, factor in factors.items():
        out[name] = (out[name] * factor).astype(out[name].dtype)
    return out
```

```python
from contextlib import ExitStack

import numpy as np

import concourse.bass as bass
from concourse import mybir

F32 = mybir.dt.float32
F32R = mybir.dt.float32r
ALU = mybir.AluOpType
ACT = mybir.ActivationFunctionType
AX = mybir.AxisListType

PART = 128
D_MODEL = 1024
KT = D_MODEL // PART
SEQ = 2048
DEC = 64
POOL_DIM = 256
N_KV = 3
GQA = 4
N_HEADS = N_KV * GQA
HD = 64
ATTN_DIM = N_HEADS * HD
KV_DIM = N_KV * HD
D_FF = 2816
HIST = 15
EPS = 1e-6
U0, Q0, K0, V0 = 0, POOL_DIM, POOL_DIM + ATTN_DIM, POOL_DIM + ATTN_DIM + KV_DIM
POOL_WINDOWS = (2, 4, 8, 16)

PARTS = 3
NT = (6, 6, 5)
TILE0 = (0, 6, 12)
TMAX = 6 * PART
SAMPLE_TILE = SEQ // PART
GROUPS = D_FF // 256
OUT_GROUPS = D_MODEL // 256
D_GROUPS = OUT_GROUPS + GROUPS
RING1 = 12 + 2 * GROUPS
RING2 = 2 * OUT_GROUPS + 4 * GROUPS
HALO = 16

SLABS = [("u", 0, U0), ("u", 1, U0 + 128), ("k", 0, K0), ("k", 1, K0 + 128)] + [
    ("q", j, Q0 + 128 * j) for j in range(6)]


class Shape:

    def __init__(self, p):
        self.p, self.nt = p, NT[p]
        self.rows = [DEC if TILE0[p] + t == SAMPLE_TILE else PART for t in range(self.nt)]
        self.T = sum(self.rows)
        self.NB = self.T // 2
        self.has_sample = p == PARTS - 1
        before = sum(NT[:p])
        self.x0 = 2 * before
        self.z0 = sum(n + 20 for n in NT[:p])
        self.o0 = 16 * p
        self.a0 = 3 * before
        self.d0 = 2 * D_GROUPS * before
        self.g0 = 4 * GROUPS * p
        self.d_of = 2 * self.nt

    def cuts(self, nb):
        a, b = nb * self.NB, (nb + 1) * self.NB
        s = self.T - DEC
        if self.has_sample and a < s < b:
            return [(a, s), (s, b)]
        return [(a, b)]

    def kcol(self, tok):
        return PART + tok + (PART if self.has_sample and tok >= self.T - DEC else 0)

    def ucol(self, tok):
        return HALO + tok + (HALO if self.has_sample and tok >= self.T - DEC else 0)

    def slot(self, t):
        return self.kcol(PART * t) // PART

    def keys(self, t):
        if TILE0[self.p] + t == 0:
            return PART, 2 * PART
        if TILE0[self.p] + t == SAMPLE_TILE:
            return 0, PART + DEC
        return 0, 2 * PART


def build(nc, x_prompt, x_sample, cache_pool, cache_k, cache_v, norm_mix, w_in, w_pool, pool_scale,
          q_norm, k_norm, sinks, w_out, norm_ffn, w_gate, w_up, w_down,
          c_bias, c_ident, c_ones, c_inv,
          y_prompt, y_sample, np_prompt, nk_prompt, nv_prompt, np_sample, nk_sample, nv_sample):
    ctx = ExitStack()
    with ctx:
        def sb(name, shape, dt=F32, scope=ctx):
            return scope.enter_context(nc.sbuf_tensor(name, shape, dt))

        def sem(name):
            return ctx.enter_context(nc.semaphore(name))

        ps = ctx.enter_context(nc.psum_tensor("ps", [PART, 8, 512], F32))

        xt_hi = sb("xt_hi", [PART, KT, TMAX], F32R)
        xt_lo = sb("xt_lo", [PART, KT, TMAX], F32R)
        h = sb("h", [PART, 6, D_MODEL])
        raw1 = sb("raw1", [PART, 2, 1024])
        w1_hi = sb("w1_hi", [PART, 2, 1024], F32R)
        w1_lo = sb("w1_lo", [PART, 2, 1024], F32R)
        g_mix = sb("g_mix", [PART, D_MODEL])
        g_ffn = sb("g_ffn", [PART, D_MODEL])
        bias = sb("bias", [PART, N_HEADS, 256])
        ident = sb("ident", [PART, PART])
        headsum = sb("headsum", [PART, PART])
        wpool = sb("wpool", [PART, 2, PART])
        inv = sb("inv", [PART, 2, HALO])
        pscale = sb("pscale", [PART, 2])
        qg = sb("qg", [PART, 1])
        kg = sb("kg", [PART, 1])
        sink = sb("sink", [PART, N_HEADS])
        nsink = sb("nsink", [PART, N_HEADS])
        eps = sb("eps", [PART, 1])
        mark = sb("mark", [1, 2])
        ss = sb("ss", [PART, 16])
        rstd = sb("rstd", [PART, 16])
        negmax = sb("negmax", [PART, 2, GQA])
        esink = sb("esink", [PART, 2, GQA])
        den = sb("den", [PART, 2, GQA])
        rden = sb("rden", [PART, 2, GQA])
        k_tail = sb("k_tail", [PART, N_KV, PART])
        v_tail = sb("v_tail", [PART, KV_DIM])
        u_tail = sb("u_tail", [PART, 2, 2, HALO])

        with ExitStack() as attend:
            s_sb = sb("s_sb", [PART, 2, GQA, 256], scope=attend)
            pt_sb = sb("pt_sb", [PART, 2, 2, GQA * PART], scope=attend)
            zs = sb("zs", [PART, 2, TMAX // 2], scope=attend)
            sq = sb("sq", [PART, 2, TMAX // 2], scope=attend)
            rr = sb("rr", [PART, 2, TMAX // 2], scope=attend)
            qt_sb = sb("qt_sb", [PART, 2, 2, TMAX], scope=attend)
            kt_sb = sb("kt_sb", [PART, N_KV, PART + TMAX], scope=attend)
            v_sb = sb("v_sb", [PART, 7, KV_DIM], scope=attend)
            ut_sb = sb("ut_sb", [PART, 2, HALO + TMAX], scope=attend)
            win = sb("win", [PART, 2, HALO + TMAX], scope=attend)
            atok = sb("atok", [PART, 6, ATTN_DIM], scope=attend)
        xn = s_sb.rearrange("p b h k -> p b (h k)")
        ck_st = pt_sb[:, 0, 0, 0:2 * KV_DIM].rearrange("p (g e d) -> p g e d", g=N_KV, e=2)
        cp_st = pt_sb[:, 1, 0, 0:POOL_DIM]
        k_st = zs.rearrange("p b n -> p (b n)")
        u_st = sq.rearrange("p b n -> p (b n)")
        with ExitStack() as ffn:
            act_hi = sb("act_hi", [PART, 2, 2, TMAX], F32R, scope=ffn)
            act_lo = sb("act_lo", [PART, 2, 2, TMAX], F32R, scope=ffn)
            sg = sb("sg", [PART, 2, TMAX // 2], scope=ffn)
            aa = sb("aa", [PART, 2, TMAX // 2], scope=ffn)
            raw2 = sb("raw2", [PART, 4, 1024], scope=ffn)
            w2_hi = sb("w2_hi", [PART, 4, 1024], F32R, scope=ffn)
            w2_lo = sb("w2_lo", [PART, 4, 1024], F32R, scope=ffn)

        const_loaded = sem("const_loaded")
        wpool_zero = sem("wpool_zero")
        const_ready = sem("const_ready")
        x_loaded = [sem(f"x_loaded{t}") for t in range(6)]
        raw1_loaded = [sem(f"raw1_loaded{i}") for i in range(2)]
        raw2_loaded = [sem(f"raw2_loaded{i}") for i in range(4)]
        cache_loaded = sem("cache_loaded")
        split1 = sem("split1")
        split2 = sem("split2")
        pool_step = sem("pool_step")
        act_step = sem("act_step")
        dve_step = sem("dve_step")
        rstd_ready = sem("rstd_ready")
        xn_ready = sem("xn_ready")
        tp_ready = sem("tp_ready")
        tp_hi = sem("tp_hi")
        tp_free = sem("tp_free")
        z_ready = sem("z_ready")
        z_free = sem("z_free")
        sq_ready = sem("sq_ready")
        ss_ready = sem("ss_ready")
        ss_free = sem("ss_free")
        r_ready = sem("r_ready")
        fin_done = sem("fin_done")
        halo_ready = sem("halo_ready")
        tails_saved = sem("tails_saved")
        pool_ready = sem("pool_ready")
        qk_ready = sem("qk_ready")
        sc_free = sem("sc_free")
        nm_ready = sem("nm_ready")
        e_ready = sem("e_ready")
        pt_ready = sem("pt_ready")
        pta_done = sem("pta_done")
        ptb_done = sem("ptb_done")
        pv_ready = sem("pv_ready")
        o_done = sem("o_done")
        d_ready = sem("d_ready")
        d_free = sem("d_free")
        g_ready = sem("g_ready")
        u_ready = sem("u_ready")
        silu_done = sem("silu_done")
        a_done = sem("a_done")
        ah_done = sem("ah_done")
        al_done = sem("al_done")
        y_stored = [sem(f"y_stored{t}") for t in range(6)]
        state_stored = sem("state_stored")

        N_CONST = 14
        shapes = [Shape(p) for p in range(PARTS)]
        TP_CACHE, TP_STATE = N_KV + 1, 3
        tp_total = [6 * s.nt + 4 + (TP_CACHE + TP_STATE if s.has_sample else 0) for s in shapes]

        w_in_k = w_in[0].rearrange("(k p) n -> p k n", p=PART)
        w_gate_k = w_gate[0].rearrange("(k p) n -> p k n", p=PART)
        w_up_k = w_up[0].rearrange("(k p) n -> p k n", p=PART)

        def tile_dram(prompt, sample, t):
            return sample[0] if t == SAMPLE_TILE else prompt[0, PART * t:PART * (t + 1), :]

        def need(eng, semaphore, value):
            if not isinstance(value, int) or value > 0:
                eng.wait_ge(semaphore, value)

        block = ctx.enter_context(nc.Block())

        @block.sync
        def _(sp):
            def load_const(dst, src):
                sp.dma_start(dst, src, allow_slow_non_contiguous=True).then_inc(const_loaded, 16)

            def ring1(s, block_id, dst_cols, src):
                b = RING1 * s.p + block_id
                need(sp, split1, b - 1)
                sp.dma_start(dst_cols, src).then_inc(raw1_loaded[b % 2], 16)

            def load_slab(s, n):
                ring1(s, 2 + n, raw1[:, n % 2].rearrange("p (k m) -> p k m", k=KT),
                      w_in_k[:, :, SLABS[n][2]:SLABS[n][2] + PART])

            def load_out(s, j):
                for c in range(2):
                    b = 2 * j + c
                    need(sp, split2, RING2 * s.p + b - 3)
                    sp.dma_start(raw2[:, b % 4], w_out[0, PART * b:PART * (b + 1), :])\
                        .then_inc(raw2_loaded[b % 4], 16)

            def load_gate_up(s, j):
                for n in range(4):
                    need(sp, split2, RING2 * s.p + 2 * OUT_GROUPS + 4 * j + n - 3)
                    w = (w_gate_k, w_up_k)[n % 2]
                    sp.dma_start(raw2[:, n].rearrange("p (k m) -> p k m", k=KT),
                                 w[:, :, bass.ds(256 * j + PART * (n // 2), PART)])\
                        .then_inc(raw2_loaded[n], 16)

            def load_down(s, j):
                for c in range(2):
                    need(sp, split1, RING1 * s.p + 12 + 2 * j + c - 1)
                    sp.dma_start(raw1[:, c], w_down[0, bass.ds(256 * j + PART * c, PART), :])\
                        .then_inc(raw1_loaded[c], 16)

            for s in shapes:
                for c in range(2):
                    ring1(s, c, raw1[:, c, 0:4 * KV_DIM].rearrange("p (k m) -> p k m", k=4),
                          w_in_k[:, 4 * c:4 * c + 4, V0:V0 + KV_DIM])
                for t in range(s.nt):
                    need(sp, y_stored[t], 16 * s.p)
                    sp.dma_start(h[0:s.rows[t], t], tile_dram(x_prompt, x_sample, TILE0[s.p] + t))\
                        .then_inc(x_loaded[t], 16)
                if s.p == 0:
                    sp.wait_ge(wpool_zero, 1)
                    load_const(g_mix[:, :], norm_mix.partition_broadcast(PART)[:, 0, :])
                    load_const(ident[:, :], c_ident)
                    for e in range(2):
                        load_const(qg[HD * e:HD * (e + 1), :], q_norm.rearrange("a d -> d a"))
                        load_const(kg[HD * e:HD * (e + 1), :], k_norm.rearrange("a d -> d a"))
                    load_const(headsum[:, :], c_ones)
                    load_const(sink[:, :], sinks.partition_broadcast(PART)[:, 0, :])
                    load_const(pscale[:, :], pool_scale[0].rearrange("(s p) -> p s", p=PART))
                    for e in range(2):
                        load_const(wpool[HD * e:HD * (e + 1), :, HD * e:HD * (e + 1)],
                                   w_pool[0].rearrange("(s e) c d -> e c s d", e=2)[e])
                    load_const(inv[:, :, :], c_inv)
                    load_const(g_ffn[:, :], norm_ffn.partition_broadcast(PART)[:, 0, :])
                    load_const(bias[:, :, :], c_bias)
                if s.has_sample:
                    sp.wait_ge(d_ready, s.d0)
                    for e in range(2):
                        sp.dma_start(ck_st[:, :, e, :], cache_k[0, 0]).then_inc(cache_loaded, 16)
                    sp.dma_start(cp_st[0:HIST, :], cache_pool[0, 0]).then_inc(cache_loaded, 16)
                    sp.dma_start(v_sb[:, s.slot(4) - 1, :], cache_v[0, 0].rearrange("r g d -> r (g d)"))\
                        .then_inc(cache_loaded, 16)
                for n in range(len(SLABS)):
                    load_slab(s, n)
                sp.wait_ge(tp_free, sum(tp_total[:s.p + 1]) - 2 * s.nt)
                for j in range(OUT_GROUPS):
                    load_out(s, j)
                load_gate_up(s, 0)
                with sp.Fori(0, (GROUPS - 1) // 2) as i:
                    load_gate_up(s, 2 * i + 1)
                    load_down(s, 2 * i)
                    load_gate_up(s, 2 * i + 2)
                    load_down(s, 2 * i + 1)
                load_down(s, GROUPS - 1)

        @block.gpsimd
        def _(pool):
            steps = [0]

            def link(ins):
                steps[0] += 1
                ins.then_inc(pool_step, 1)
                pool.wait_ge(pool_step, steps[0])

            hi_steps = [0]

            def split(raw, hi, lo, done, step_no, size=1024):
                nc.gpsimd.tensor_copy(hi[:, 0:size], raw[:, 0:size]).then_inc(split_hi, 1)
                pool.wait_ge(split_hi, step_no)
                nc.gpsimd.tensor_tensor(lo[:, 0:size], raw[:, 0:size], hi[:, 0:size].bitcast(F32),
                                        ALU.subtract).then_inc(done, 1)

            def split_ring1(s, block_id, step_no, use, size=1024):
                b = block_id % 2
                pool.wait_ge(raw1_loaded[b], use)
                split(raw1[:, b], w1_hi[:, b], w1_lo[:, b], split1, step_no, size)

            def split_ring2(s, slot, step_no, use):
                pool.wait_ge(raw2_loaded[slot], use)
                split(raw2[:, slot], w2_hi[:, slot], w2_lo[:, slot], split2, step_no)

            def gate_copy():
                nc.gpsimd.tensor_tensor(mark[:, 1:2], mark[:, 0:1], mark[:, 0:1], ALU.add)

            def split_gate_up(s, j, step0):
                for n in range(4):
                    c, which = n // 2, (g_ready, u_ready)[n % 2]
                    if isinstance(j, int) and j == 0:
                        pool.wait_ge(d_ready, s.d0 + s.d_of * (OUT_GROUPS - 1 + c))
                    else:
                        pool.wait_ge(which, s.g0 + 4 * (j - 1) + 2 * c + 2)
                    pool.wait_ge(raw2_loaded[n], 16 * (RING2 // 4 * s.p + 2 + j + 1))
                    gate_copy()
                    split(raw2[:, n], w2_hi[:, n], w2_lo[:, n], split2, step0 + n + 1)

            def split_down(s, j, step0):
                for c in range(2):
                    if isinstance(j, int) and j == 0:
                        pool.wait_ge(z_ready, s.z0 + s.nt + 20)
                    else:
                        pool.wait_ge(d_ready, s.d0 + s.d_of * (OUT_GROUPS + j))
                    pool.wait_ge(raw1_loaded[c], 16 * (RING1 // 2 * s.p + 6 + j + 1))
                    gate_copy()
                    split(raw1[:, c], w1_hi[:, c], w1_lo[:, c], split1, step0 + c + 1)

            def windows(s):
                n = HALO + s.T + (HALO if s.has_sample else 0)
                pool.wait_ge(z_free, s.z0 + s.nt + 4)
                pool.wait_ge(tails_saved, s.p + 1)
                for b in range(2):
                    u, a, c = ut_sb[:, b], win[:, 0], win[:, 1]
                    lo_w, hi_w = POOL_WINDOWS[2 * b], POOL_WINDOWS[2 * b + 1]
                    src, dst, w = u, a, 1
                    while 2 * w <= lo_w:
                        w *= 2
                        link(nc.gpsimd.tensor_tensor(dst[:, w:n], src[:, w:n], src[:, w - w // 2:n - w // 2],
                                                     ALU.add))
                        src, dst = dst, (c if dst is a else a)
                    w *= 2
                    link(nc.gpsimd.tensor_tensor(dst[HD:PART, w:n], src[HD:PART, w:n],
                                                 src[HD:PART, w - w // 2:n - w // 2], ALU.add))
                    for e, summed in ((0, src), (1, dst)):
                        r = slice(HD * e, HD * (e + 1))
                        width = (lo_w, hi_w)[e]
                        first = HALO
                        if s.p == 0:
                            link(nc.gpsimd.tensor_tensor(summed[r, HALO:2 * HALO], summed[r, HALO:2 * HALO],
                                                         inv[r, b, :], ALU.mult))
                            first = 2 * HALO
                        link(nc.gpsimd.tensor_scalar(summed[r, first:n], summed[r, first:n], 1.0 / width, None,
                                                     ALU.mult))
                        ins = nc.gpsimd.tensor_tensor(u[r, HALO:n], summed[r, HALO:n], u[r, HALO:n],
                                                      ALU.subtract)
                        if b == 1 and e == 1:
                            ins.then_inc(pool_ready, 1)
                        else:
                            link(ins)

            split_hi = sem("split_hi")
            nc.gpsimd.memset(wpool[:, :, :], 0.0).then_inc(wpool_zero, 1)
            link(nc.gpsimd.memset(mark[:, :], 0.0))
            pool.wait_ge(const_loaded, 16 * N_CONST)
            done = 0
            for s in shapes:
                b1 = RING1 * s.p
                for c in range(2):
                    need(pool, d_ready, s.d0)
                    split_ring1(s, c, done + 1, 16 * ((b1 + c) // 2 + 1), 4 * KV_DIM)
                    done += 1
                for n in range(len(SLABS)):
                    pool.wait_ge(z_ready, s.z0 + s.nt + (2 * (n - 2) + 2 if n >= 2 else 0))
                    split_ring1(s, 2 + n, done + 1, 16 * ((b1 + 2 + n) // 2 + 1))
                    done += 1
                windows(s)
                pool.wait_ge(tp_free, sum(tp_total[:s.p + 1]) - 2 * s.nt)
                for b in range(2 * OUT_GROUPS):
                    if b >= 4:
                        pool.wait_ge(d_ready, s.d0 + s.d_of * ((b - 4) // 2 + 1))
                    split_ring2(s, b % 4, done + 1, 16 * (RING2 // 4 * s.p + b // 4 + 1))
                    done += 1
                split_gate_up(s, 0, done)
                done += 4
                with pool.Fori(0, (GROUPS - 1) // 2) as i:
                    split_gate_up(s, 2 * i + 1, done + 12 * i)
                    split_down(s, 2 * i, done + 12 * i + 4)
                    split_gate_up(s, 2 * i + 2, done + 12 * i + 6)
                    split_down(s, 2 * i + 1, done + 12 * i + 10)
                done += 12 * ((GROUPS - 1) // 2)
                split_down(s, GROUPS - 1, done)
                done += 2

        @block.tensor
        def _(pe):
            tp = [0]

            def split_products(out, w_hi, w_lo, m_hi, m_lo, first, last):
                nc.tensor.matmul(out, w_hi, m_hi, start=first, stop=False)
                nc.tensor.matmul(out, w_hi, m_lo, start=False, stop=False)
                return nc.tensor.matmul(out, w_lo, m_hi, start=False, stop=last)

            def tp_bank():
                need(pe, tp_free, tp[0] - 3)
                tp[0] += 1
                return ps[:, 4 + (tp[0] - 1) % 4]

            def transposed(src, cols, rows):
                bank = tp_bank()
                for n, c in enumerate(cols):
                    last = nc.tensor.transpose(bank[:, n * rows:(n + 1) * rows],
                                               src[0:rows, PART * c:PART * (c + 1)], ident[0:rows, 0:rows])
                last.then_inc(tp_ready, 1)

            def norm_transposes(s, x0):
                for t in range(s.nt):
                    pe.wait_ge(xn_ready, x0 + t + 1)
                    for half in range(2):
                        transposed(xn[:, (x0 + t) % 2], range(4 * half, 4 * half + 4), s.rows[t])

            def cache_transposes(s):
                pe.wait_ge(cache_loaded, 16 * 4)
                for g in range(N_KV):
                    bank = tp_bank()
                    nc.tensor.transpose(bank[:, 0:PART], ck_st[:, g].rearrange("p e d -> p (e d)"),
                                        ident[:, :]).then_inc(tp_ready, 1)
                bank = tp_bank()
                for b in range(2):
                    last = nc.tensor.transpose(bank[:, HALO * b:HALO * b + HIST],
                                               cp_st[0:HIST, PART * b:PART * (b + 1)], ident[0:HIST, 0:HIST])
                last.then_inc(tp_ready, 1)

            def state_transposes(s):
                for c0, rows in ((s.kcol(3 * PART), PART), (s.kcol(4 * PART), DEC)):
                    bank = tp_bank()
                    for g in range(N_KV):
                        last = nc.tensor.transpose(bank[0:rows, PART * g:PART * (g + 1)],
                                                   kt_sb[:, g, c0:c0 + rows], ident[:, :])
                    last.then_inc(tp_ready, 1)
                bank = tp_bank()
                for w in range(2):
                    for b in range(2):
                        n = 2 * w + b
                        last = nc.tensor.transpose(bank[0:HIST, PART * n:PART * (n + 1)],
                                                   u_tail[:, w, b, 1:HALO], ident[:, :])
                last.then_inc(tp_ready, 1)

            def v_tiles(s):
                for c in range(2):
                    pe.wait_ge(split1, RING1 * s.p + c + 1)
                for t in range(s.nt):
                    zi = s.z0 + t
                    need(pe, z_free, zi - 1)
                    out = ps[0:s.rows[t], zi % 2, 0:KV_DIM]
                    tok = slice(PART * t, PART * t + s.rows[t])
                    for k in range(KT):
                        cols = slice(KV_DIM * (k % 4), KV_DIM * (k % 4 + 1))
                        last = split_products(out, xt_hi[:, k, tok], xt_lo[:, k, tok],
                                              w1_hi[:, k // 4, cols], w1_lo[:, k // 4, cols],
                                              k == 0, k == KT - 1)
                    last.then_inc(z_ready, 1)

            def slab_unit(s, n, nb):
                zi = s.z0 + s.nt + 2 * n + nb
                pe.wait_ge(split1, RING1 * s.p + 2 + n + 1)
                need(pe, z_free, zi - 1)
                out = ps[:, zi % 2, 0:s.NB]
                tok = slice(nb * s.NB, (nb + 1) * s.NB)
                for k in range(KT):
                    cols = slice(PART * k, PART * (k + 1))
                    last = split_products(out, w1_hi[:, n % 2, cols], w1_lo[:, n % 2, cols],
                                          xt_hi[:, k, tok], xt_lo[:, k, tok], k == 0, k == KT - 1)
                last.then_inc(z_ready, 1)

            def head_sums(s, oi):
                pe.wait_ge(sq_ready, oi + 1)
                need(pe, ss_free, oi)
                nc.tensor.matmul(ps[:, 2, 0:s.NB], headsum[:, :], sq[:, oi % 2, 0:s.NB],
                                 start=True, stop=True).then_inc(ss_ready, 1)

            def scores(s, g, t):
                ai, rows = s.a0 + s.nt * g + t, s.rows[t]
                c0, c1 = s.keys(t)
                need(pe, sc_free, ai)
                k0 = PART * (s.slot(t) - 1)
                for hh in range(GQA):
                    e, j = hh % 2, hh // 2
                    last = nc.tensor.matmul(ps[0:rows, 4 + e, 256 * j + c0:256 * j + c1],
                                            qt_sb[HD * e:HD * (e + 1), g % 2, j, PART * t:PART * t + rows],
                                            kt_sb[HD * e:HD * (e + 1), g, k0 + c0:k0 + c1],
                                            start=True, stop=True)
                last.then_inc(qk_ready, 1)

            pta = [0]

            def prob_transposes(s, g, t):
                ai, rows = s.a0 + s.nt * g + t, s.rows[t]
                c0, c1 = s.keys(t)
                pe.wait_ge(e_ready, ai + 1)
                need(pe, pta_done, pta[0])
                need(pe, ptb_done, ai)
                for half in range(2):
                    a, b = max(c0, PART * half), min(c1, PART * (half + 1))
                    if a >= b:
                        continue
                    pta[0] += half == 0
                    for hh in range(GQA):
                        last = nc.tensor.transpose(ps[0:b - a, 6 + half, rows * hh:rows * (hh + 1)],
                                                   s_sb[0:rows, ai % 2, hh, a:b], ident[0:rows, 0:rows])
                last.then_inc(pt_ready, 1)

            def weighted_values(s, g, t, pta_seen):
                ai, rows = s.a0 + s.nt * g + t, s.rows[t]
                c0, c1 = s.keys(t)
                need(pe, pta_done, pta_seen)
                pe.wait_ge(ptb_done, ai + 1)
                need(pe, o_done, ai)
                for hh in range(GQA):
                    for half in range(2):
                        a, b = max(c0, PART * half), min(c1, PART * (half + 1))
                        if a >= b:
                            continue
                        last = nc.tensor.matmul(ps[0:rows, 3, HD * hh:HD * (hh + 1)],
                                                pt_sb[0:b - a, ai % 2, half, rows * hh:rows * (hh + 1)],
                                                v_sb[0:b - a, s.slot(t) - 1 + half, HD * g:HD * (g + 1)],
                                                start=a == c0, stop=half == 1)
                last.then_inc(pv_ready, 1)

            def attend(s, g):
                scores(s, g, 0)
                seen = []
                for t in range(s.nt):
                    if t + 1 < s.nt:
                        scores(s, g, t + 1)
                    if g + 1 < N_KV and t < 4:
                        slab_unit(s, 4 + 2 * (g + 1) + t // 2, t % 2)
                    if g + 1 < N_KV and 1 <= t <= 4:
                        head_sums(s, s.o0 + 4 + 4 * (g + 1) + t - 1)
                    prob_transposes(s, g, t)
                    seen.append(pta[0])
                    if t >= 1:
                        weighted_values(s, g, t - 1, seen[t - 1])
                weighted_values(s, g, s.nt - 1, seen[-1])

            def mix(s):
                pe.wait_ge(pool_ready, s.p + 1)
                for b in range(2):
                    for nb in range(2):
                        bank = tp_bank()
                        for a, e in s.cuts(nb):
                            last = nc.tensor.matmul(bank[:, a - nb * s.NB:e - nb * s.NB], wpool[:, b, :],
                                                    ut_sb[:, b, s.ucol(a):s.ucol(a) + e - a],
                                                    start=True, stop=True)
                        last.then_inc(tp_ready, 1)
                for t in range(s.nt):
                    pe.wait_ge(o_done, s.a0 + 2 * s.nt + t + 1)
                    for half in range(2):
                        transposed(atok[:, t], range(3 * half, 3 * half + 3), s.rows[t])

            def add_group(s, d0, bank0, w_hi, w_lo, m_hi, m_lo):
                for t in range(s.nt):
                    tok = slice(PART * t, PART * t + s.rows[t])
                    for nh in range(2):
                        di = d0 + 2 * t + nh
                        need(pe, d_free, di - 3)
                        out = ps[0:s.rows[t], (2 * t + nh + bank0) % 4, :]
                        cols = slice(512 * nh, 512 * (nh + 1))
                        for c in range(2):
                            last = split_products(out, m_hi[:, c, tok], m_lo[:, c, tok],
                                                  w_hi[:, c, cols], w_lo[:, c, cols], c == 0, c == 1)
                        last.then_inc(d_ready, 1)

            def gate_up(s, j):
                for c in range(2):
                    for nb in range(2):
                        gi = s.g0 + 4 * j + 2 * c + nb
                        tok = slice(nb * s.NB, (nb + 1) * s.NB)
                        for which, (ready, freed) in enumerate(((g_ready, silu_done), (u_ready, a_done))):
                            slot = 2 * c + which
                            pe.wait_ge(split2, RING2 * s.p + 2 * OUT_GROUPS + 4 * j + slot + 1)
                            need(pe, freed, gi - 1)
                            out = ps[:, 4 + 2 * which + nb, 0:s.NB]
                            for k in range(KT):
                                cols = slice(PART * k, PART * (k + 1))
                                last = split_products(out, w2_hi[:, slot, cols], w2_lo[:, slot, cols],
                                                      xt_hi[:, k, tok], xt_lo[:, k, tok],
                                                      k == 0, k == KT - 1)
                            last.then_inc(ready, 1)

            def down(s, j, parity):
                pe.wait_ge(split1, RING1 * s.p + 12 + 2 * j + 2)
                pe.wait_ge(al_done, s.g0 + 4 * j + 4)
                add_group(s, s.d0 + s.d_of * (OUT_GROUPS + j), s.d_of * parity, w1_hi, w1_lo,
                          act_hi[:, parity], act_lo[:, parity])

            pe.wait_ge(const_loaded, 16 * N_CONST)
            for s in shapes:
                need(pe, a_done, s.g0)
                norm_transposes(s, s.x0)
                if s.has_sample:
                    cache_transposes(s)
                pe.wait_ge(tp_free, tp[0])
                need(pe, d_free, s.d0)
                v_tiles(s)
                for n in range(4):
                    for nb in range(2):
                        slab_unit(s, n, nb)
                        if 2 * n + nb >= 5:
                            head_sums(s, s.o0 + 2 * n + nb - 5)
                for n in range(4, 6):
                    for nb in range(2):
                        slab_unit(s, n, nb)
                        head_sums(s, s.o0 + 2 * n + nb - 5)
                head_sums(s, s.o0 + 7)
                need(pe, halo_ready, s.p)
                for g in range(N_KV):
                    pe.wait_ge(fin_done, s.o0 + 8 + 4 * g)
                    attend(s, g)
                mix(s)
                if s.has_sample:
                    state_transposes(s)
                pe.wait_ge(tp_free, tp[0])
                for j in range(OUT_GROUPS):
                    pe.wait_ge(split2, RING2 * s.p + 2 * j + 2)
                    slots = slice(2 * (j % 2), 2 * (j % 2) + 2)
                    add_group(s, s.d0 + s.d_of * j, s.d_of * j, w2_hi[:, slots], w2_lo[:, slots],
                              xt_hi[:, 2 * j:2 * j + 2], xt_lo[:, 2 * j:2 * j + 2])
                norm_transposes(s, s.x0 + s.nt)
                pe.wait_ge(tp_free, tp[0])
                gate_up(s, 0)
                with pe.Fori(0, (GROUPS - 1) // 2) as i:
                    gate_up(s, 2 * i + 1)
                    down(s, 2 * i, 0)
                    gate_up(s, 2 * i + 2)
                    down(s, 2 * i + 1, 1)
                down(s, GROUPS - 1, 0)

        @block.scalar
        def _(act):
            steps, tp = [0], [0]

            def link(ins):
                steps[0] += 1
                ins.then_inc(act_step, 1)
                act.wait_ge(act_step, steps[0])

            def tp_copy(dst, src, scale=1.0):
                tp[0] += 1
                act.wait_ge(tp_ready, tp[0])
                nc.scalar.activation(dst, src, ACT.Copy, scale=scale).then_inc(tp_hi, 1)

            def tp_unit(k0, nk, tok):
                n = tok.stop - tok.start
                tp_copy(xt_hi[:, k0:k0 + nk, tok],
                        ps[:, 4 + tp[0] % 4, 0:nk * n].rearrange("p (k t) -> p k t", k=nk))

            def row_norm(s, x0, col0, ready):
                tp_start = tp[0]
                for t in range(s.nt):
                    rows, c = s.rows[t], col0 + t
                    ready(t)
                    if t >= 2:
                        act.wait_ge(tp_ready, tp_start + 2 * (t - 1))
                    link(nc.scalar.activation(xn[0:rows, (x0 + t) % 2], h[0:rows, t], ACT.Square,
                                              accum_out=ss[0:rows, c:c + 1]))
                    link(nc.scalar.activation(ss[0:rows, c:c + 1], ss[0:rows, c:c + 1], ACT.Ln,
                                              bias=eps[0:rows, :], scale=1.0 / D_MODEL))
                    nc.scalar.activation(rstd[0:rows, c:c + 1], ss[0:rows, c:c + 1], ACT.Exp,
                                         scale=-0.5).then_inc(rstd_ready, 1)
                    if t >= 1:
                        norm_copies(s, t - 1)
                norm_copies(s, s.nt - 1)

            def norm_copies(s, t):
                for half in range(2):
                    tp_unit(4 * half, 4, slice(PART * t, PART * t + s.rows[t]))

            def slab_read(s, n, nb):
                kind, j, _ = SLABS[n]
                zi = s.z0 + s.nt + 2 * n + nb
                oi = s.o0 + 2 * n + nb - 4
                z = ps[:, zi % 2, 0:s.NB]
                act.wait_ge(z_ready, zi + 1)
                if kind == "u":
                    for a, e in s.cuts(nb):
                        last = nc.scalar.activation(ut_sb[:, j, s.ucol(a):s.ucol(a) + e - a],
                                                    z[:, a - nb * s.NB:e - nb * s.NB], ACT.Copy)
                    last.then_inc(z_free, 1)
                    return
                need(act, ss_ready, oi - 1)
                nc.scalar.activation(sq[:, oi % 2, 0:s.NB], z, ACT.Square).then_inc(sq_ready, 1)
                if kind == "k":
                    need(act, fin_done, oi - 1)
                    dst, scale = zs[:, oi % 2, 0:s.NB], kg[:, :]
                else:
                    g = j // 2
                    if g >= 2:
                        act.wait_ge(qk_ready, s.a0 + s.nt * (g - 1))
                    dst, scale = qt_sb[:, g % 2, j % 2, nb * s.NB:(nb + 1) * s.NB], qg[:, :]
                nc.scalar.activation(dst, z, ACT.Copy, scale=scale).then_inc(z_free, 1)

            def head_rstd(s, oi):
                act.wait_ge(ss_ready, oi + 1)
                need(act, fin_done, oi - 1)
                r = rr[:, oi % 2, 0:s.NB]
                nc.scalar.activation(r, ps[:, 2, 0:s.NB], ACT.Ln, bias=eps[:, :],
                                     scale=1.0 / HD).then_inc(ss_free, 1)
                act.wait_ge(ss_free, oi + 1)
                nc.scalar.activation(r, r, ACT.Exp, scale=-0.5).then_inc(r_ready, 1)

            def exps(s, g, t):
                ai, rows = s.a0 + s.nt * g + t, s.rows[t]
                c0, c1 = s.keys(t)
                act.wait_ge(nm_ready, ai + 1)
                for hh in range(GQA):
                    p = s_sb[0:rows, ai % 2, hh, c0:c1]
                    nc.scalar.activation(p, p, ACT.Exp, bias=negmax[0:rows, ai % 2, hh:hh + 1],
                                         accum_out=den[0:rows, ai % 2, hh:hh + 1])
                nc.scalar.activation(esink[0:rows, ai % 2, :], esink[0:rows, ai % 2, :],
                                     ACT.Exp).then_inc(e_ready, 1)

            def prob_copy(s, g, t):
                ai, rows = s.a0 + s.nt * g + t, s.rows[t]
                if s.keys(t)[0] > 0:
                    return
                act.wait_ge(pt_ready, ai + 1)
                need(act, pv_ready, ai - 1)
                nc.scalar.activation(pt_sb[:, ai % 2, 0, 0:GQA * rows], ps[:, 6, 0:GQA * rows],
                                     ACT.Copy).then_inc(pta_done, 1)

            def attend(s, g):
                if g == 0:
                    exps(s, g, 0)
                for t in range(s.nt):
                    if t + 1 < s.nt:
                        exps(s, g, t + 1)
                    if g + 1 < N_KV and t < 4:
                        slab_read(s, 4 + 2 * (g + 1) + t // 2, t % 2)
                    if g + 1 < N_KV and 1 <= t <= 4:
                        head_rstd(s, s.o0 + 4 + 4 * (g + 1) + t - 1)
                    prob_copy(s, g, t)
                if g + 1 < N_KV:
                    exps(s, g + 1, 0)

            def gate_unit(s, j, n, parity):
                gi = s.g0 + 4 * j + n
                act.wait_ge(g_ready, gi + 1)
                need(act, a_done, gi - 1)
                nc.scalar.activation(sg[:, n % 2, 0:s.NB], ps[:, 4 + n % 2, 0:s.NB],
                                     ACT.Silu).then_inc(silu_done, 1)
                if n >= 1:
                    high_part(s, j, n - 1, parity)

            def high_part(s, j, n, parity):
                act.wait_ge(a_done, s.g0 + 4 * j + n + 1)
                nc.scalar.activation(act_hi[:, parity, n // 2, (n % 2) * s.NB:(n % 2 + 1) * s.NB],
                                     aa[:, n % 2, 0:s.NB], ACT.Copy).then_inc(ah_done, 1)

            def gates(s, j, parity):
                for n in range(4):
                    gate_unit(s, j, n, parity)
                high_part(s, j, 3, parity)

            def store_states(s):
                act.wait_ge(tp_free, tp[0])
                act.dma_start(nk_prompt[0, 0].rearrange("r g d -> r (g d)"), k_st[:, 0:KV_DIM])\
                    .then_inc(state_stored, 16)
                act.dma_start(nk_sample[0, 0, PART - DEC:PART].rearrange("r g d -> r (g d)"),
                              k_st[0:DEC, KV_DIM:2 * KV_DIM]).then_inc(state_stored, 16)
                act.dma_start(nk_sample[0, 0, 0:PART - DEC], cache_k[0, 0, DEC:PART])\
                    .then_inc(state_stored, 16)
                act.dma_start(nv_sample[0, 0, 0:PART - DEC], cache_v[0, 0, DEC:PART])\
                    .then_inc(state_stored, 16)
                act.dma_start(nv_prompt[0, 0].rearrange("r g d -> r (g d)"), v_tail[:, :])\
                    .then_inc(state_stored, 16)
                act.dma_start(nv_sample[0, 0, PART - DEC:PART].rearrange("r g d -> r (g d)"),
                              k_st[0:DEC, 2 * KV_DIM:3 * KV_DIM]).then_inc(state_stored, 16)
                act.dma_start(np_prompt[0, 0], u_st[0:HIST, 0:POOL_DIM]).then_inc(state_stored, 16)
                act.dma_start(np_sample[0, 0], u_st[0:HIST, POOL_DIM:2 * POOL_DIM])\
                    .then_inc(state_stored, 16)
                act.wait_ge(state_stored, 16 * 8)

            act.wait_ge(const_ready, 3)
            for s in shapes:
                nc.scalar.preload_act_table_set("natural_log_exp_and_others")
                need(act, d_ready, s.d0)
                row_norm(s, s.x0, 0, lambda t: act.wait_ge(x_loaded[t], 16 * (s.p + 1)))
                if s.has_sample:
                    c0 = PART * (s.slot(4) - 1)
                    for g in range(N_KV):
                        tp_copy(kt_sb[0:HD, g, c0:c0 + PART], ps[0:HD, 4 + tp[0] % 4, 0:PART])
                    u0 = s.ucol(s.T - DEC) - HIST
                    tp_copy(ut_sb[:, 0, u0:u0 + HIST], ps[:, 4 + tp[0] % 4, 0:HIST])
                for t in range(s.nt):
                    zi = s.z0 + t
                    act.wait_ge(z_ready, zi + 1)
                    nc.scalar.activation(v_sb[0:s.rows[t], s.slot(t), :], ps[0:s.rows[t], zi % 2, 0:KV_DIM],
                                         ACT.Copy).then_inc(z_free, 1)
                for n in range(6):
                    for nb in range(2):
                        slab_read(s, n, nb)
                        if 2 * n + nb >= 5:
                            head_rstd(s, s.o0 + 2 * n + nb - 5)
                head_rstd(s, s.o0 + 7)
                for g in range(N_KV):
                    attend(s, g)
                for b in range(2):
                    for nb in range(2):
                        tp_copy(xt_hi[:, b, nb * s.NB:(nb + 1) * s.NB], ps[:, 4 + tp[0] % 4, 0:s.NB],
                                scale=pscale[:, b:b + 1])
                for t in range(s.nt):
                    for half in range(2):
                        tp_unit(2 + 3 * half, 3, slice(PART * t, PART * t + s.rows[t]))
                if s.has_sample:
                    for n, rows in enumerate((PART, DEC)):
                        tp_copy(k_st[0:rows, KV_DIM * n:KV_DIM * n + 2 * HD].rearrange("p (g d) -> p g d", g=2),
                                ps[0:rows, 4 + tp[0] % 4, 0:2 * PART]
                                .rearrange("p (g d) -> p g d", g=2)[:, :, 0:HD])
                    tp_copy(u_st[0:HIST, 0:POOL_DIM], ps[0:HIST, 4 + tp[0] % 4, 0:POOL_DIM])
                    store_states(s)
                last = s.d0 + s.d_of * (OUT_GROUPS - 1)
                row_norm(s, s.x0 + s.nt, 8, lambda t: act.wait_ge(d_free, last + 2 * t + 2))
                nc.scalar.preload_act_table(ACT.Silu)
                gates(s, 0, 0)
                with act.Fori(0, (GROUPS - 1) // 2) as i:
                    gates(s, 2 * i + 1, 1)
                    gates(s, 2 * i + 2, 0)
                last = s.d0 + s.d_of * (D_GROUPS - 1)
                for t in range(s.nt):
                    act.wait_ge(d_free, last + 2 * t + 2)
                    act.dma_start(tile_dram(y_prompt, y_sample, TILE0[s.p] + t), h[0:s.rows[t], t])\
                        .then_inc(y_stored[t], 16)
            for t in range(6):
                act.wait_ge(y_stored[t], 16 * sum(t < n for n in NT))

        @block.vector
        def _(dve):
            steps, tp = [0], [0]

            def link(ins):
                steps[0] += 1
                ins.then_inc(dve_step, 1)
                dve.wait_ge(dve_step, steps[0])

            def tp_wait():
                tp[0] += 1
                dve.wait_ge(tp_hi, tp[0])
                return ps[:, 4 + (tp[0] - 1) % 4]

            def tp_unit(k0, nk, tok):
                bank, n = tp_wait(), tok.stop - tok.start
                nc.vector.tensor_tensor(xt_lo[:, k0:k0 + nk, tok],
                                        bank[:, 0:nk * n].rearrange("p (k t) -> p k t", k=nk),
                                        xt_hi[:, k0:k0 + nk, tok].bitcast(F32), ALU.subtract)\
                    .then_inc(tp_free, 1)

            def norm_low(s, t):
                for half in range(2):
                    tp_unit(4 * half, 4, slice(PART * t, PART * t + s.rows[t]))

            def row_norm(s, x0, col0, weight):
                for t in range(s.nt):
                    rows = s.rows[t]
                    dve.wait_ge(rstd_ready, x0 + t + 1)
                    nc.vector.scalar_tensor_tensor(xn[0:rows, (x0 + t) % 2], h[0:rows, t],
                                                   rstd[0:rows, col0 + t:col0 + t + 1], weight[0:rows, :],
                                                   ALU.mult, ALU.mult).then_inc(xn_ready, 1)
                    if t >= 1:
                        norm_low(s, t - 1)
                norm_low(s, s.nt - 1)

            def normed(s, n, nb):
                kind, j, _ = SLABS[n]
                oi, zi = s.o0 + 2 * n + nb - 4, s.z0 + s.nt + 2 * n + nb
                dve.wait_ge(r_ready, oi + 1)
                dve.wait_ge(z_free, zi + 1)
                r = rr[:, oi % 2, 0:s.NB]
                if kind == "q":
                    q = qt_sb[:, j // 2 % 2, j % 2, nb * s.NB:(nb + 1) * s.NB]
                    nc.vector.tensor_tensor(q, q, r, ALU.mult).then_inc(fin_done, 1)
                    return
                z = zs[:, oi % 2, 0:s.NB]
                for g in ((0, 1), (2,))[j]:
                    src = slice(HD * (g % 2), HD * (g % 2 + 1))
                    for e in range(2):
                        for a, b in s.cuts(nb):
                            cols = slice(a - nb * s.NB, b - nb * s.NB)
                            last = nc.vector.tensor_tensor(
                                kt_sb[HD * e:HD * (e + 1), g, s.kcol(a):s.kcol(a) + b - a],
                                z[src, cols], r[src, cols], ALU.mult)
                last.then_inc(fin_done, 1)

            def restore_tails(s):
                nc.vector.tensor_copy(kt_sb[:, :, 0:PART], k_tail[:, :, :])
                nc.vector.tensor_copy(v_sb[:, 0, :], v_tail[:, :])
                nc.vector.tensor_copy(ut_sb[:, :, 0:HALO], u_tail[:, 0]).then_inc(halo_ready, 1)

            def save_tails(s):
                end = s.T - (DEC if s.has_sample else 0)
                dve.wait_ge(z_free, s.z0 + s.nt + 4)
                dve.wait_ge(fin_done, s.o0 + 4)
                nc.vector.tensor_copy(k_tail[:, :, :], kt_sb[:, :, end:end + PART])
                nc.vector.tensor_copy(v_tail[:, :], v_sb[:, end // PART, :])
                if s.has_sample:
                    c = s.ucol(s.T - DEC) + DEC
                    nc.vector.tensor_copy(u_tail[:, 1], ut_sb[:, :, c - HALO:c])
                    nc.vector.tensor_copy(k_st[0:DEC, 2 * KV_DIM:3 * KV_DIM], v_sb[0:DEC, s.slot(4), :])
                nc.vector.tensor_copy(u_tail[:, 0], ut_sb[:, :, end:end + HALO]).then_inc(tails_saved, 1)

            def softmax_top(s, g, t):
                ai, rows = s.a0 + s.nt * g + t, s.rows[t]
                c0, c1 = s.keys(t)
                b = ai % 2
                dve.wait_ge(qk_ready, ai + 1)
                need(dve, pt_ready, ai - 1)
                need(dve, e_ready, ai - 1)
                by_bank = "p (j e) k -> p j e k"
                nc.vector.tensor_tensor(
                    s_sb[0:rows, b].rearrange(by_bank, e=2)[:, :, :, c0:c1],
                    ps[0:rows, 4:6, :].rearrange("p e (j k) -> p j e k", j=2)[:, :, :, c0:c1],
                    bias[0:rows, GQA * g:GQA * (g + 1)].rearrange(by_bank, e=2)[:, :, :, c0:c1], ALU.add)\
                    .then_inc(sc_free, 1)
                dve.wait_ge(sc_free, ai + 1)
                link(nc.vector.tensor_reduce(negmax[0:rows, b, :], s_sb[0:rows, b, :, c0:c1], AX.X, ALU.max,
                                             negate=True))
                link(nc.vector.tensor_tensor(negmax[0:rows, b, :], negmax[0:rows, b, :],
                                             nsink[0:rows, GQA * g:GQA * (g + 1)], ALU.min))
                nc.vector.tensor_tensor(esink[0:rows, b, :], negmax[0:rows, b, :],
                                        sink[0:rows, GQA * g:GQA * (g + 1)], ALU.add).then_inc(nm_ready, 1)

            def prob_copy(s, g, t):
                ai, rows = s.a0 + s.nt * g + t, s.rows[t]
                keys = s.keys(t)[1] - PART
                dve.wait_ge(pt_ready, ai + 1)
                need(dve, pv_ready, ai - 1)
                nc.vector.tensor_copy(pt_sb[0:keys, ai % 2, 1, 0:GQA * rows],
                                      ps[0:keys, 7, 0:GQA * rows]).then_inc(ptb_done, 1)

            def denominators(s, g, t):
                ai, rows = s.a0 + s.nt * g + t, s.rows[t]
                b = ai % 2
                dve.wait_ge(e_ready, ai + 1)
                link(nc.vector.tensor_tensor(den[0:rows, b, :], den[0:rows, b, :], esink[0:rows, b, :], ALU.add))
                link(nc.vector.reciprocal(rden[0:rows, b, :], den[0:rows, b, :]))

            def outputs(s, g, t):
                ai, rows = s.a0 + s.nt * g + t, s.rows[t]
                dve.wait_ge(pv_ready, ai + 1)
                cols = slice(GQA * HD * g, GQA * HD * (g + 1))
                nc.vector.tensor_tensor(atok[0:rows, t, cols].rearrange("p (h d) -> p h d", h=GQA),
                                        ps[0:rows, 3, 0:GQA * HD].rearrange("p (h d) -> p h d", h=GQA),
                                        rden[0:rows, ai % 2, :].unsqueeze(2).to_broadcast([rows, GQA, HD]),
                                        ALU.mult).then_inc(o_done, 1)

            def attend(s, g):
                if g == 0:
                    softmax_top(s, g, 0)
                for t in range(s.nt):
                    if t + 1 < s.nt:
                        softmax_top(s, g, t + 1)
                    if g + 1 < N_KV and 1 <= t <= 4:
                        normed(s, 4 + 2 * (g + 1) + (t - 1) // 2, (t - 1) % 2)
                    prob_copy(s, g, t)
                    denominators(s, g, t)
                    if t >= 1:
                        outputs(s, g, t - 1)
                outputs(s, g, s.nt - 1)
                if g + 1 < N_KV:
                    softmax_top(s, g + 1, 0)

            def accumulate(s, d0, parity):
                for t in range(s.nt):
                    for nh in range(2):
                        rows, cols = s.rows[t], slice(512 * nh, 512 * (nh + 1))
                        dve.wait_ge(d_ready, d0 + 2 * t + nh + 1)
                        nc.vector.tensor_tensor(h[0:rows, t, cols],
                                                ps[0:rows, (2 * t + nh + s.d_of * parity) % 4, :],
                                                h[0:rows, t, cols], ALU.add).then_inc(d_free, 1)

            def activations(s, j, parity):
                for n in range(4):
                    gi = s.g0 + 4 * j + n
                    dve.wait_ge(silu_done, gi + 1)
                    dve.wait_ge(u_ready, gi + 1)
                    need(dve, ah_done, gi - 1)
                    need(dve, al_done, gi - 1)
                    nc.vector.tensor_tensor(aa[:, n % 2, 0:s.NB], ps[:, 6 + n % 2, 0:s.NB],
                                            sg[:, n % 2, 0:s.NB], ALU.mult).then_inc(a_done, 1)
                    if n >= 1:
                        low_part(s, j, n - 1, parity)
                low_part(s, j, 3, parity)

            def low_part(s, j, n, parity):
                dve.wait_ge(ah_done, s.g0 + 4 * j + n + 1)
                at = (slice(None), parity, n // 2, slice((n % 2) * s.NB, (n % 2 + 1) * s.NB))
                nc.vector.tensor_tensor(act_lo[at], aa[:, n % 2, 0:s.NB], act_hi[at].bitcast(F32),
                                        ALU.subtract).then_inc(al_done, 1)

            nc.vector.memset(eps[:, :], EPS).then_inc(const_ready, 1)
            dve.wait_ge(const_loaded, 16 * N_CONST)
            nc.vector.tensor_scalar(nsink[:, :], sink[:, :], -1.0, None, ALU.mult).then_inc(const_ready, 1)
            nc.vector.tensor_scalar(qg[:, :], qg[:, :], HD ** -0.5, None, ALU.mult).then_inc(const_ready, 1)
            link(nc.vector.memset(u_tail[:, :, :, :], 0.0))
            for s in shapes:
                need(dve, d_ready, s.d0)
                row_norm(s, s.x0, 0, g_mix)
                if s.p > 0:
                    restore_tails(s)
                else:
                    link(nc.vector.memset(ut_sb[:, :, 0:HALO], 0.0))
                if s.has_sample:
                    c0 = PART * (s.slot(4) - 1)
                    for g in range(N_KV):
                        bank = tp_wait()
                        nc.vector.tensor_copy(kt_sb[HD:PART, g, c0:c0 + PART], bank[HD:PART, 0:PART])\
                            .then_inc(tp_free, 1)
                    u0 = s.ucol(s.T - DEC) - HIST
                    nc.vector.memset(ut_sb[:, :, u0 - 1:u0], 0.0)
                    bank = tp_wait()
                    nc.vector.tensor_copy(ut_sb[:, 1, u0:u0 + HIST], bank[:, HALO:HALO + HIST])\
                        .then_inc(tp_free, 1)
                for n in range(2, 6):
                    for nb in range(2):
                        normed(s, n, nb)
                    if n == 3:
                        save_tails(s)
                for g in range(N_KV):
                    attend(s, g)
                for b in range(2):
                    for nb in range(2):
                        bank, tok = tp_wait(), slice(nb * s.NB, (nb + 1) * s.NB)
                        nc.vector.scalar_tensor_tensor(xt_lo[:, b, tok], bank[:, 0:s.NB], pscale[:, b:b + 1],
                                                       xt_hi[:, b, tok].bitcast(F32), ALU.mult,
                                                       ALU.subtract).then_inc(tp_free, 1)
                for t in range(s.nt):
                    for half in range(2):
                        tp_unit(2 + 3 * half, 3, slice(PART * t, PART * t + s.rows[t]))
                if s.has_sample:
                    for n, rows in enumerate((PART, DEC)):
                        bank = tp_wait()
                        nc.vector.tensor_copy(k_st[0:rows, KV_DIM * n + 2 * HD:KV_DIM * (n + 1)],
                                              bank[0:rows, 2 * PART:2 * PART + HD]).then_inc(tp_free, 1)
                    bank = tp_wait()
                    nc.vector.tensor_copy(u_st[0:HIST, POOL_DIM:2 * POOL_DIM],
                                          bank[0:HIST, POOL_DIM:2 * POOL_DIM]).then_inc(tp_free, 1)
                for j in range(OUT_GROUPS):
                    accumulate(s, s.d0 + s.d_of * j, j)
                row_norm(s, s.x0 + s.nt, 8, g_ffn)
                activations(s, 0, 0)
                down0 = s.d0 + s.d_of * OUT_GROUPS
                with dve.Fori(0, (GROUPS - 1) // 2) as i:
                    activations(s, 2 * i + 1, 1)
                    accumulate(s, down0 + s.d_of * (2 * i), 0)
                    activations(s, 2 * i + 2, 0)
                    accumulate(s, down0 + s.d_of * (2 * i + 1), 1)
                accumulate(s, down0 + s.d_of * (GROUPS - 1), 0)


def constants():
    slope = 2.0 ** (-8.0 * (np.arange(N_HEADS, dtype=np.float32) + 1.0) / N_HEADS)
    row, col = np.arange(PART)[:, None], np.arange(2 * PART)[None, :]
    dist = np.abs(row + PART - col).astype(np.float32)
    chunk = (row // 64) * 64
    valid = (col >= chunk) & (col < chunk + PART + 64)
    bias = np.where(valid[:, None, :], -slope.astype(np.float32)[None, :, None] * dist[:, None, :],
                    np.float32(-1e30)).astype(np.float32)
    ident = np.eye(PART, dtype=np.float32)
    heads = np.kron(np.eye(2, dtype=np.float32), np.ones((HD, HD), np.float32))
    width = np.repeat(np.array(POOL_WINDOWS, np.float32), 64).reshape(2, PART)
    count = np.minimum(np.arange(1, HALO + 1, dtype=np.float32)[None, None, :], width.T[:, :, None])
    return {"c_bias": bias, "c_ident": ident, "c_ones": heads, "c_inv": (1.0 / count).astype(np.float32)}


_INS = ['x_prompt', 'x_sample', 'cache_pool', 'cache_k', 'cache_v', 'norm_mix', 'w_in', 'w_pool', 'pool_scale',
        'q_norm', 'k_norm', 'sinks', 'w_out', 'norm_ffn', 'w_gate', 'w_up', 'w_down']
_OUTS = [(1, 2048, 1024), (1, 64, 1024), (1, 1, 15, 256), (1, 1, 128, 3, 64), (1, 1, 128, 3, 64),
         (1, 1, 15, 256), (1, 1, 128, 3, 64), (1, 1, 128, 3, 64)]


def kernel(**inputs):
    import concourse.bacc as bacc
    from concourse.bass_utils import run_bass_kernel_spmd

    nc = bacc.Bacc("TRN2", target_bir_lowering=False, num_devices=1)
    arrays, args = {}, []
    given = {name: np.ascontiguousarray(inputs[name]) for name in _INS} | constants()
    for name, a in given.items():
        arrays[f"in_{name}"] = a
        args.append(nc.dram_tensor(f"in_{name}", a.shape, mybir.dt.from_np(a.dtype), kind="ExternalInput").ap())
    for i, shape in enumerate(_OUTS):
        args.append(nc.dram_tensor(f"out_{i}", shape, F32, kind="ExternalOutput").ap())
    build(nc, *args)
    r = run_bass_kernel_spmd(nc, [arrays], core_ids=[0])
    return tuple(r.results[0][f"out_{i}"] for i in range(len(_OUTS)))
```

```python
from contextlib import ExitStack

import numpy as np

import concourse.bass as bass
from concourse import mybir

F32 = mybir.dt.float32
F32R = mybir.dt.float32r
ALU = mybir.AluOpType
ACT = mybir.ActivationFunctionType
AX = mybir.AxisListType

PART = 128
D_MODEL = 1024
KT = D_MODEL // PART
SEQ = 2048
DEC = 64
POOL_DIM = 256
N_KV = 3
GQA = 4
N_HEADS = N_KV * GQA
HD = 64
ATTN_DIM = N_HEADS * HD
KV_DIM = N_KV * HD
D_FF = 2816
HIST = 15
EPS = 1e-6
U0, Q0, K0, V0 = 0, POOL_DIM, POOL_DIM + ATTN_DIM, POOL_DIM + ATTN_DIM + KV_DIM
POOL_WINDOWS = (2, 4, 8, 16)

PARTS = 3
NT = (6, 6, 5)
TILE0 = (0, 6, 12)
TMAX = 6 * PART
SAMPLE_TILE = SEQ // PART
GROUPS = D_FF // 256
LOOPS = (GROUPS - 3) // 2
OUT_GROUPS = D_MODEL // 256
D_GROUPS = OUT_GROUPS + GROUPS
HALO = 16

SLABS = [("u", 0, U0), ("u", 1, U0 + 128), ("k", 0, K0), ("k", 1, K0 + 128)] + [
    ("q", j, Q0 + 128 * j) for j in range(6)]
EARLY = 6

V_ID, OUT_ID, DOWN_ID = EARLY, len(SLABS) + 2, len(SLABS) + 2 + 4
RING1 = DOWN_ID + 2 * (GROUPS - 1)
GATE_ID, LAST_ID = 4, 4 + 4 * GROUPS
RING2 = LAST_ID + 2
USES2 = (GROUPS + 2, GROUPS + 2, GROUPS + 1, GROUPS + 1)

LATE = 2 * (len(SLABS) - EARLY)
MEANS_AT = (3, 6)
MIX_AT, OUT_AT = 8, 10
SLOPES = [float(np.float32(2.0) ** np.float32(-8.0 * (h + 1) / N_HEADS)) for h in range(N_HEADS)]


def slab_id(m):
    return m if m < EARLY else m + 2


class Shape:

    def __init__(self, p):
        self.p, self.nt = p, NT[p]
        self.rows = [DEC if TILE0[p] + t == SAMPLE_TILE else PART for t in range(self.nt)]
        self.T = sum(self.rows)
        self.NB = self.T // 2
        self.units = [(g, t) for g in range(N_KV) for t in range(self.nt)]
        self.has_sample = p == PARTS - 1
        before = sum(NT[:p])
        self.x0 = 2 * before
        self.z0 = sum(n + 20 for n in NT[:p])
        self.o0 = 16 * p
        self.a0 = 3 * before
        self.d0 = 2 * D_GROUPS * before
        self.g0 = 4 * GROUPS * p
        self.d_of = 2 * self.nt

    def z_unit(self, m, nb):
        return self.z0 + 2 * m + nb + (self.nt if m >= EARLY else 0)

    def v_unit(self, t):
        return self.z0 + 2 * EARLY + t

    def oi(self, m, nb):
        return self.o0 + 2 * (m - 2) + nb

    def d_unit(self, group, t, nh=0):
        return self.d0 + self.d_of * group + 2 * t + nh

    def late_at(self, n):
        ahead = max(NT) - self.nt
        return range(n + ahead if n else 0, n + ahead + 1)

    def cuts(self, nb):
        a, b = nb * self.NB, (nb + 1) * self.NB
        s = self.T - DEC
        if self.has_sample and a < s < b:
            return [(a, s), (s, b)]
        return [(a, b)]

    def kcol(self, tok):
        return PART + tok + (PART if self.has_sample and tok >= self.T - DEC else 0)

    def ucol(self, tok):
        return HALO + tok + (HALO if self.has_sample and tok >= self.T - DEC else 0)

    def slot(self, t):
        return self.kcol(PART * t) // PART

    def keys(self, t):
        if TILE0[self.p] + t == 0:
            return PART, 2 * PART
        if TILE0[self.p] + t == SAMPLE_TILE:
            return 0, PART + DEC
        return 0, 2 * PART


def build(nc, x_prompt, x_sample, cache_pool, cache_k, cache_v, norm_mix, w_in, w_pool, pool_scale,
          q_norm, k_norm, sinks, w_out, norm_ffn, w_gate, w_up, w_down,
          c_dist, c_ident, c_ones, c_inv,
          y_prompt, y_sample, np_prompt, nk_prompt, nv_prompt, np_sample, nk_sample, nv_sample):
    ctx = ExitStack()
    with ctx:
        def sb(name, shape, dt=F32, scope=ctx):
            return scope.enter_context(nc.sbuf_tensor(name, shape, dt))

        def sem(name):
            return ctx.enter_context(nc.semaphore(name))

        ps = ctx.enter_context(nc.psum_tensor("ps", [PART, 8, 512], F32))

        xt_hi = sb("xt_hi", [PART, KT, TMAX], F32R)
        xt_lo = sb("xt_lo", [PART, KT, TMAX], F32R)
        h = sb("h", [PART, 6, D_MODEL])
        raw1 = sb("raw1", [PART, 2, 1024])
        w1_hi = sb("w1_hi", [PART, 2, 1024], F32R)
        w1_lo = sb("w1_lo", [PART, 2, 1024], F32R)
        g_mix = sb("g_mix", [PART, D_MODEL])
        g_ffn = sb("g_ffn", [PART, D_MODEL])
        dist = sb("dist", [PART, 256])
        ident = sb("ident", [PART, PART])
        headsum = sb("headsum", [PART, PART])
        wpool = sb("wpool", [PART, 2, PART])
        inv = sb("inv", [PART, 2, HALO])
        pscale = sb("pscale", [PART, 2])
        qg = sb("qg", [PART, 1])
        kg = sb("kg", [PART, 1])
        sink = sb("sink", [PART, N_HEADS])
        nsink = sb("nsink", [PART, N_HEADS])
        eps = sb("eps", [PART, 1])
        xload = sb("xload", [PART, 2, D_MODEL])
        xn = sb("xn", [PART, 2, D_MODEL])
        win = xn.rearrange("p b n -> p (b n)")[:, 0:2 * (HALO + TMAX)].rearrange("p (b n) -> p b n", b=2)
        ss = sb("ss", [PART, 16])
        rstd = sb("rstd", [PART, 16])
        negmax = sb("negmax", [PART, 2, GQA])
        esink = sb("esink", [PART, 2, GQA])
        den = sb("den", [PART, 2, GQA])
        rden = sb("rden", [PART, 2, GQA])
        k_tail = sb("k_tail", [PART, N_KV, PART])
        v_tail = sb("v_tail", [PART, KV_DIM])
        u_tail = sb("u_tail", [PART, 2, 2, HALO])

        with ExitStack() as attend:
            s_sb = sb("s_sb", [PART, 2, GQA, 256], scope=attend)
            pt_sb = sb("pt_sb", [PART, 2, 2, GQA * PART], scope=attend)
            zs = sb("zs", [PART, 2, TMAX // 2], scope=attend)
            sq = sb("sq", [PART, 2, TMAX // 2], scope=attend)
            rr = sb("rr", [PART, 2, TMAX // 2], scope=attend)
            qt_sb = sb("qt_sb", [PART, 2, 2, TMAX], scope=attend)
            kt_sb = sb("kt_sb", [PART, N_KV, PART + TMAX], scope=attend)
            v_sb = sb("v_sb", [PART, 7, KV_DIM], scope=attend)
            ut_sb = sb("ut_sb", [PART, 2, HALO + TMAX], scope=attend)
            atok = sb("atok", [PART, 6, ATTN_DIM], scope=attend)
        ck_st = pt_sb[:, 0, 0, 0:2 * KV_DIM].rearrange("p (g e d) -> p g e d", g=N_KV, e=2)
        cp_st = pt_sb[:, 1, 0, 0:POOL_DIM]
        k_st = zs.rearrange("p b n -> p (b n)")
        u_st = sq.rearrange("p b n -> p (b n)")
        with ExitStack() as ffn:
            act_hi = sb("act_hi", [PART, 2, 2, TMAX], F32R, scope=ffn)
            act_lo = sb("act_lo", [PART, 2, 2, TMAX], F32R, scope=ffn)
            sg = sb("sg", [PART, 2, TMAX // 2], scope=ffn)
            aa = sb("aa", [PART, 2, TMAX // 2], scope=ffn)
            raw2 = sb("raw2", [PART, 4, 1024], scope=ffn)
            w2_hi = sb("w2_hi", [PART, 4, 1024], F32R, scope=ffn)
            w2_lo = sb("w2_lo", [PART, 4, 1024], F32R, scope=ffn)

        ident_loaded = sem("ident_loaded")
        gmix_loaded = sem("gmix_loaded")
        const_loaded = sem("const_loaded")
        wpool_zero = sem("wpool_zero")
        const_ready = sem("const_ready")
        x_loaded = [sem(f"x_loaded{i}") for i in range(2)]
        h_loaded = [sem(f"h_loaded{t}") for t in range(6)]
        raw1_loaded = [sem(f"raw1_loaded{i}") for i in range(2)]
        raw2_loaded = [sem(f"raw2_loaded{i}") for i in range(4)]
        cache_loaded = sem("cache_loaded")
        hi_done = sem("hi_done")
        split1 = sem("split1")
        split2 = sem("split2")
        pool_step = sem("pool_step")
        act_step = sem("act_step")
        dve_step = sem("dve_step")
        rstd_ready = sem("rstd_ready")
        xn_ready = sem("xn_ready")
        tp_ready = sem("tp_ready")
        tp_hi = sem("tp_hi")
        tp_free = sem("tp_free")
        z_ready = sem("z_ready")
        z_free = sem("z_free")
        sq_ready = sem("sq_ready")
        ss_ready = sem("ss_ready")
        ss_free = sem("ss_free")
        r_ready = sem("r_ready")
        fin_done = sem("fin_done")
        halo_ready = sem("halo_ready")
        tails_saved = sem("tails_saved")
        windows_ready = sem("windows_ready")
        windows_used = sem("windows_used")
        m_ready = sem("m_ready")
        m_hi = sem("m_hi")
        m_free = sem("m_free")
        qk_ready = sem("qk_ready")
        sc_free = sem("sc_free")
        nm_ready = sem("nm_ready")
        e_ready = sem("e_ready")
        pt_ready = sem("pt_ready")
        pt_done = sem("pt_done")
        pv_ready = sem("pv_ready")
        o_done = sem("o_done")
        d_ready = sem("d_ready")
        d_free = sem("d_free")
        g_ready = sem("g_ready")
        u_ready = sem("u_ready")
        silu_done = sem("silu_done")
        a_done = sem("a_done")
        ah_done = sem("ah_done")
        al_done = sem("al_done")
        y_stored = [sem(f"y_stored{t}") for t in range(6)]
        state_stored = sem("state_stored")

        N_CONST = 12
        shapes = [Shape(p) for p in range(PARTS)]
        TP_CACHE, TP_STATE = N_KV + 1, 3
        tp_total = [6 * s.nt + (TP_CACHE + TP_STATE if s.has_sample else 0) for s in shapes]

        def mixed(s):
            return sum(tp_total[:s.p + 1]) - 2 * s.nt

        w_in_k = w_in[0].rearrange("(k p) n -> p k n", p=PART)
        w_gate_k = w_gate[0].rearrange("(k p) n -> p k n", p=PART)
        w_up_k = w_up[0].rearrange("(k p) n -> p k n", p=PART)

        def tile_dram(prompt, sample, t):
            return sample[0] if t == SAMPLE_TILE else prompt[0, PART * t:PART * (t + 1), :]

        def need(eng, semaphore, value):
            if not isinstance(value, int) or value > 0:
                eng.wait_ge(semaphore, value)

        block = ctx.enter_context(nc.Block())

        @block.sync
        def _(sp):
            def load_const(dst, src, semaphore=const_loaded):
                sp.dma_start(dst, src, allow_slow_non_contiguous=True).then_inc(semaphore, 16)

            x_uses = [0, 0]

            def load_x(s, t):
                b = (s.x0 // 2 + t) % 2
                if s.x0 // 2 + t >= 2:
                    before = s.x0 + t - 2 if t >= 2 else shapes[s.p - 1].x0 + shapes[s.p - 1].nt + t - 2
                    sp.wait_ge(xn_ready, before + 1)
                sp.dma_start(xload[0:s.rows[t], b], tile_dram(x_prompt, x_sample, TILE0[s.p] + t))\
                    .then_inc(x_loaded[b], 16)

            def ring1(s, block_id, dst, src):
                b = RING1 * s.p + block_id
                need(sp, split1, b - 1)
                sp.dma_start(dst, src).then_inc(raw1_loaded[b % 2], 16)

            def load_slab(s, m):
                ring1(s, slab_id(m), raw1[:, slab_id(m) % 2].rearrange("p (k m) -> p k m", k=KT),
                      w_in_k[:, :, SLABS[m][2]:SLABS[m][2] + PART])

            def load_v(s):
                for c in range(2):
                    ring1(s, V_ID + c, raw1[:, c, 0:4 * KV_DIM].rearrange("p (k m) -> p k m", k=4),
                          w_in_k[:, 4 * c:4 * c + 4, V0:V0 + KV_DIM])

            def load_out(s, b):
                rows = w_out[0, PART * b:PART * (b + 1), :]
                if b < 4:
                    ring1(s, OUT_ID + b, raw1[:, b % 2], rows)
                else:
                    need(sp, split2, RING2 * s.p + b - 4 - 3)
                    sp.dma_start(raw2[:, b - 4], rows).then_inc(raw2_loaded[b - 4], 16)

            def load_gate_up(s, j):
                for n in range(4):
                    sp.wait_ge(split2, RING2 * s.p + GATE_ID + 4 * j + n - 3)
                    w = (w_gate_k, w_up_k)[n % 2]
                    sp.dma_start(raw2[:, n].rearrange("p (k m) -> p k m", k=KT),
                                 w[:, :, bass.ds(256 * j + PART * (n // 2), PART)])\
                        .then_inc(raw2_loaded[n], 16)

            def load_down(s, j):
                for c in range(2):
                    sp.wait_ge(split1, RING1 * s.p + DOWN_ID + 2 * j + c - 1)
                    sp.dma_start(raw1[:, c], w_down[0, bass.ds(256 * j + PART * c, PART), :])\
                        .then_inc(raw1_loaded[c], 16)

            for s in shapes:
                load_x(s, 0)
                if s.p == 0:
                    load_const(ident[:, :], c_ident, ident_loaded)
                    load_const(g_mix[:, :], norm_mix.partition_broadcast(PART)[:, 0, :], gmix_loaded)
                load_x(s, 1)
                load_slab(s, 0)
                load_slab(s, 1)
                if s.p == 0:
                    sp.wait_ge(wpool_zero, 1)
                    for e in range(2):
                        load_const(qg[HD * e:HD * (e + 1), :], q_norm.rearrange("a d -> d a"))
                        load_const(kg[HD * e:HD * (e + 1), :], k_norm.rearrange("a d -> d a"))
                    load_const(headsum[:, :], c_ones)
                    load_const(sink[:, :], sinks.partition_broadcast(PART)[:, 0, :])
                    load_const(pscale[:, :], pool_scale[0].rearrange("(s p) -> p s", p=PART))
                    for e in range(2):
                        load_const(wpool[HD * e:HD * (e + 1), :, HD * e:HD * (e + 1)],
                                   w_pool[0].rearrange("(s e) c d -> e c s d", e=2)[e])
                    load_const(inv[:, :, :], c_inv)
                    load_const(g_ffn[:, :], norm_ffn.partition_broadcast(PART)[:, 0, :])
                    load_const(dist[:, :], c_dist)
                for t in range(2, s.nt):
                    load_x(s, t)
                if s.has_sample:
                    sp.wait_ge(d_ready, s.d0)
                    for e in range(2):
                        sp.dma_start(ck_st[:, :, e, :], cache_k[0, 0]).then_inc(cache_loaded, 16)
                    sp.dma_start(cp_st[0:HIST, :], cache_pool[0, 0]).then_inc(cache_loaded, 16)
                    sp.dma_start(v_sb[:, s.slot(4) - 1, :], cache_v[0, 0].rearrange("r g d -> r (g d)"))\
                        .then_inc(cache_loaded, 16)
                for m in range(2, EARLY):
                    load_slab(s, m)
                for t in range(s.nt):
                    need(sp, y_stored[t], 16 * s.p)
                    sp.dma_start(h[0:s.rows[t], t], tile_dram(x_prompt, x_sample, TILE0[s.p] + t))\
                        .then_inc(h_loaded[t], 16)
                load_v(s)
                for m in range(EARLY, len(SLABS)):
                    load_slab(s, m)
                for b in range(4):
                    load_out(s, b)
                sp.wait_ge(tp_free, mixed(s))
                for b in range(4, 8):
                    load_out(s, b)
                load_gate_up(s, 0)
                load_gate_up(s, 1)
                with sp.Fori(0, LOOPS) as i:
                    for half in range(2):
                        load_down(s, 2 * i + half)
                        load_gate_up(s, 2 * i + half + 2)
                load_down(s, GROUPS - 3)
                load_gate_up(s, GROUPS - 1)
                load_down(s, GROUPS - 2)
                for c in range(2):
                    sp.wait_ge(split2, RING2 * s.p + LAST_ID + c - 3)
                    r = 256 * (GROUPS - 1) + PART * c
                    sp.dma_start(raw2[:, c], w_down[0, r:r + PART, :]).then_inc(raw2_loaded[c], 16)

        @block.gpsimd
        def _(pool):
            steps = [0]

            def link(ins):
                steps[0] += 1
                ins.then_inc(pool_step, 1)
                pool.wait_ge(pool_step, steps[0])

            def low(raw, hi, lo, done, number, size=1024):
                pool.wait_ge(hi_done, number)
                nc.gpsimd.tensor_tensor(lo[:, 0:size], raw[:, 0:size], hi[:, 0:size].bitcast(F32),
                                        ALU.subtract).then_inc(done, 1)

            def low1(block_id, number, size=1024):
                b = block_id % 2
                low(raw1[:, b], w1_hi[:, b], w1_lo[:, b], split1, number, size)

            def low2(slot, number):
                low(raw2[:, slot], w2_hi[:, slot], w2_lo[:, slot], split2, number)

            def windows(s, b):
                n = HALO + s.T + (HALO if s.has_sample else 0)
                u = ut_sb[:, b]
                if b == 0:
                    pool.wait_ge(z_free, s.z_unit(1, 1) + 1)
                    pool.wait_ge(halo_ready, s.p + 1)
                    if s.has_sample:
                        pool.wait_ge(tp_free, sum(tp_total[:s.p]) + 2 * s.nt + TP_CACHE)
                else:
                    pool.wait_ge(windows_used, 2 * s.p + 1)
                levels = [u] + [win[:, 0], win[:, 1]][:1 + b] + ([win[:, 0]] if b else [])
                w = 1
                for src, dst in zip(levels, levels[1:]):
                    w *= 2
                    link(nc.gpsimd.tensor_tensor(dst[:, w:n], src[:, w:n], src[:, w - w // 2:n - w // 2],
                                                 ALU.add))
                top, w = slice(HD, PART), 2 * w
                assert POOL_WINDOWS[2 * b:2 * b + 2] == (w // 2, w)
                ins = nc.gpsimd.tensor_tensor(win[top, 1, w:n], win[top, 0, w:n],
                                              win[top, 0, w - w // 2:n - w // 2], ALU.add)
                if s.p == 0:
                    pool.wait_ge(const_loaded, 16 * N_CONST)
                    link(ins)
                    link(nc.gpsimd.tensor_tensor(win[0:HD, 0, HALO:2 * HALO], win[0:HD, 0, HALO:2 * HALO],
                                                 inv[0:HD, b, :], ALU.mult))
                    ins = nc.gpsimd.tensor_tensor(win[top, 1, HALO:2 * HALO], win[top, 1, HALO:2 * HALO],
                                                  inv[top, b, :], ALU.mult)
                ins.then_inc(windows_ready, 1)
                pool.wait_ge(windows_ready, 2 * s.p + b + 1)

            nc.gpsimd.memset(wpool[:, :, :], 0.0).then_inc(wpool_zero, 1)
            done = 0
            for s in shapes:
                for block_id in range(OUT_ID + 4):
                    done += 1
                    low1(block_id, done, 4 * KV_DIM if block_id in (V_ID, V_ID + 1) else 1024)
                    if block_id == V_ID + 3:
                        windows(s, 0)
                    if block_id == V_ID + 5:
                        windows(s, 1)
                for slot in (0, 1, 2, 3) * 3:
                    done += 1
                    low2(slot, done)
                with pool.Fori(0, LOOPS) as i:
                    for n in range(12):
                        number = done + 12 * i + n + 1
                        if n % 6 < 2:
                            low1(n % 6, number)
                        else:
                            low2(n % 6 - 2, number)
                done += 12 * LOOPS
                for ring, slot in ((1, 0), (1, 1), (2, 0), (2, 1), (2, 2), (2, 3), (1, 0), (1, 1),
                                   (2, 0), (2, 1)):
                    done += 1
                    (low1 if ring == 1 else low2)(slot, done)

        @block.tensor
        def _(pe):
            tp = [0]

            def split_products(out, w_hi, w_lo, m_hi, m_lo, first, last):
                nc.tensor.matmul(out, w_hi, m_hi, start=first, stop=False)
                nc.tensor.matmul(out, w_hi, m_lo, start=False, stop=False)
                return nc.tensor.matmul(out, w_lo, m_hi, start=False, stop=last)

            def tp_bank():
                need(pe, tp_free, tp[0] - 3)
                tp[0] += 1
                return ps[:, 4 + (tp[0] - 1) % 4]

            def transposed(src, cols, rows):
                bank = tp_bank()
                for n, c in enumerate(cols):
                    last = nc.tensor.transpose(bank[:, n * rows:(n + 1) * rows],
                                               src[0:rows, PART * c:PART * (c + 1)], ident[0:rows, 0:rows])
                last.then_inc(tp_ready, 1)

            def norm_transposes(s, x0, t):
                pe.wait_ge(xn_ready, x0 + t + 1)
                for half in range(2):
                    transposed(xn[:, (x0 + t) % 2], range(4 * half, 4 * half + 4), s.rows[t])

            def mix_transposes(s, t):
                pe.wait_ge(o_done, s.a0 + 2 * s.nt + t + 1)
                for half in range(2):
                    transposed(atok[:, t], range(3 * half, 3 * half + 3), s.rows[t])

            def cache_transposes(s):
                pe.wait_ge(cache_loaded, 16 * 4)
                for g in range(N_KV):
                    bank = tp_bank()
                    nc.tensor.transpose(bank[:, 0:PART], ck_st[:, g].rearrange("p e d -> p (e d)"),
                                        ident[:, :]).then_inc(tp_ready, 1)
                bank = tp_bank()
                for b in range(2):
                    last = nc.tensor.transpose(bank[:, HALO * b:HALO * b + HIST],
                                               cp_st[0:HIST, PART * b:PART * (b + 1)], ident[0:HIST, 0:HIST])
                last.then_inc(tp_ready, 1)

            def state_transposes(s):
                pe.wait_ge(tails_saved, s.p + 1)
                for c0, rows in ((s.kcol(3 * PART), PART), (s.kcol(4 * PART), DEC)):
                    bank = tp_bank()
                    for g in range(N_KV):
                        last = nc.tensor.transpose(bank[0:rows, PART * g:PART * (g + 1)],
                                                   kt_sb[:, g, c0:c0 + rows], ident[:, :])
                    last.then_inc(tp_ready, 1)
                bank = tp_bank()
                for w in range(2):
                    for b in range(2):
                        n = 2 * w + b
                        last = nc.tensor.transpose(bank[0:HIST, PART * n:PART * (n + 1)],
                                                   u_tail[:, w, b, 1:HALO], ident[:, :])
                last.then_inc(tp_ready, 1)

            def v_tile(s, t):
                zi = s.v_unit(t)
                need(pe, z_free, zi - 1)
                out = ps[0:s.rows[t], zi % 2, 0:KV_DIM]
                tok = slice(PART * t, PART * t + s.rows[t])
                for k in range(KT):
                    if t == 0 and k % 4 == 0:
                        pe.wait_ge(split1, RING1 * s.p + V_ID + k // 4 + 1)
                    cols = slice(KV_DIM * (k % 4), KV_DIM * (k % 4 + 1))
                    last = split_products(out, xt_hi[:, k, tok], xt_lo[:, k, tok],
                                          w1_hi[:, k // 4, cols], w1_lo[:, k // 4, cols],
                                          k == 0, k == KT - 1)
                last.then_inc(z_ready, 1)

            def slab_unit(s, m, nb):
                zi, slot = s.z_unit(m, nb), slab_id(m) % 2
                pe.wait_ge(split1, RING1 * s.p + slab_id(m) + 1)
                need(pe, z_free, zi - 1)
                out = ps[:, zi % 2, 0:s.NB]
                tok = slice(nb * s.NB, (nb + 1) * s.NB)
                for k in range(KT):
                    cols = slice(PART * k, PART * (k + 1))
                    last = split_products(out, w1_hi[:, slot, cols], w1_lo[:, slot, cols],
                                          xt_hi[:, k, tok], xt_lo[:, k, tok], k == 0, k == KT - 1)
                last.then_inc(z_ready, 1)

            def head_sums(s, oi):
                pe.wait_ge(sq_ready, oi + 1)
                need(pe, ss_free, oi)
                nc.tensor.matmul(ps[:, 2, 0:s.NB], headsum[:, :], sq[:, oi % 2, 0:s.NB],
                                 start=True, stop=True).then_inc(ss_ready, 1)

            def scores(s, n):
                g, t = s.units[n]
                ai, rows = s.a0 + n, s.rows[t]
                c0, c1 = s.keys(t)
                pe.wait_ge(fin_done, s.o0 + 8 + 4 * g)
                need(pe, sc_free, ai)
                k0 = PART * (s.slot(t) - 1)
                for hh in range(GQA):
                    e, j = hh % 2, hh // 2
                    last = nc.tensor.matmul(ps[0:rows, 4 + e, 256 * j + c0:256 * j + c1],
                                            qt_sb[HD * e:HD * (e + 1), g % 2, j, PART * t:PART * t + rows],
                                            kt_sb[HD * e:HD * (e + 1), g, k0 + c0:k0 + c1],
                                            start=True, stop=True)
                last.then_inc(qk_ready, 1)

            def prob_transposes(s, n):
                ai, rows = s.a0 + n, s.rows[s.units[n][1]]
                c0, c1 = s.keys(s.units[n][1])
                pe.wait_ge(e_ready, ai + 1)
                need(pe, pt_done, ai)
                for half in range(2):
                    a, b = max(c0, PART * half), min(c1, PART * (half + 1))
                    if a >= b:
                        continue
                    for hh in range(GQA):
                        last = nc.tensor.transpose(ps[0:b - a, 6 + half, rows * hh:rows * (hh + 1)],
                                                   s_sb[0:rows, ai % 2, hh, a:b], ident[0:rows, 0:rows])
                last.then_inc(pt_ready, 1)

            def weighted_values(s, n):
                g, t = s.units[n]
                ai, rows = s.a0 + n, s.rows[t]
                c0, c1 = s.keys(t)
                pe.wait_ge(pt_done, ai + 1)
                need(pe, o_done, ai)
                for hh in range(GQA):
                    for half in range(2):
                        a, b = max(c0, PART * half), min(c1, PART * (half + 1))
                        if a >= b:
                            continue
                        last = nc.tensor.matmul(ps[0:rows, 3, HD * hh:HD * (hh + 1)],
                                                pt_sb[0:b - a, ai % 2, half, rows * hh:rows * (hh + 1)],
                                                v_sb[0:b - a, s.slot(t) - 1 + half, HD * g:HD * (g + 1)],
                                                start=a == c0, stop=half == 1)
                last.then_inc(pv_ready, 1)

            def pool_map(s, b):
                pe.wait_ge(windows_used, 2 * s.p + b + 1)
                pe.wait_ge(z_free, s.z0 + 2 * len(SLABS) + s.nt)
                for nb in range(2):
                    mi = 4 * s.p + 2 * b + nb
                    need(pe, m_free, mi - 1)
                    for a, e in s.cuts(nb):
                        last = nc.tensor.matmul(ps[:, mi % 2, a - nb * s.NB:e - nb * s.NB], wpool[:, b, :],
                                                ut_sb[:, b, s.ucol(a):s.ucol(a) + e - a],
                                                start=True, stop=True)
                    last.then_inc(m_ready, 1)

            def add_unit(s, bank, t, nh, w_hi, w_lo, m_hi, m_lo):
                tok, cols = slice(PART * t, PART * t + s.rows[t]), slice(512 * nh, 512 * (nh + 1))
                for c in range(2):
                    last = split_products(ps[0:s.rows[t], bank, :], m_hi[:, c, tok], m_lo[:, c, tok],
                                          w_hi[:, c, cols], w_lo[:, c, cols], c == 0, c == 1)
                last.then_inc(d_ready, 1)

            def add_tile(s, d0, parity, t, *operands):
                for nh in range(2):
                    need(pe, d_free, d0 + 2 * t + nh - 3)
                    add_unit(s, (2 * t + nh + s.d_of * parity) % 4, t, nh, *operands)

            def out_operands(j):
                w_hi, w_lo = (w1_hi, w1_lo) if j < 2 else (w2_hi, w2_lo)
                slots = slice(0, 2) if j < 3 else slice(2, 4)
                return (w_hi[:, slots], w_lo[:, slots], xt_hi[:, 2 * j:2 * j + 2], xt_lo[:, 2 * j:2 * j + 2])

            def attend(s):
                last = len(s.units) - 1
                scores(s, 0)
                for n in range(last + 1):
                    if n < last:
                        scores(s, n + 1)
                    for d in s.late_at(n):
                        if d < LATE:
                            slab_unit(s, EARLY + d // 2, d % 2)
                        if 1 <= d <= LATE:
                            head_sums(s, s.o0 + 8 + d - 1)
                    if MIX_AT <= n < MIX_AT + 2:
                        pool_map(s, n - MIX_AT)
                    t = n - OUT_AT
                    if 0 <= t < s.nt:
                        if t == 0:
                            pe.wait_ge(m_free, 4 * s.p + 4)
                            pe.wait_ge(split1, RING1 * s.p + OUT_ID + 2)
                        for nh in range(2):
                            need(pe, d_free, s.d_unit(0, t, nh) - 1)
                            add_unit(s, nh, t, nh, *out_operands(0))
                    prob_transposes(s, n)
                    if n == 1:
                        pe.wait_ge(z_free, s.v_unit(s.nt - 1) + 1)
                    if n >= 1:
                        weighted_values(s, n - 1)
                weighted_values(s, last)

            def gate_up_unit(s, j, c, nb, which, bank):
                slot = 2 * c + which
                gi = s.g0 + 4 * j + 2 * c + nb
                pe.wait_ge(split2, RING2 * s.p + GATE_ID + 4 * j + slot + 1)
                need(pe, (silu_done, a_done)[which], gi - 1)
                out, tok = ps[:, bank, 0:s.NB], slice(nb * s.NB, (nb + 1) * s.NB)
                for k in range(KT):
                    cols = slice(PART * k, PART * (k + 1))
                    last = split_products(out, w2_hi[:, slot, cols], w2_lo[:, slot, cols],
                                          xt_hi[:, k, tok], xt_lo[:, k, tok], k == 0, k == KT - 1)
                last.then_inc((g_ready, u_ready)[which], 1)

            def gate_up(s, j, first=0):
                for n in range(first, 4):
                    for which in range(2):
                        gate_up_unit(s, j, n // 2, n % 2, which, 4 + 2 * which + n % 2)

            def down(s, j, parity):
                pe.wait_ge(split1, RING1 * s.p + DOWN_ID + 2 * j + 2)
                pe.wait_ge(al_done, s.g0 + 4 * j + 4)
                for t in range(s.nt):
                    add_tile(s, s.d0 + s.d_of * (OUT_GROUPS + j), parity, t, w1_hi, w1_lo,
                             act_hi[:, parity], act_lo[:, parity])

            def boundary(prev, s):
                if prev:
                    pe.wait_ge(split2, RING2 * prev.p + RING2)
                    pe.wait_ge(al_done, prev.g0 + 4 * GROUPS)
                if s:
                    need(pe, a_done, s.g0)
                for t in range(max(prev.nt if prev else 0, s.nt + 1 if s else 0)):
                    if prev and t < prev.nt:
                        add_tile(prev, prev.d_unit(D_GROUPS - 1, 0), 0, t, w2_hi[:, 0:2], w2_lo[:, 0:2],
                                 act_hi[:, 0], act_lo[:, 0])
                    if s and 1 <= t <= s.nt:
                        norm_transposes(s, s.x0, t - 1)

            pe.wait_ge(ident_loaded, 16)
            prev = None
            for s in shapes:
                xt_start = tp[0]
                boundary(prev, s)
                need(pe, d_free, s.d0)
                for m in range(EARLY):
                    for nb in range(2):
                        if m == 0:
                            pe.wait_ge(tp_free, xt_start + (2 * -(-s.NB // PART), 2 * s.nt)[nb])
                        slab_unit(s, m, nb)
                        if m == 2 and nb == 0 and s.p == 0:
                            pe.wait_ge(const_loaded, 16 * N_CONST)
                        if s.oi(m, nb) > s.o0:
                            head_sums(s, s.oi(m, nb) - 1)
                    if m == 1 and s.has_sample:
                        cache_transposes(s)
                for t in range(s.nt):
                    v_tile(s, t)
                    if t == 0:
                        head_sums(s, s.o0 + 7)
                pe.wait_ge(halo_ready, s.p + 1)
                pe.wait_ge(tp_free, tp[0])
                attend(s)
                pe.wait_ge(sc_free, s.a0 + len(s.units))
                pe.wait_ge(pt_done, s.a0 + len(s.units))
                if s.has_sample:
                    state_transposes(s)
                mix_start = tp[0]
                mix_transposes(s, 0)
                mix_transposes(s, 1)
                pe.wait_ge(split1, RING1 * s.p + OUT_ID + 4)
                pe.wait_ge(ss_free, s.o0 + 16)
                pe.wait_ge(d_free, s.d_unit(1, 0))
                for t in range(s.nt):
                    if t + 2 < s.nt:
                        mix_transposes(s, t + 2)
                    if t == 0:
                        pe.wait_ge(o_done, s.a0 + len(s.units))
                    pe.wait_ge(tp_free, mix_start + 2 * (t + 1))
                    add_tile(s, s.d_unit(1, 0), 1, t, *out_operands(1))
                for j in (2, 3):
                    pe.wait_ge(split2, RING2 * s.p + 2 * (j - 1))
                    for t in range(s.nt):
                        add_tile(s, s.d_unit(j, 0), j % 2, t, *out_operands(j))
                        if j == 3 and t >= 2:
                            norm_transposes(s, s.x0 + s.nt, t - 2)
                norm_transposes(s, s.x0 + s.nt, s.nt - 2)
                pe.wait_ge(d_free, s.d_unit(OUT_GROUPS, 0))
                pe.wait_ge(tp_free, tp[0] - 2 * (s.nt - 1) + 2 * -(-s.NB // PART))
                gate_up_unit(s, 0, 0, 0, 0, 0)
                norm_transposes(s, s.x0 + s.nt, s.nt - 1)
                gate_up_unit(s, 0, 0, 0, 1, 1)
                pe.wait_ge(tp_free, tp[0])
                gate_up(s, 0, first=1)
                with pe.Fori(0, LOOPS) as i:
                    gate_up(s, 2 * i + 1)
                    down(s, 2 * i, 0)
                    gate_up(s, 2 * i + 2)
                    down(s, 2 * i + 1, 1)
                gate_up(s, GROUPS - 2)
                down(s, GROUPS - 3, 0)
                gate_up(s, GROUPS - 1)
                down(s, GROUPS - 2, 1)
                prev = s
            boundary(prev, None)

        @block.scalar
        def _(act):
            steps, tp = [0], [0]

            def link(ins):
                steps[0] += 1
                ins.then_inc(act_step, 1)
                act.wait_ge(act_step, steps[0])

            def high1(s, block_id):
                b, size = block_id % 2, 4 * KV_DIM if block_id in (V_ID, V_ID + 1) else 1024
                act.wait_ge(raw1_loaded[b], 16 * ((RING1 * s.p + block_id) // 2 + 1))
                nc.scalar.activation(w1_hi[:, b, 0:size], raw1[:, b, 0:size], ACT.Copy).then_inc(hi_done, 1)

            def high1_down(s, j):
                for c in range(2):
                    act.wait_ge(raw1_loaded[c], 16 * ((RING1 * s.p + DOWN_ID) // 2 + j + 1))
                    nc.scalar.activation(w1_hi[:, c], raw1[:, c], ACT.Copy).then_inc(hi_done, 1)

            def high2(s, slots, use):
                for n in slots:
                    act.wait_ge(raw2_loaded[n], 16 * (USES2[n] * s.p + use + 1))
                    nc.scalar.activation(w2_hi[:, n], raw2[:, n], ACT.Copy).then_inc(hi_done, 1)

            def tp_copy(dst, src, scale=1.0):
                tp[0] += 1
                act.wait_ge(tp_ready, tp[0])
                nc.scalar.activation(dst, src, ACT.Copy, scale=scale).then_inc(tp_hi, 1)

            def tp_unit(k0, nk, tok):
                n = tok.stop - tok.start
                tp_copy(xt_hi[:, k0:k0 + nk, tok],
                        ps[:, 4 + tp[0] % 4, 0:nk * n].rearrange("p (k t) -> p k t", k=nk))

            def row_rstd(s, src, xi, c, t, tp_start):
                rows = s.rows[t]
                if t >= 2:
                    act.wait_ge(tp_ready, tp_start + 2 * (t - 1))
                link(nc.scalar.activation(xn[0:rows, xi % 2], src, ACT.Square,
                                          accum_out=ss[0:rows, c:c + 1]))
                link(nc.scalar.activation(ss[0:rows, c:c + 1], ss[0:rows, c:c + 1], ACT.Ln,
                                          bias=eps[0:rows, :], scale=1.0 / D_MODEL))
                nc.scalar.activation(rstd[0:rows, c:c + 1], ss[0:rows, c:c + 1], ACT.Exp,
                                     scale=-0.5).then_inc(rstd_ready, 1)

            def norm_copies(s, t):
                for half in range(2):
                    tp_unit(4 * half, 4, slice(PART * t, PART * t + s.rows[t]))

            def boundary(prev, s):
                tp_start = tp[0]
                if s:
                    nc.scalar.preload_act_table_set("natural_log_exp_and_others")
                for t in range(1 + max(prev.nt if prev else 0, s.nt if s else 0)):
                    if s and t < s.nt:
                        xi = s.x0 // 2 + t
                        act.wait_ge(x_loaded[xi % 2], 16 * (xi // 2 + 1))
                        row_rstd(s, xload[0:s.rows[t], xi % 2], s.x0 + t, t, t, tp_start)
                    if s and t < 2:
                        if prev and t == 0:
                            act.wait_ge(d_ready, prev.d_unit(D_GROUPS - 1, 0))
                        high1(s, t)
                    if s and 1 <= t <= s.nt:
                        norm_copies(s, t - 1)
                    if prev and 1 <= t <= prev.nt:
                        act.wait_ge(d_free, prev.d_unit(D_GROUPS - 1, t))
                        act.dma_start(tile_dram(y_prompt, y_sample, TILE0[prev.p] + t - 1),
                                      h[0:prev.rows[t - 1], t - 1]).then_inc(y_stored[t - 1], 16)

            def slab_read(s, m, nb):
                kind, j, _ = SLABS[m]
                zi, oi = s.z_unit(m, nb), s.oi(m, nb)
                z = ps[:, zi % 2, 0:s.NB]
                act.wait_ge(z_ready, zi + 1)
                if nb == 1:
                    high1(s, slab_id(m) + 2)
                if kind == "u":
                    for a, e in s.cuts(nb):
                        last = nc.scalar.activation(ut_sb[:, j, s.ucol(a):s.ucol(a) + e - a],
                                                    z[:, a - nb * s.NB:e - nb * s.NB], ACT.Copy)
                    last.then_inc(z_free, 1)
                    return
                need(act, ss_ready, oi - 1)
                nc.scalar.activation(sq[:, oi % 2, 0:s.NB], z, ACT.Square).then_inc(sq_ready, 1)
                if kind == "k":
                    need(act, fin_done, oi - 1)
                    dst, scale = zs[:, oi % 2, 0:s.NB], kg[:, :]
                else:
                    g = j // 2
                    if g >= 2:
                        act.wait_ge(qk_ready, s.a0 + s.nt * (g - 1))
                    dst, scale = qt_sb[:, g % 2, j % 2, nb * s.NB:(nb + 1) * s.NB], qg[:, :]
                nc.scalar.activation(dst, z, ACT.Copy, scale=scale).then_inc(z_free, 1)

            def head_rstd(s, oi):
                act.wait_ge(ss_ready, oi + 1)
                need(act, fin_done, oi - 1)
                r = rr[:, oi % 2, 0:s.NB]
                nc.scalar.activation(r, ps[:, 2, 0:s.NB], ACT.Ln, bias=eps[:, :],
                                     scale=1.0 / HD).then_inc(ss_free, 1)
                act.wait_ge(ss_free, oi + 1)
                nc.scalar.activation(r, r, ACT.Exp, scale=-0.5).then_inc(r_ready, 1)

            def v_read(s, t):
                zi = s.v_unit(t)
                act.wait_ge(z_ready, zi + 1)
                nc.scalar.activation(v_sb[0:s.rows[t], s.slot(t), :], ps[0:s.rows[t], zi % 2, 0:KV_DIM],
                                     ACT.Copy).then_inc(z_free, 1)

            def exps(s, n):
                ai, rows = s.a0 + n, s.rows[s.units[n][1]]
                c0, c1 = s.keys(s.units[n][1])
                act.wait_ge(nm_ready, ai + 1)
                for hh in range(GQA):
                    p = s_sb[0:rows, ai % 2, hh, c0:c1]
                    nc.scalar.activation(p, p, ACT.Exp, bias=negmax[0:rows, ai % 2, hh:hh + 1],
                                         accum_out=den[0:rows, ai % 2, hh:hh + 1])
                nc.scalar.activation(esink[0:rows, ai % 2, :], esink[0:rows, ai % 2, :],
                                     ACT.Exp).then_inc(e_ready, 1)

            def prob_copy(s, n):
                ai, rows = s.a0 + n, s.rows[s.units[n][1]]
                c0, c1 = s.keys(s.units[n][1])
                act.wait_ge(pt_ready, ai + 1)
                need(act, pv_ready, ai - 1)
                if c1 - c0 == 2 * PART:
                    pieces = [(slice(0, PART), slice(0, 2))]
                else:
                    pieces = [(slice(0, min(c1, PART * (half + 1)) - PART * half), slice(half, half + 1))
                              for half in range(2) if c0 < PART * (half + 1)]
                for keys, halves in pieces:
                    last = nc.scalar.activation(
                        pt_sb[keys, ai % 2, halves, 0:GQA * rows],
                        ps[keys, slice(6 + halves.start, 6 + halves.stop), 0:GQA * rows], ACT.Copy)
                last.then_inc(pt_done, 1)

            def pool_high(s, b):
                for nb in range(2):
                    mi = 4 * s.p + 2 * b + nb
                    act.wait_ge(m_ready, mi + 1)
                    nc.scalar.activation(xt_hi[:, b, nb * s.NB:(nb + 1) * s.NB], ps[:, mi % 2, 0:s.NB],
                                         ACT.Copy, scale=pscale[:, b:b + 1]).then_inc(m_hi, 1)

            def attend(s):
                last = len(s.units) - 1
                exps(s, 0)
                for n in range(last + 1):
                    if n < last:
                        exps(s, n + 1)
                    for d in s.late_at(n):
                        if d < LATE:
                            slab_read(s, EARLY + d // 2, d % 2)
                        if 1 <= d <= LATE:
                            head_rstd(s, s.o0 + 8 + d - 1)
                    if MIX_AT <= n < MIX_AT + 2:
                        pool_high(s, n - MIX_AT)
                    prob_copy(s, n)
                    if n == min(OUT_AT + s.nt, last):
                        act.wait_ge(d_ready, s.d_unit(1, 0))
                        for c in range(2):
                            high1(s, OUT_ID + 2 + c)

            def gates(s, j, parity, begin=None, bank0=4):
                if begin != "first":
                    act.wait_ge(d_ready, s.d0 + s.d_of * (OUT_GROUPS - 1 + j))
                    high1_down(s, j - 1)
                for n in range(4):
                    gi = s.g0 + 4 * j + n
                    act.wait_ge(g_ready, gi + 1)
                    need(act, a_done, gi - 1)
                    nc.scalar.activation(sg[:, n % 2, 0:s.NB], ps[:, bank0 if n == 0 else 4 + n % 2, 0:s.NB],
                                         ACT.Silu).then_inc(silu_done, 1)
                    if n == 2:
                        high2(s, (0, 1), 1 + j + 1)
                    if n >= 1:
                        high_part(s, j, n - 1, parity)
                high_part(s, j, 3, parity)
                if begin != "last":
                    act.wait_ge(u_ready, s.g0 + 4 * j + 4)
                    high2(s, (2, 3), 1 + j + 1)

            def high_part(s, j, n, parity):
                act.wait_ge(a_done, s.g0 + 4 * j + n + 1)
                nc.scalar.activation(act_hi[:, parity, n // 2, (n % 2) * s.NB:(n % 2 + 1) * s.NB],
                                     aa[:, n % 2, 0:s.NB], ACT.Copy).then_inc(ah_done, 1)

            def state_copies(s):
                for n, rows in enumerate((PART, DEC)):
                    tp_copy(k_st[0:rows, KV_DIM * n:KV_DIM * n + 2 * HD].rearrange("p (g d) -> p g d", g=2),
                            ps[0:rows, 4 + tp[0] % 4, 0:2 * PART]
                            .rearrange("p (g d) -> p g d", g=2)[:, :, 0:HD])
                tp_copy(u_st[0:HIST, 0:POOL_DIM], ps[0:HIST, 4 + tp[0] % 4, 0:POOL_DIM])

            def store_states(s):
                act.wait_ge(tp_free, mixed(s))
                act.dma_start(nk_prompt[0, 0].rearrange("r g d -> r (g d)"), k_st[:, 0:KV_DIM])\
                    .then_inc(state_stored, 16)
                act.dma_start(nk_sample[0, 0, PART - DEC:PART].rearrange("r g d -> r (g d)"),
                              k_st[0:DEC, KV_DIM:2 * KV_DIM]).then_inc(state_stored, 16)
                act.dma_start(nk_sample[0, 0, 0:PART - DEC], cache_k[0, 0, DEC:PART])\
                    .then_inc(state_stored, 16)
                act.dma_start(nv_sample[0, 0, 0:PART - DEC], cache_v[0, 0, DEC:PART])\
                    .then_inc(state_stored, 16)
                act.dma_start(nv_prompt[0, 0].rearrange("r g d -> r (g d)"), v_tail[:, :])\
                    .then_inc(state_stored, 16)
                act.dma_start(nv_sample[0, 0, PART - DEC:PART].rearrange("r g d -> r (g d)"),
                              k_st[0:DEC, 2 * KV_DIM:3 * KV_DIM]).then_inc(state_stored, 16)
                act.dma_start(np_prompt[0, 0], u_st[0:HIST, 0:POOL_DIM]).then_inc(state_stored, 16)
                act.dma_start(np_sample[0, 0], u_st[0:HIST, POOL_DIM:2 * POOL_DIM])\
                    .then_inc(state_stored, 16)

            act.wait_ge(const_ready, 1)
            prev = None
            for s in shapes:
                boundary(prev, s)
                if s.p == 0:
                    act.wait_ge(const_ready, 3)
                for m in range(EARLY):
                    for nb in range(2):
                        slab_read(s, m, nb)
                        if s.oi(m, nb) > s.o0:
                            head_rstd(s, s.oi(m, nb) - 1)
                    if m == 1 and s.has_sample:
                        c0 = PART * (s.slot(4) - 1)
                        for g in range(N_KV):
                            tp_copy(kt_sb[0:HD, g, c0:c0 + PART], ps[0:HD, 4 + tp[0] % 4, 0:PART])
                        u0 = s.ucol(s.T - DEC) - HIST
                        tp_copy(ut_sb[:, 0, u0:u0 + HIST], ps[:, 4 + tp[0] % 4, 0:HIST])
                for t in range(s.nt):
                    if t == s.nt - 1:
                        act.wait_ge(z_ready, s.v_unit(t) + 1)
                        high1(s, V_ID + 2)
                    v_read(s, t)
                    if t == 0:
                        head_rstd(s, s.o0 + 7)
                high1(s, V_ID + 3)
                attend(s)
                if s.has_sample:
                    state_copies(s)
                for t in range(s.nt):
                    for half in range(2):
                        tp_unit(2 + 3 * half, 3, slice(PART * t, PART * t + s.rows[t]))
                act.wait_ge(tp_free, mixed(s))
                high2(s, (0, 1, 2, 3), 0)
                if s.has_sample:
                    store_states(s)
                act.wait_ge(d_ready, s.d_unit(3, 0))
                high2(s, (0, 1), 1)
                tp_start = tp[0]
                for t in range(s.nt):
                    act.wait_ge(d_free, s.d_unit(3, t) + 2)
                    row_rstd(s, h[0:s.rows[t], t], s.x0 + s.nt + t, 8 + t, t, tp_start)
                    if t >= 1:
                        norm_copies(s, t - 1)
                high2(s, (2, 3), 1)
                norm_copies(s, s.nt - 1)
                nc.scalar.preload_act_table(ACT.Silu)
                if s.has_sample:
                    act.wait_ge(state_stored, 16 * 8)
                gates(s, 0, 0, "first", bank0=0)
                with act.Fori(0, LOOPS) as i:
                    gates(s, 2 * i + 1, 1)
                    gates(s, 2 * i + 2, 0)
                gates(s, GROUPS - 2, 1)
                gates(s, GROUPS - 1, 0, "last")
                prev = s
            boundary(prev, None)
            for t in range(6):
                act.wait_ge(y_stored[t], 16 * sum(t < n for n in NT))

        @block.vector
        def _(dve):
            steps, tp = [0], [0]

            def link(ins):
                steps[0] += 1
                ins.then_inc(dve_step, 1)
                dve.wait_ge(dve_step, steps[0])

            def tp_wait():
                tp[0] += 1
                dve.wait_ge(tp_hi, tp[0])
                return ps[:, 4 + (tp[0] - 1) % 4]

            def tp_unit(k0, nk, tok):
                bank, n = tp_wait(), tok.stop - tok.start
                nc.vector.tensor_tensor(xt_lo[:, k0:k0 + nk, tok],
                                        bank[:, 0:nk * n].rearrange("p (k t) -> p k t", k=nk),
                                        xt_hi[:, k0:k0 + nk, tok].bitcast(F32), ALU.subtract)\
                    .then_inc(tp_free, 1)

            def norm_low(s, t):
                for half in range(2):
                    tp_unit(4 * half, 4, slice(PART * t, PART * t + s.rows[t]))

            def normalise(s, src, xi, c, t, weight):
                rows = s.rows[t]
                dve.wait_ge(rstd_ready, xi + 1)
                nc.vector.scalar_tensor_tensor(xn[0:rows, xi % 2], src, rstd[0:rows, c:c + 1],
                                               weight[0:rows, :], ALU.mult, ALU.mult).then_inc(xn_ready, 1)

            def accumulate_unit(s, di, bank, t, nh):
                rows, cols = s.rows[t], slice(512 * nh, 512 * (nh + 1))
                dve.wait_ge(d_ready, di + 1)
                nc.vector.tensor_tensor(h[0:rows, t, cols], ps[0:rows, bank, :], h[0:rows, t, cols],
                                        ALU.add).then_inc(d_free, 1)

            def accumulate_tile(s, d0, parity, t):
                for nh in range(2):
                    accumulate_unit(s, d0 + 2 * t + nh, (2 * t + nh + s.d_of * parity) % 4, t, nh)

            def accumulate(s, d0, parity):
                for t in range(s.nt):
                    accumulate_tile(s, d0, parity, t)

            def boundary(prev, s):
                for t in range(max(prev.nt if prev else 0, s.nt + 1 if s else 0)):
                    if s and t < s.nt:
                        normalise(s, xload[0:s.rows[t], (s.x0 // 2 + t) % 2], s.x0 + t, t, t, g_mix)
                    if prev and t < prev.nt:
                        accumulate_tile(prev, prev.d_unit(D_GROUPS - 1, 0), 0, t)
                    if s and 1 <= t <= s.nt:
                        norm_low(s, t - 1)

            def normed(s, m, nb):
                kind, j, _ = SLABS[m]
                oi = s.oi(m, nb)
                dve.wait_ge(r_ready, oi + 1)
                dve.wait_ge(z_free, s.z_unit(m, nb) + 1)
                r = rr[:, oi % 2, 0:s.NB]
                if kind == "q":
                    q = qt_sb[:, j // 2 % 2, j % 2, nb * s.NB:(nb + 1) * s.NB]
                    nc.vector.tensor_tensor(q, q, r, ALU.mult).then_inc(fin_done, 1)
                    return
                z = zs[:, oi % 2, 0:s.NB]
                for g in ((0, 1), (2,))[j]:
                    src = slice(HD * (g % 2), HD * (g % 2 + 1))
                    for e in range(2):
                        for a, b in s.cuts(nb):
                            cols = slice(a - nb * s.NB, b - nb * s.NB)
                            last = nc.vector.tensor_tensor(
                                kt_sb[HD * e:HD * (e + 1), g, s.kcol(a):s.kcol(a) + b - a],
                                z[src, cols], r[src, cols], ALU.mult)
                last.then_inc(fin_done, 1)

            def restore_tails(s):
                if s.p == 0:
                    nc.vector.memset(ut_sb[:, :, 0:HALO], 0.0).then_inc(halo_ready, 1)
                    return
                nc.vector.tensor_copy(kt_sb[:, :, 0:PART], k_tail[:, :, :])
                nc.vector.tensor_copy(v_sb[:, 0, :], v_tail[:, :])
                nc.vector.tensor_copy(ut_sb[:, :, 0:HALO], u_tail[:, 0]).then_inc(halo_ready, 1)

            def save_tails(s):
                end = s.T - (DEC if s.has_sample else 0)
                dve.wait_ge(z_free, s.v_unit(s.nt - 1) + 1)
                dve.wait_ge(fin_done, s.o0 + 4)
                nc.vector.tensor_copy(k_tail[:, :, :], kt_sb[:, :, end:end + PART])
                nc.vector.tensor_copy(v_tail[:, :], v_sb[:, end // PART, :])
                if s.has_sample:
                    c = s.ucol(s.T - DEC) + DEC
                    nc.vector.tensor_copy(u_tail[:, 1], ut_sb[:, :, c - HALO:c])
                    nc.vector.tensor_copy(k_st[0:DEC, 2 * KV_DIM:3 * KV_DIM], v_sb[0:DEC, s.slot(4), :])
                nc.vector.tensor_copy(u_tail[:, 0], ut_sb[:, :, end:end + HALO]).then_inc(tails_saved, 1)

            def pool_means(s, b):
                n = HALO + s.T + (HALO if s.has_sample else 0)
                dve.wait_ge(windows_ready, 2 * s.p + b + 1)
                dve.wait_ge(tails_saved, s.p + 1)
                for half in range(2):
                    rows = slice(HD * half, HD * (half + 1))
                    last = nc.vector.scalar_tensor_tensor(
                        ut_sb[rows, b, HALO:n], win[rows, half, HALO:n], 1.0 / POOL_WINDOWS[2 * b + half],
                        ut_sb[rows, b, HALO:n], ALU.mult, ALU.subtract)
                last.then_inc(windows_used, 1)

            def pool_low(s, b):
                for nb in range(2):
                    mi, tok = 4 * s.p + 2 * b + nb, slice(nb * s.NB, (nb + 1) * s.NB)
                    dve.wait_ge(m_hi, mi + 1)
                    nc.vector.scalar_tensor_tensor(xt_lo[:, b, tok], ps[:, mi % 2, 0:s.NB], pscale[:, b:b + 1],
                                                   xt_hi[:, b, tok].bitcast(F32), ALU.mult,
                                                   ALU.subtract).then_inc(m_free, 1)

            def softmax_top(s, n):
                g, t = s.units[n]
                ai, rows = s.a0 + n, s.rows[t]
                c0, c1 = s.keys(t)
                b = ai % 2
                dve.wait_ge(qk_ready, ai + 1)
                need(dve, pt_ready, ai - 1)
                need(dve, e_ready, ai - 1)
                for hh in range(GQA):
                    e, j = hh % 2, hh // 2
                    last = nc.vector.scalar_tensor_tensor(
                        s_sb[0:rows, b, hh, c0:c1], dist[0:rows, c0:c1], SLOPES[GQA * g + hh],
                        ps[0:rows, 4 + e, 256 * j + c0:256 * j + c1], ALU.mult, ALU.add)
                last.then_inc(sc_free, 1)
                dve.wait_ge(sc_free, ai + 1)
                link(nc.vector.tensor_reduce(negmax[0:rows, b, :], s_sb[0:rows, b, :, c0:c1], AX.X, ALU.max,
                                             negate=True))
                link(nc.vector.tensor_tensor(negmax[0:rows, b, :], negmax[0:rows, b, :],
                                             nsink[0:rows, GQA * g:GQA * (g + 1)], ALU.min))
                nc.vector.tensor_tensor(esink[0:rows, b, :], negmax[0:rows, b, :],
                                        sink[0:rows, GQA * g:GQA * (g + 1)], ALU.add).then_inc(nm_ready, 1)

            def denominators(s, n):
                ai, rows = s.a0 + n, s.rows[s.units[n][1]]
                b = ai % 2
                dve.wait_ge(e_ready, ai + 1)
                link(nc.vector.tensor_tensor(den[0:rows, b, :], den[0:rows, b, :], esink[0:rows, b, :], ALU.add))
                link(nc.vector.reciprocal(rden[0:rows, b, :], den[0:rows, b, :]))

            def outputs(s, n):
                g, t = s.units[n]
                ai, rows = s.a0 + n, s.rows[t]
                dve.wait_ge(pv_ready, ai + 1)
                cols = slice(GQA * HD * g, GQA * HD * (g + 1))
                nc.vector.tensor_tensor(atok[0:rows, t, cols].rearrange("p (h d) -> p h d", h=GQA),
                                        ps[0:rows, 3, 0:GQA * HD].rearrange("p (h d) -> p h d", h=GQA),
                                        rden[0:rows, ai % 2, :].unsqueeze(2).to_broadcast([rows, GQA, HD]),
                                        ALU.mult).then_inc(o_done, 1)

            def attend(s):
                last = len(s.units) - 1
                softmax_top(s, 0)
                for n in range(last + 1):
                    if n < last:
                        softmax_top(s, n + 1)
                    for d in s.late_at(n):
                        if 1 <= d <= LATE:
                            normed(s, EARLY + (d - 1) // 2, (d - 1) % 2)
                    if MIX_AT <= n < MIX_AT + 2:
                        pool_low(s, n - MIX_AT)
                    denominators(s, n)
                    t = n - OUT_AT
                    if 0 <= t < s.nt:
                        dve.wait_ge(h_loaded[t], 16 * (s.p + 1))
                        for nh in range(2):
                            accumulate_unit(s, s.d_unit(0, t, nh), nh, t, nh)
                    if n >= 1:
                        outputs(s, n - 1)
                    if n in MEANS_AT:
                        pool_means(s, MEANS_AT.index(n))
                outputs(s, last)

            def activations(s, j, parity, bank0=6):
                for n in range(4):
                    gi = s.g0 + 4 * j + n
                    dve.wait_ge(silu_done, gi + 1)
                    dve.wait_ge(u_ready, gi + 1)
                    need(dve, ah_done, gi - 1)
                    need(dve, al_done, gi - 1)
                    nc.vector.tensor_tensor(aa[:, n % 2, 0:s.NB], ps[:, bank0 if n == 0 else 6 + n % 2, 0:s.NB],
                                            sg[:, n % 2, 0:s.NB], ALU.mult).then_inc(a_done, 1)
                    if n >= 1:
                        low_part(s, j, n - 1, parity)
                low_part(s, j, 3, parity)

            def low_part(s, j, n, parity):
                dve.wait_ge(ah_done, s.g0 + 4 * j + n + 1)
                at = (slice(None), parity, n // 2, slice((n % 2) * s.NB, (n % 2 + 1) * s.NB))
                nc.vector.tensor_tensor(act_lo[at], aa[:, n % 2, 0:s.NB], act_hi[at].bitcast(F32),
                                        ALU.subtract).then_inc(al_done, 1)

            nc.vector.memset(eps[:, :], EPS).then_inc(const_ready, 1)
            link(nc.vector.memset(u_tail[:, :, :, :], 0.0))
            dve.wait_ge(gmix_loaded, 16)
            prev = None
            for s in shapes:
                boundary(prev, s)
                restore_tails(s)
                if s.p == 0:
                    dve.wait_ge(const_loaded, 16 * N_CONST)
                    nc.vector.tensor_scalar(nsink[:, :], sink[:, :], -1.0, None, ALU.mult)\
                        .then_inc(const_ready, 1)
                    nc.vector.tensor_scalar(qg[:, :], qg[:, :], HD ** -0.5, None, ALU.mult)\
                        .then_inc(const_ready, 1)
                if s.has_sample:
                    c0 = PART * (s.slot(4) - 1)
                    for g in range(N_KV):
                        bank = tp_wait()
                        nc.vector.tensor_copy(kt_sb[HD:PART, g, c0:c0 + PART], bank[HD:PART, 0:PART])\
                            .then_inc(tp_free, 1)
                    u0 = s.ucol(s.T - DEC) - HIST
                    nc.vector.memset(ut_sb[:, :, u0 - 1:u0], 0.0)
                    bank = tp_wait()
                    nc.vector.tensor_copy(ut_sb[:, 1, u0:u0 + HIST], bank[:, HALO:HALO + HIST])\
                        .then_inc(tp_free, 1)
                for m in range(2, EARLY):
                    for nb in range(2):
                        normed(s, m, nb)
                save_tails(s)
                attend(s)
                if s.has_sample:
                    for n, rows in enumerate((PART, DEC)):
                        bank = tp_wait()
                        nc.vector.tensor_copy(k_st[0:rows, KV_DIM * n + 2 * HD:KV_DIM * (n + 1)],
                                              bank[0:rows, 2 * PART:2 * PART + HD]).then_inc(tp_free, 1)
                    bank = tp_wait()
                    nc.vector.tensor_copy(u_st[0:HIST, POOL_DIM:2 * POOL_DIM],
                                          bank[0:HIST, POOL_DIM:2 * POOL_DIM]).then_inc(tp_free, 1)
                for t in range(s.nt + 2):
                    if t < s.nt:
                        for half in range(2):
                            tp_unit(2 + 3 * half, 3, slice(PART * t, PART * t + s.rows[t]))
                    if t >= 2:
                        accumulate_tile(s, s.d_unit(1, 0), 1, t - 2)
                accumulate(s, s.d_unit(2, 0), 0)
                for t in range(s.nt):
                    accumulate_tile(s, s.d_unit(3, 0), 1, t)
                    if t >= 1:
                        normalise(s, h[0:s.rows[t - 1], t - 1], s.x0 + s.nt + t - 1, 8 + t - 1, t - 1, g_ffn)
                    if t >= 2:
                        norm_low(s, t - 2)
                t = s.nt - 1
                normalise(s, h[0:s.rows[t], t], s.x0 + s.nt + t, 8 + t, t, g_ffn)
                norm_low(s, t - 1)
                norm_low(s, t)
                down0 = s.d_unit(OUT_GROUPS, 0)
                activations(s, 0, 0, bank0=1)
                with dve.Fori(0, LOOPS) as i:
                    activations(s, 2 * i + 1, 1)
                    accumulate(s, down0 + s.d_of * (2 * i), 0)
                    activations(s, 2 * i + 2, 0)
                    accumulate(s, down0 + s.d_of * (2 * i + 1), 1)
                activations(s, GROUPS - 2, 1)
                accumulate(s, down0 + s.d_of * (GROUPS - 3), 0)
                activations(s, GROUPS - 1, 0)
                accumulate(s, down0 + s.d_of * (GROUPS - 2), 1)
                prev = s
            boundary(prev, None)


def constants():
    row, col = np.arange(PART)[:, None], np.arange(2 * PART)[None, :]
    chunk = (row // 64) * 64
    valid = (col >= chunk) & (col < chunk + PART + 64)
    dist = np.where(valid, -np.abs(row + PART - col), -1e30 / SLOPES[-1]).astype(np.float32)
    ident = np.eye(PART, dtype=np.float32)
    heads = np.kron(np.eye(2, dtype=np.float32), np.ones((HD, HD), np.float32))
    width = np.repeat(np.array(POOL_WINDOWS, np.float32), 64).reshape(2, PART).T[:, :, None]
    count = np.minimum(np.arange(1, HALO + 1, dtype=np.float32)[None, None, :], width)
    return {"c_dist": dist, "c_ident": ident, "c_ones": heads, "c_inv": (width / count).astype(np.float32)}


_INS = ['x_prompt', 'x_sample', 'cache_pool', 'cache_k', 'cache_v', 'norm_mix', 'w_in', 'w_pool', 'pool_scale',
        'q_norm', 'k_norm', 'sinks', 'w_out', 'norm_ffn', 'w_gate', 'w_up', 'w_down']
_OUTS = [(1, 2048, 1024), (1, 64, 1024), (1, 1, 15, 256), (1, 1, 128, 3, 64), (1, 1, 128, 3, 64),
         (1, 1, 15, 256), (1, 1, 128, 3, 64), (1, 1, 128, 3, 64)]


def kernel(**inputs):
    import concourse.bacc as bacc
    from concourse.bass_utils import run_bass_kernel_spmd

    nc = bacc.Bacc("TRN2", target_bir_lowering=False, num_devices=1)
    arrays, args = {}, []
    given = {name: np.ascontiguousarray(inputs[name]) for name in _INS} | constants()
    for name, a in given.items():
        arrays[f"in_{name}"] = a
        args.append(nc.dram_tensor(f"in_{name}", a.shape, mybir.dt.from_np(a.dtype), kind="ExternalInput").ap())
    for i, shape in enumerate(_OUTS):
        args.append(nc.dram_tensor(f"out_{i}", shape, F32, kind="ExternalOutput").ap())
    build(nc, *args)
    r = run_bass_kernel_spmd(nc, [arrays], core_ids=[0])
    return tuple(r.results[0][f"out_{i}"] for i in range(len(_OUTS)))
```

```python
from contextlib import ExitStack

import numpy as np

import concourse.bass as bass
from concourse import mybir

F32 = mybir.dt.float32
F32R = mybir.dt.float32r
ALU = mybir.AluOpType
ACT = mybir.ActivationFunctionType
AX = mybir.AxisListType

PART = 128
D_MODEL = 1024
KT = D_MODEL // PART
SEQ = 2048
DEC = 64
POOL_DIM = 256
N_KV = 3
GQA = 4
N_HEADS = N_KV * GQA
HD = 64
ATTN_DIM = N_HEADS * HD
KV_DIM = N_KV * HD
D_FF = 2816
HIST = 15
EPS = 1e-6
U0, Q0, K0, V0 = 0, POOL_DIM, POOL_DIM + ATTN_DIM, POOL_DIM + ATTN_DIM + KV_DIM
POOL_WINDOWS = (2, 4, 8, 16)

PARTS = 3
NT = (6, 6, 5)
TILE0 = (0, 6, 12)
TMAX = 6 * PART
SAMPLE_TILE = SEQ // PART
GROUPS = D_FF // 256
LOOPS = (GROUPS - 3) // 2
OUT_GROUPS = D_MODEL // 256
D_GROUPS = OUT_GROUPS + GROUPS
HALO = 16

SLABS = [("u", 0, U0), ("u", 1, U0 + 128), ("k", 0, K0), ("k", 1, K0 + 128), ("v", 0, V0 + 64)] + [
    ("q", j, Q0 + 128 * j) for j in range(6)]
V_SLAB = 4
EARLY = 7

OUT_ID = len(SLABS) + 1
DOWN_ID = OUT_ID + 4
RING1 = DOWN_ID - 1 + 2 * (GROUPS - 1)
USES1 = (RING1 // 2 + 1, RING1 // 2)
GATE_ID, LAST_ID = 4, 4 + 4 * GROUPS
RING2 = LAST_ID + 2
USES2 = (GROUPS + 2, GROUPS + 2, GROUPS + 1, GROUPS + 1)

LATE = 2 * (len(SLABS) - EARLY)
MEANS_AT = (1, 5)
SPLIT_SUMS = 7
SLOPES = [float(np.float32(2.0) ** np.float32(-8.0 * (h + 1) / N_HEADS)) for h in range(N_HEADS)]
EARLY_UNITS = [(m, nb) for m in range(2, EARLY) for nb in range(2)]
FIRST_UNITS = [(0, 0), (1, 0), (0, 1), (1, 1)]


def order1(block_id):
    return block_id - (block_id >= OUT_ID)


class Shape:

    def __init__(self, p):
        self.p, self.nt = p, NT[p]
        self.rows = [DEC if TILE0[p] + t == SAMPLE_TILE else PART for t in range(self.nt)]
        self.T = sum(self.rows)
        self.NB = self.T // 2
        self.units = [(g, t) for g in range(N_KV) for t in range(self.nt)]
        self.has_sample = p == PARTS - 1
        before = sum(NT[:p])
        self.x0 = 2 * before
        self.z0 = 2 * len(SLABS) * p
        self.o0 = 16 * p
        self.a0 = 3 * before
        self.d0 = 2 * D_GROUPS * before
        self.g0 = 4 * GROUPS * p
        self.d_of = 2 * self.nt
        self.mix_at = self.nt + 2
        self.out_at = self.nt + 3
        self.out1_early = len(self.units) - self.out_at - self.nt

    def xi(self, t):
        return self.x0 // 2 - NT[0] + t

    def z_unit(self, m, nb):
        if m < 2:
            return self.z0 + FIRST_UNITS.index((m, nb))
        return self.z0 + 2 * m + nb

    def oi(self, m, nb):
        return self.o0 + 2 * (m - 2 - (m > V_SLAB)) + nb

    def whole(self, oi):
        return oi >= self.o0 + SPLIT_SUMS

    def splits(self, oi):
        return SPLIT_SUMS * self.p + min(oi - self.o0, SPLIT_SUMS)

    def loads1(self, block_id):
        slot = block_id % 2
        return USES1[slot] * self.p + block_id // 2 + 1 - (slot == 1 and block_id > OUT_ID)

    def d_unit(self, group, t, nh=0):
        return self.d0 + self.d_of * group + 2 * t + nh

    def late_unit(self, n):
        d = n + 1 if n < 3 else n - self.nt + 6
        return d if d < 4 and n < 3 or 4 <= d < LATE else None

    def dense_first(self, n):
        return 2 <= n < self.mix_at

    def v_tiles(self, m, nb):
        first = 2 * (2 * (m - V_SLAB - 1) + nb) - 2
        return range(first, min(first + 2, self.nt)) if first >= 0 else ()

    def bank(self, parity, t, nh):
        return (2 * t + nh + 2 + self.d_of * parity) % 4

    def cuts(self, nb):
        a, b = nb * self.NB, (nb + 1) * self.NB
        s = self.T - DEC
        if self.has_sample and a < s < b:
            return [(a, s), (s, b)]
        return [(a, b)]

    def kcol(self, tok):
        return PART + tok + (PART if self.has_sample and tok >= self.T - DEC else 0)

    def ucol(self, tok):
        return HALO + tok + (HALO if self.has_sample and tok >= self.T - DEC else 0)

    def slot(self, t):
        return self.kcol(PART * t) // PART

    def keys(self, t):
        if TILE0[self.p] + t == 0:
            return PART, 2 * PART
        if TILE0[self.p] + t == SAMPLE_TILE:
            return 0, PART + DEC
        return 0, 2 * PART


def build(nc, x_prompt, x_sample, cache_pool, cache_k, cache_v, norm_mix, w_in, w_pool, pool_scale,
          q_norm, k_norm, sinks, w_out, norm_ffn, w_gate, w_up, w_down,
          c_dist, c_ident, c_ones, c_inv,
          y_prompt, y_sample, np_prompt, nk_prompt, nv_prompt, np_sample, nk_sample, nv_sample):
    ctx = ExitStack()
    with ctx:
        def sb(name, shape, dt=F32, scope=ctx):
            return scope.enter_context(nc.sbuf_tensor(name, shape, dt))

        def sem(name):
            return ctx.enter_context(nc.semaphore(name))

        ps = ctx.enter_context(nc.psum_tensor("ps", [PART, 8, 512], F32))

        xt_hi = sb("xt_hi", [PART, KT, TMAX], F32R)
        xt_lo = sb("xt_lo", [PART, KT, TMAX], F32R)
        h = sb("h", [PART, 6, D_MODEL])
        raw1 = sb("raw1", [PART, 2, 1024])
        w1_hi = sb("w1_hi", [PART, 2, 1024], F32R)
        w1_lo = sb("w1_lo", [PART, 2, 1024], F32R)
        g_mix = sb("g_mix", [PART, D_MODEL])
        g_ffn = sb("g_ffn", [PART, D_MODEL])
        dist = sb("dist", [PART, 256])
        ident = sb("ident", [PART, PART])
        headsum = sb("headsum", [PART, PART])
        headsum_r = sb("headsum_r", [PART, PART], F32R)
        wpool = sb("wpool", [PART, 2, PART])
        inv = sb("inv", [PART, 2, HALO])
        pscale = sb("pscale", [PART, 2])
        qg = sb("qg", [PART, 1])
        kg = sb("kg", [PART, 1])
        sink = sb("sink", [PART, N_HEADS])
        nsink = sb("nsink", [PART, N_HEADS])
        eps = sb("eps", [PART, 1])
        xload = sb("xload", [PART, 2, D_MODEL])
        xn = sb("xn", [PART, 2, D_MODEL])
        win = xn.rearrange("p b n -> p (b n)")[:, 0:2 * (HALO + TMAX)].rearrange("p (b n) -> p b n", b=2)
        ss = sb("ss", [PART, 16])
        rstd = sb("rstd", [PART, 16])
        negmax = sb("negmax", [PART, 2, GQA])
        esink = sb("esink", [PART, 2, GQA])
        den = sb("den", [PART, 2, GQA])
        rden = sb("rden", [PART, 2, GQA])
        k_tail = sb("k_tail", [PART, N_KV, PART])
        v_tail = sb("v_tail", [PART, KV_DIM])
        u_tail = sb("u_tail", [PART, 2, 2, HALO])

        with ExitStack() as attend:
            atok = sb("atok", [PART, 6, ATTN_DIM], scope=attend)
            qt_sb = sb("qt_sb", [PART, 2, 2, TMAX], scope=attend)
            s_sb = sb("s_sb", [PART, 2, GQA, 256], scope=attend)
            pt_sb = sb("pt_sb", [PART, 2, 2, GQA * PART], scope=attend)
            zs = sb("zs", [PART, 2, TMAX // 2], scope=attend)
            sq = sb("sq", [PART, 2, TMAX // 2], scope=attend)
            sq_hi = sb("sq_hi", [PART, TMAX // 2], F32R, scope=attend)
            sq_lo = sb("sq_lo", [PART, TMAX // 2], F32R, scope=attend)
            rr = sb("rr", [PART, 2, TMAX // 2], scope=attend)
            kt_sb = sb("kt_sb", [PART, N_KV, PART + TMAX], scope=attend)
            v_sb = sb("v_sb", [PART, 7, KV_DIM], scope=attend)
            ut_sb = sb("ut_sb", [PART, 2, HALO + TMAX], scope=attend)
        ck_st = pt_sb[:, 0, 0, 0:2 * KV_DIM].rearrange("p (g e d) -> p g e d", g=N_KV, e=2)
        cp_st = pt_sb[:, 1, 0, 0:POOL_DIM]
        vt_sb = s_sb.rearrange("p b h k -> p b (h k)")
        k_st, u_st = qt_sb[:, 0, 0], qt_sb[:, 1, 0]
        with ExitStack() as ffn:
            act_hi = sb("act_hi", [PART, 2, 2, TMAX], F32R, scope=ffn)
            act_lo = sb("act_lo", [PART, 2, 2, TMAX], F32R, scope=ffn)
            sg = sb("sg", [PART, 2, TMAX // 2], scope=ffn)
            aa = sb("aa", [PART, 2, TMAX // 2], scope=ffn)
            raw2 = sb("raw2", [PART, 4, 1024], scope=ffn)
            w2_hi = sb("w2_hi", [PART, 4, 1024], F32R, scope=ffn)
            w2_lo = sb("w2_lo", [PART, 4, 1024], F32R, scope=ffn)

        ident_loaded = sem("ident_loaded")
        gmix_loaded = sem("gmix_loaded")
        const_loaded = sem("const_loaded")
        wpool_zero = sem("wpool_zero")
        const_ready = sem("const_ready")
        headsum_ready = sem("headsum_ready")
        x_loaded = [sem(f"x_loaded{i}") for i in range(2)]
        h_loaded = [sem(f"h_loaded{t}") for t in range(6)]
        raw1_loaded = [sem(f"raw1_loaded{i}") for i in range(2)]
        raw2_loaded = [sem(f"raw2_loaded{i}") for i in range(4)]
        cache_loaded = sem("cache_loaded")
        hi_done = sem("hi_done")
        split1 = sem("split1")
        split2 = sem("split2")
        pool_step = sem("pool_step")
        act_step = sem("act_step")
        dve_step = sem("dve_step")
        rstd_ready = sem("rstd_ready")
        xn_ready = sem("xn_ready")
        tp_ready = sem("tp_ready")
        tp_hi = sem("tp_hi")
        tp_free = sem("tp_free")
        z_ready = sem("z_ready")
        z_free = sem("z_free")
        sq_ready = sem("sq_ready")
        sq_high = sem("sq_high")
        sq_low = sem("sq_low")
        ss_ready = sem("ss_ready")
        ss_free = sem("ss_free")
        r_ready = sem("r_ready")
        fin_done = sem("fin_done")
        halo_ready = sem("halo_ready")
        tails_saved = sem("tails_saved")
        windows_ready = sem("windows_ready")
        windows_used = sem("windows_used")
        m_ready = sem("m_ready")
        m_hi = sem("m_hi")
        m_free = sem("m_free")
        group0_ready = sem("group0_ready")
        group0_hi = sem("group0_hi")
        group0_free = sem("group0_free")
        qk_ready = sem("qk_ready")
        sc_free = sem("sc_free")
        nm_ready = sem("nm_ready")
        e_ready = sem("e_ready")
        pt_ready = sem("pt_ready")
        pt_done = sem("pt_done")
        pv_ready = sem("pv_ready")
        o_done = sem("o_done")
        d_ready = sem("d_ready")
        d_free = sem("d_free")
        half_sum = sem("half_sum")
        g_ready = sem("g_ready")
        u_ready = sem("u_ready")
        silu_done = sem("silu_done")
        a_done = sem("a_done")
        ah_done = sem("ah_done")
        al_done = sem("al_done")
        y_stored = [sem(f"y_stored{t}") for t in range(6)]
        state_stored = sem("state_stored")

        N_CONST = 12
        HI_BLOCKS = RING1 + RING2
        shapes = [Shape(p) for p in range(PARTS)]
        TP_CACHE, TP_STATE = N_KV + 1, 3
        tp_total = [6 * s.nt + (TP_CACHE + TP_STATE if s.has_sample else 0) for s in shapes]

        def state_read(s):
            return sum(tp_total[:s.p + 1]) - 3 * s.nt

        w_in_k = w_in[0].rearrange("(k p) n -> p k n", p=PART)
        w_gate_k = w_gate[0].rearrange("(k p) n -> p k n", p=PART)
        w_up_k = w_up[0].rearrange("(k p) n -> p k n", p=PART)

        def tile_dram(prompt, sample, t):
            return sample[0] if t == SAMPLE_TILE else prompt[0, PART * t:PART * (t + 1), :]

        def need(eng, semaphore, value):
            if not isinstance(value, int) or value > 0:
                eng.wait_ge(semaphore, value)

        block = ctx.enter_context(nc.Block())

        @block.sync
        def _(sp):
            def load_const(dst, src, semaphore=const_loaded):
                sp.dma_start(dst, src, allow_slow_non_contiguous=True).then_inc(semaphore, 16)

            def load_x(s, t):
                b = s.xi(t) % 2
                if s.xi(t) >= 2:
                    before = s.x0 + t - 2 if t >= 2 else shapes[s.p - 1].x0 + shapes[s.p - 1].nt + t - 2
                    sp.wait_ge(xn_ready, before + 1)
                sp.dma_start(xload[0:s.rows[t], b], tile_dram(x_prompt, x_sample, TILE0[s.p] + t))\
                    .then_inc(x_loaded[b], 16)

            def load_h(s, t):
                need(sp, y_stored[t], 16 * s.p)
                sp.dma_start(h[0:s.rows[t], t], tile_dram(x_prompt, x_sample, TILE0[s.p] + t))\
                    .then_inc(h_loaded[t], 16)

            def ring1(s, block_id, dst, src):
                need(sp, split1, RING1 * s.p + order1(block_id) - (block_id != OUT_ID))
                sp.dma_start(dst, src).then_inc(raw1_loaded[block_id % 2], 16)

            def load_slab(s, m):
                ring1(s, m, raw1[:, m % 2].rearrange("p (k m) -> p k m", k=KT),
                      w_in_k[:, :, SLABS[m][2]:SLABS[m][2] + PART])

            def load_out(s, b):
                rows = w_out[0, PART * b:PART * (b + 1), :]
                if b < 4:
                    ring1(s, OUT_ID + b, raw1[:, b % 2], rows)
                else:
                    need(sp, split2, RING2 * s.p + b - 4 - 3)
                    sp.dma_start(raw2[:, b - 4], rows).then_inc(raw2_loaded[b - 4], 16)

            def load_gate_up(s, j):
                for n in range(4):
                    sp.wait_ge(split2, RING2 * s.p + GATE_ID + 4 * j + n - 3)
                    w = (w_gate_k, w_up_k)[n % 2]
                    sp.dma_start(raw2[:, n].rearrange("p (k m) -> p k m", k=KT),
                                 w[:, :, bass.ds(256 * j + PART * (n // 2), PART)])\
                        .then_inc(raw2_loaded[n], 16)

            def load_down(s, j):
                for c in range(2):
                    sp.wait_ge(split1, RING1 * s.p + order1(DOWN_ID) + 2 * j + c - 1)
                    sp.dma_start(raw1[:, c], w_down[0, bass.ds(256 * j + PART * c, PART), :])\
                        .then_inc(raw1_loaded[c], 16)

            for s in shapes:
                if s.p == 0:
                    load_h(s, 0)
                    load_const(ident[:, :], c_ident, ident_loaded)
                    load_const(g_mix[:, :], norm_mix.partition_broadcast(PART)[:, 0, :], gmix_loaded)
                    load_h(s, 1)
                    load_h(s, 2)
                    load_slab(s, 0)
                    load_h(s, 3)
                    load_slab(s, 1)
                    load_h(s, 4)
                    load_h(s, 5)
                else:
                    load_x(s, 0)
                    load_x(s, 1)
                    load_slab(s, 0)
                    load_slab(s, 1)
                if s.p == 0:
                    sp.wait_ge(wpool_zero, 1)
                    for e in range(2):
                        load_const(qg[HD * e:HD * (e + 1), :], q_norm.rearrange("a d -> d a"))
                        load_const(kg[HD * e:HD * (e + 1), :], k_norm.rearrange("a d -> d a"))
                    load_const(headsum[:, :], c_ones)
                    load_const(sink[:, :], sinks.partition_broadcast(PART)[:, 0, :])
                    load_const(pscale[:, :], pool_scale[0].rearrange("(s p) -> p s", p=PART))
                    for e in range(2):
                        load_const(wpool[HD * e:HD * (e + 1), :, HD * e:HD * (e + 1)],
                                   w_pool[0].rearrange("(s e) c d -> e c s d", e=2)[e])
                    load_const(inv[:, :, :], c_inv)
                    load_const(g_ffn[:, :], norm_ffn.partition_broadcast(PART)[:, 0, :])
                    load_const(dist[:, :], c_dist)
                for t in range(2, s.nt if s.p > 0 else 0):
                    load_x(s, t)
                if s.has_sample:
                    sp.wait_ge(d_ready, s.d0)
                    for e in range(2):
                        sp.dma_start(ck_st[:, :, e, :], cache_k[0, 0]).then_inc(cache_loaded, 16)
                    sp.dma_start(cp_st[0:HIST, :], cache_pool[0, 0]).then_inc(cache_loaded, 16)
                    sp.dma_start(v_sb[:, s.slot(4) - 1, :], cache_v[0, 0].rearrange("r g d -> r (g d)"))\
                        .then_inc(cache_loaded, 16)
                for m in range(2, EARLY):
                    load_slab(s, m)
                for t in range(s.nt if s.p > 0 else 0):
                    load_h(s, t)
                for m in range(EARLY, len(SLABS)):
                    load_slab(s, m)
                for b in range(4):
                    load_out(s, b)
                sp.wait_ge(pv_ready, s.a0 + len(s.units))
                if s.has_sample:
                    sp.wait_ge(tp_free, state_read(s))
                for b in range(4, 8):
                    load_out(s, b)
                load_gate_up(s, 0)
                load_gate_up(s, 1)
                with sp.Fori(0, LOOPS) as i:
                    for half in range(2):
                        load_down(s, 2 * i + half)
                        load_gate_up(s, 2 * i + half + 2)
                load_down(s, GROUPS - 3)
                load_gate_up(s, GROUPS - 1)
                load_down(s, GROUPS - 2)
                for c in range(2):
                    sp.wait_ge(split2, RING2 * s.p + LAST_ID + c - 3)
                    r = 256 * (GROUPS - 1) + PART * c
                    sp.dma_start(raw2[:, c], w_down[0, r:r + PART, :]).then_inc(raw2_loaded[c], 16)

        @block.gpsimd
        def _(pool):
            steps = [0]

            def link(ins):
                steps[0] += 1
                ins.then_inc(pool_step, 1)
                pool.wait_ge(pool_step, steps[0])

            def low(raw, hi, lo, done, number):
                pool.wait_ge(hi_done, number)
                nc.gpsimd.tensor_tensor(lo, raw, hi.bitcast(F32), ALU.subtract).then_inc(done, 1)

            def low1(block_id, number):
                b = block_id % 2
                low(raw1[:, b], w1_hi[:, b], w1_lo[:, b], split1, number)

            def low2(slot, number):
                low(raw2[:, slot], w2_hi[:, slot], w2_lo[:, slot], split2, number)

            def windows(s, b):
                n = HALO + s.T + (HALO if s.has_sample else 0)
                u = ut_sb[:, b]
                if b == 0:
                    pool.wait_ge(z_free, s.z_unit(1, 1) + 1)
                    pool.wait_ge(halo_ready, s.p + 1)
                    if s.has_sample:
                        pool.wait_ge(tp_free, sum(tp_total[:s.p]) + 2 * s.nt + TP_CACHE)
                else:
                    pool.wait_ge(windows_used, 2 * s.p + 1)
                levels = [u] + [win[:, 0], win[:, 1]][:1 + b] + ([win[:, 0]] if b else [])
                w = 1
                for src, dst in zip(levels, levels[1:]):
                    w *= 2
                    link(nc.gpsimd.tensor_tensor(dst[:, w:n], src[:, w:n], src[:, w - w // 2:n - w // 2],
                                                 ALU.add))
                top, w = slice(HD, PART), 2 * w
                assert POOL_WINDOWS[2 * b:2 * b + 2] == (w // 2, w)
                ins = nc.gpsimd.tensor_tensor(win[top, 1, w:n], win[top, 0, w:n],
                                              win[top, 0, w - w // 2:n - w // 2], ALU.add)
                if s.p == 0:
                    pool.wait_ge(const_loaded, 16 * N_CONST)
                    link(ins)
                    link(nc.gpsimd.tensor_tensor(win[0:HD, 0, HALO:2 * HALO], win[0:HD, 0, HALO:2 * HALO],
                                                 inv[0:HD, b, :], ALU.mult))
                    ins = nc.gpsimd.tensor_tensor(win[top, 1, HALO:2 * HALO], win[top, 1, HALO:2 * HALO],
                                                  inv[top, b, :], ALU.mult)
                ins.then_inc(windows_ready, 1)
                pool.wait_ge(windows_ready, 2 * s.p + b + 1)

            nc.gpsimd.memset(wpool[:, :, :], 0.0).then_inc(wpool_zero, 1)
            done = 0
            for s in shapes:
                for block_id in list(range(len(SLABS))) + [OUT_ID, OUT_ID + 1]:
                    done += 1
                    if done <= 2:
                        pool.wait_ge(raw1_loaded[block_id], 16)
                        nc.gpsimd.tensor_copy(w1_hi[:, block_id], raw1[:, block_id]).then_inc(hi_done, 1)
                    low1(block_id, done)
                    if block_id == EARLY:
                        windows(s, 0)
                    if block_id == EARLY + 2:
                        windows(s, 1)
                done += 2
                for slot in (0, 1, 2, 3) * 3:
                    done += 1
                    low2(slot, done)
                with pool.Fori(0, LOOPS) as i:
                    for n in range(12):
                        number = done + 12 * i + n + 1
                        if n % 6 < 2:
                            low1(n % 6, number)
                        else:
                            low2(n % 6 - 2, number)
                done += 12 * LOOPS
                for ring, slot in ((1, 0), (1, 1), (2, 0), (2, 1), (2, 2), (2, 3), (1, 0), (1, 1),
                                   (2, 0), (2, 1)):
                    done += 1
                    (low1 if ring == 1 else low2)(slot, done)

        @block.tensor
        def _(pe):
            tp = [0]

            def split_products(out, w_hi, w_lo, m_hi, m_lo, first, last):
                nc.tensor.matmul(out, w_hi, m_hi, start=first, stop=False)
                nc.tensor.matmul(out, w_hi, m_lo, start=False, stop=False)
                return nc.tensor.matmul(out, w_lo, m_hi, start=False, stop=last)

            def tp_bank():
                need(pe, tp_free, tp[0] - 3)
                tp[0] += 1
                return ps[:, 4 + (tp[0] - 1) % 4]

            def transposed(src, cols, rows):
                bank = tp_bank()
                for n, c in enumerate(cols):
                    last = nc.tensor.transpose(bank[:, n * rows:(n + 1) * rows],
                                               src[0:rows, PART * c:PART * (c + 1)], ident[0:rows, 0:rows])
                last.then_inc(tp_ready, 1)

            def norm_transposes(s, x0, t):
                pe.wait_ge(xn_ready, x0 + t + 1)
                for half in range(2):
                    transposed(xn[:, (x0 + t) % 2], range(4 * half, 4 * half + 4), s.rows[t])

            def mix_transposes(s, t):
                pe.wait_ge(o_done, s.a0 + 2 * s.nt + t + 1)
                transposed(atok[:, t], range(2, 6), s.rows[t])

            def group0_transposes(s, t):
                n, rows = s.x0 // 2 + t, s.rows[t]
                pe.wait_ge(ss_free, s.o0 + 16)
                need(pe, group0_free, n)
                for c in range(2):
                    last = nc.tensor.transpose(ps[:, 2, c * rows:(c + 1) * rows],
                                               atok[0:rows, t, PART * c:PART * (c + 1)],
                                               ident[0:rows, 0:rows])
                last.then_inc(group0_ready, 1)

            def cache_transposes(s):
                pe.wait_ge(cache_loaded, 16 * 4)
                for g in range(N_KV):
                    bank = tp_bank()
                    nc.tensor.transpose(bank[:, 0:PART], ck_st[:, g].rearrange("p e d -> p (e d)"),
                                        ident[:, :]).then_inc(tp_ready, 1)
                bank = tp_bank()
                for b in range(2):
                    last = nc.tensor.transpose(bank[:, HALO * b:HALO * b + HIST],
                                               cp_st[0:HIST, PART * b:PART * (b + 1)], ident[0:HIST, 0:HIST])
                last.then_inc(tp_ready, 1)

            def state_transposes(s):
                pe.wait_ge(tails_saved, s.p + 1)
                for c0, rows in ((s.kcol(3 * PART), PART), (s.kcol(4 * PART), DEC)):
                    bank = tp_bank()
                    for g in range(N_KV):
                        last = nc.tensor.transpose(bank[0:rows, PART * g:PART * (g + 1)],
                                                   kt_sb[:, g, c0:c0 + rows], ident[:, :])
                    last.then_inc(tp_ready, 1)
                bank = tp_bank()
                for w in range(2):
                    for b in range(2):
                        n = 2 * w + b
                        last = nc.tensor.transpose(bank[0:HIST, PART * n:PART * (n + 1)],
                                                   u_tail[:, w, b, 1:HALO], ident[:, :])
                last.then_inc(tp_ready, 1)

            def v_transposes(s, t):
                rows, bank = s.rows[t], tp_bank()
                pe.wait_ge(z_free, s.z_unit(V_SLAB, 1) + 1)
                for c in range(2):
                    last = nc.tensor.transpose(bank[0:rows, PART * c:PART * (c + 1)],
                                               vt_sb[:, c, PART * t:PART * t + rows], ident[:, :])
                last.then_inc(tp_ready, 1)

            def slab_unit(s, m, nb):
                zi, slot = s.z_unit(m, nb), m % 2
                pe.wait_ge(split1, RING1 * s.p + m + 1)
                need(pe, z_free, zi - 1)
                out = ps[:, zi % 2, 0:s.NB]
                tok = slice(nb * s.NB, (nb + 1) * s.NB)
                for k in range(KT):
                    cols = slice(PART * k, PART * (k + 1))
                    last = split_products(out, w1_hi[:, slot, cols], w1_lo[:, slot, cols],
                                          xt_hi[:, k, tok], xt_lo[:, k, tok], k == 0, k == KT - 1)
                last.then_inc(z_ready, 1)

            def head_sums(s, oi):
                need(pe, ss_free, oi)
                if s.whole(oi):
                    pe.wait_ge(sq_ready, oi + 1)
                    nc.tensor.matmul(ps[:, 2, 0:s.NB], headsum[:, :], sq[:, oi % 2, 0:s.NB],
                                     start=True, stop=True).then_inc(ss_ready, 1)
                    return
                pe.wait_ge(sq_low, s.splits(oi) + 1)
                nc.tensor.matmul(ps[:, 2, 0:s.NB], headsum_r[:, :], sq_hi[:, 0:s.NB], start=True, stop=False)
                nc.tensor.matmul(ps[:, 2, 0:s.NB], headsum_r[:, :], sq_lo[:, 0:s.NB],
                                 start=False, stop=True).then_inc(ss_ready, 1)

            def scores(s, n):
                g, t = s.units[n]
                ai, rows = s.a0 + n, s.rows[t]
                c0, c1 = s.keys(t)
                pe.wait_ge(fin_done, s.o0 + 8 + 4 * g)
                need(pe, sc_free, ai)
                k0 = PART * (s.slot(t) - 1)
                for hh in range(GQA):
                    e, j = hh % 2, hh // 2
                    last = nc.tensor.matmul(ps[0:rows, 4 + e, 256 * j + c0:256 * j + c1],
                                            qt_sb[HD * e:HD * (e + 1), g % 2, j, PART * t:PART * t + rows],
                                            kt_sb[HD * e:HD * (e + 1), g, k0 + c0:k0 + c1],
                                            start=True, stop=True)
                last.then_inc(qk_ready, 1)

            def prob_transposes(s, n):
                ai, rows = s.a0 + n, s.rows[s.units[n][1]]
                c0, c1 = s.keys(s.units[n][1])
                pe.wait_ge(e_ready, ai + 1)
                need(pe, pt_done, ai)
                for half in range(2):
                    a, b = max(c0, PART * half), min(c1, PART * (half + 1))
                    if a >= b:
                        continue
                    for hh in range(GQA):
                        last = nc.tensor.transpose(ps[0:b - a, 6 + half, rows * hh:rows * (hh + 1)],
                                                   s_sb[0:rows, ai % 2, hh, a:b], ident[0:rows, 0:rows])
                last.then_inc(pt_ready, 1)

            def weighted_values(s, n):
                g, t = s.units[n]
                ai, rows = s.a0 + n, s.rows[t]
                c0, c1 = s.keys(t)
                pe.wait_ge(pt_done, ai + 1)
                need(pe, o_done, ai)
                for hh in range(GQA):
                    for half in range(2):
                        a, b = max(c0, PART * half), min(c1, PART * (half + 1))
                        if a >= b:
                            continue
                        last = nc.tensor.matmul(ps[0:rows, 3, HD * hh:HD * (hh + 1)],
                                                pt_sb[0:b - a, ai % 2, half, rows * hh:rows * (hh + 1)],
                                                v_sb[0:b - a, s.slot(t) - 1 + half, HD * g:HD * (g + 1)],
                                                start=a == c0, stop=half == 1)
                last.then_inc(pv_ready, 1)

            def pool_map(s, b):
                pe.wait_ge(windows_used, 2 * s.p + b + 1)
                pe.wait_ge(z_free, s.z0 + 2 * len(SLABS))
                for nb in range(2):
                    mi = 4 * s.p + 2 * b + nb
                    need(pe, m_free, mi - 1)
                    for a, e in s.cuts(nb):
                        last = nc.tensor.matmul(ps[:, mi % 2, a - nb * s.NB:e - nb * s.NB], wpool[:, b, :],
                                                ut_sb[:, b, s.ucol(a):s.ucol(a) + e - a],
                                                start=True, stop=True)
                    last.then_inc(m_ready, 1)

            def add_unit(s, bank, t, nh, w_hi, w_lo, m_hi, m_lo):
                rows, cols = s.rows[t], slice(512 * nh, 512 * (nh + 1))
                tok = slice(PART * t, PART * t + rows)
                if rows < PART:
                    both = slice(tok.start, tok.start + PART)
                    nc.tensor.matmul(ps[:, bank, :], m_hi[:, 0, both], w_hi[:, 0, cols], start=True, stop=False)
                    for c in range(2):
                        nc.tensor.matmul(ps[0:rows, bank, :], m_hi[:, c, tok], w_lo[:, c, cols],
                                         start=False, stop=False)
                    nc.tensor.matmul(ps[:, bank, :], m_hi[:, 1, both], w_hi[:, 1, cols], start=False,
                                     stop=True).then_inc(d_ready, 1)
                    return
                for c in range(2):
                    last = split_products(ps[0:s.rows[t], bank, :], m_hi[:, c, tok], m_lo[:, c, tok],
                                          w_hi[:, c, cols], w_lo[:, c, cols], c == 0, c == 1)
                last.then_inc(d_ready, 1)

            def add_tile(s, d0, parity, t, *operands):
                for nh in range(2):
                    add_half(s, d0, parity, t, nh, *operands)

            def add_half(s, d0, parity, t, nh, *operands):
                need(pe, d_free, d0 + 2 * t + nh - 3)
                add_unit(s, s.bank(parity, t, nh), t, nh, *operands)

            def out_tile(s, j, t):
                if j == 1:
                    pe.wait_ge(group0_free, s.x0 // 2 + t + 1)
                for nh in range(2):
                    need(pe, d_free, s.d_unit(j, t, nh) - 1)
                    add_unit(s, nh, t, nh, *out_operands(j))

            def out_operands(j):
                w_hi, w_lo = (w1_hi, w1_lo) if j < 2 else (w2_hi, w2_lo)
                slots = slice(0, 2) if j < 3 else slice(2, 4)
                return (w_hi[:, slots], w_lo[:, slots], xt_hi[:, 2 * j:2 * j + 2], xt_lo[:, 2 * j:2 * j + 2])

            def late_unit(s, n):
                d = s.late_unit(n)
                if d is not None:
                    slab_unit(s, EARLY + d // 2, d % 2)

            def late_sums(s, n):
                d = s.late_unit(n - 1)
                if d is not None:
                    head_sums(s, s.o0 + 8 + d)

            def attend(s):
                last = len(s.units) - 1
                late_unit(s, -1)
                scores(s, 0)
                late_unit(s, 0)
                head_sums(s, s.o0 + 8)
                for n in range(last + 1):
                    if n == 1:
                        late_unit(s, 1)
                    if n < last:
                        scores(s, n + 1)
                    if n == 1:
                        head_sums(s, s.o0 + 9)
                    if s.dense_first(n):
                        late_sums(s, n)
                        late_unit(s, n)
                    if n == last:
                        out_tile(s, *divmod(n - s.out_at, s.nt))
                    if n == s.mix_at:
                        pool_map(s, 0)
                    prob_transposes(s, n)
                    t = n - s.out_at
                    if 0 <= t < s.nt:
                        group0_transposes(s, t)
                    if n >= 1:
                        weighted_values(s, n - 1)
                    if n >= s.mix_at:
                        late_sums(s, n)
                    if n == s.mix_at:
                        pool_map(s, 1)
                    if t == 0:
                        pe.wait_ge(m_free, 4 * s.p + 4)
                    if t in (0, s.nt):
                        pe.wait_ge(split1, RING1 * s.p + order1(OUT_ID) + 2 + 2 * (t > 0))
                    if t >= 0 and n < last:
                        out_tile(s, *divmod(t, s.nt))
                weighted_values(s, last)

            def gate_up_unit(s, j, c, nb, which, bank):
                slot = 2 * c + which
                gi = s.g0 + 4 * j + 2 * c + nb
                pe.wait_ge(split2, RING2 * s.p + GATE_ID + 4 * j + slot + 1)
                need(pe, (silu_done, a_done)[which], gi - 1)
                out, tok = ps[:, bank, 0:s.NB], slice(nb * s.NB, (nb + 1) * s.NB)
                for k in range(KT):
                    cols = slice(PART * k, PART * (k + 1))
                    last = split_products(out, w2_hi[:, slot, cols], w2_lo[:, slot, cols],
                                          xt_hi[:, k, tok], xt_lo[:, k, tok], k == 0, k == KT - 1)
                last.then_inc((g_ready, u_ready)[which], 1)

            def gate_up(s, j, first=0):
                for n in range(first, 4):
                    for which in range(2):
                        gate_up_unit(s, j, n // 2, n % 2, which, 4 + 2 * which + n % 2)

            def down(s, j, parity):
                pe.wait_ge(split1, RING1 * s.p + order1(DOWN_ID) + 2 * j + 2)
                pe.wait_ge(al_done, s.g0 + 4 * j + 4)
                for t in range(s.nt):
                    add_tile(s, s.d0 + s.d_of * (OUT_GROUPS + j), parity, t, w1_hi, w1_lo,
                             act_hi[:, parity], act_lo[:, parity])

            def boundary(prev, s):
                if prev:
                    pe.wait_ge(split2, RING2 * prev.p + RING2)
                    pe.wait_ge(al_done, prev.g0 + 4 * GROUPS)
                if s:
                    need(pe, a_done, s.g0)
                start = tp[0]
                for t in range(max(prev.nt if prev else 0, s.nt if s else 0)):
                    if prev and t < prev.nt:
                        add_tile(prev, prev.d_unit(D_GROUPS - 1, 0), 0, t, w2_hi[:, 0:2], w2_lo[:, 0:2],
                                 act_hi[:, 0], act_lo[:, 0])
                    if s and t < s.nt:
                        norm_transposes(s, s.x0, t)
                    if not prev and t in (3, 5):
                        pe.wait_ge(tp_free, start + 6)
                        slab_unit(s, *FIRST_UNITS[t // 4])

            pe.wait_ge(ident_loaded, 16)
            prev = None
            for s in shapes:
                xt_start = tp[0]
                boundary(prev, s)
                need(pe, d_free, s.d0)
                for m, nb in FIRST_UNITS[0 if prev else 2:]:
                    pe.wait_ge(tp_free, xt_start + (2 * -(-s.NB // PART), 2 * s.nt)[nb])
                    slab_unit(s, m, nb)
                if s.has_sample:
                    cache_transposes(s)
                if s.p == 0:
                    pe.wait_ge(const_loaded, 16 * N_CONST)
                    pe.wait_ge(headsum_ready, 1)
                for n, (m, nb) in enumerate(EARLY_UNITS):
                    slab_unit(s, m, nb)
                    if n > 0 and EARLY_UNITS[n - 1][0] != V_SLAB:
                        head_sums(s, s.oi(*EARLY_UNITS[n - 1]))
                    for t in s.v_tiles(m, nb):
                        v_transposes(s, t)
                head_sums(s, s.o0 + 7)
                pe.wait_ge(halo_ready, s.p + 1)
                pe.wait_ge(tp_free, tp[0])
                attend(s)
                pe.wait_ge(sc_free, s.a0 + len(s.units))
                pe.wait_ge(pt_done, s.a0 + len(s.units))
                if s.has_sample:
                    state_transposes(s)
                mix_start = tp[0]
                for n in range(s.nt - s.out1_early):
                    for t in range(2 * n, min(2 * n + 2, s.nt)):
                        mix_transposes(s, t)
                    out_tile(s, 1, s.out1_early + n)
                short = s.nt < max(NT)
                for j in (2, 3):
                    pe.wait_ge(split2, RING2 * s.p + 2 * (j - 1))
                    for t in range(s.nt):
                        if j == 2:
                            pe.wait_ge(tp_free, mix_start + t + 1)
                        for nh in range(2):
                            add_half(s, s.d_unit(j, 0), j % 2, t, nh, *out_operands(j))
                            if j == 3 and nh == 0 and t >= 2 and not (short and t == s.nt - 1):
                                norm_transposes(s, s.x0 + s.nt, t - 2)
                            if j == 3 and nh == 1 and short and t == s.nt - 2:
                                norm_transposes(s, s.x0 + s.nt, t - 1)
                norm_start = tp[0] - 2 * (s.nt - 2)
                if short:
                    norm_transposes(s, s.x0 + s.nt, s.nt - 2)
                pe.wait_ge(d_free, s.d_unit(OUT_GROUPS, 0) - 1)
                pe.wait_ge(tp_free, norm_start + 2 * -(-s.NB // PART))
                gate_up_unit(s, 0, 0, 0, 0, 0)
                if not short:
                    norm_transposes(s, s.x0 + s.nt, s.nt - 2)
                norm_transposes(s, s.x0 + s.nt, s.nt - 1)
                pe.wait_ge(d_free, s.d_unit(OUT_GROUPS, 0))
                gate_up_unit(s, 0, 0, 0, 1, 1)
                pe.wait_ge(tp_free, tp[0])
                gate_up(s, 0, first=1)
                with pe.Fori(0, LOOPS) as i:
                    gate_up(s, 2 * i + 1)
                    down(s, 2 * i, 0)
                    gate_up(s, 2 * i + 2)
                    down(s, 2 * i + 1, 1)
                gate_up(s, GROUPS - 2)
                down(s, GROUPS - 3, 0)
                gate_up(s, GROUPS - 1)
                down(s, GROUPS - 2, 1)
                prev = s
            boundary(prev, None)

        @block.scalar
        def _(act):
            steps, tp = [0], [0]

            def link(ins):
                steps[0] += 1
                ins.then_inc(act_step, 1)
                act.wait_ge(act_step, steps[0])

            def high1(s, block_id):
                b = block_id % 2
                act.wait_ge(raw1_loaded[b], 16 * s.loads1(block_id))
                nc.scalar.activation(w1_hi[:, b], raw1[:, b], ACT.Copy).then_inc(hi_done, 1)

            def high1_down(s, j):
                for c in range(2):
                    act.wait_ge(raw1_loaded[c], 16 * (s.loads1(DOWN_ID + c) + j))
                    nc.scalar.activation(w1_hi[:, c], raw1[:, c], ACT.Copy).then_inc(hi_done, 1)

            def high2(s, slots, use):
                for n in slots:
                    act.wait_ge(raw2_loaded[n], 16 * (USES2[n] * s.p + use + 1))
                    nc.scalar.activation(w2_hi[:, n], raw2[:, n], ACT.Copy).then_inc(hi_done, 1)

            def tp_copy(dst, src, scale=1.0):
                tp[0] += 1
                act.wait_ge(tp_ready, tp[0])
                nc.scalar.activation(dst, src, ACT.Copy, scale=scale).then_inc(tp_hi, 1)

            def tp_unit(k0, nk, tok):
                n = tok.stop - tok.start
                tp_copy(xt_hi[:, k0:k0 + nk, tok],
                        ps[:, 4 + tp[0] % 4, 0:nk * n].rearrange("p (k t) -> p k t", k=nk))

            def row_rstd(s, src, xi, c, t, tp_start):
                rows = s.rows[t]
                if t >= 2:
                    act.wait_ge(tp_ready, tp_start + 2 * (t - 1))
                link(nc.scalar.activation(xn[0:rows, xi % 2], src, ACT.Square,
                                          accum_out=ss[0:rows, c:c + 1]))
                link(nc.scalar.activation(ss[0:rows, c:c + 1], ss[0:rows, c:c + 1], ACT.Ln,
                                          bias=eps[0:rows, :], scale=1.0 / D_MODEL))
                nc.scalar.activation(rstd[0:rows, c:c + 1], ss[0:rows, c:c + 1], ACT.Exp,
                                     scale=-0.5).then_inc(rstd_ready, 1)

            def norm_copies(s, t):
                for half in range(2):
                    tp_unit(4 * half, 4, slice(PART * t, PART * t + s.rows[t]))

            def boundary(prev, s):
                tp_start = tp[0]
                if s:
                    nc.scalar.preload_act_table_set("natural_log_exp_and_others")
                def rstd_of(t):
                    src = h[0:s.rows[t], t]
                    if prev:
                        src = xload[0:s.rows[t], s.xi(t) % 2]
                        act.wait_ge(x_loaded[s.xi(t) % 2], 16 * (s.xi(t) // 2 + 1))
                    else:
                        act.wait_ge(h_loaded[t], 16)
                    row_rstd(s, src, s.x0 + t, t, t, tp_start)

                if s:
                    rstd_of(0)
                    rstd_of(1)
                for t in range(1 + max(prev.nt if prev else 0, s.nt if s else 0)):
                    if s and prev and t < 2:
                        if t == 0:
                            act.wait_ge(d_ready, prev.d_unit(D_GROUPS - 1, 0))
                        high1(s, t)
                    if s and t < s.nt:
                        norm_copies(s, t)
                    if s and t + 2 < s.nt:
                        rstd_of(t + 2)
                    if prev and 1 <= t <= prev.nt:
                        act.wait_ge(d_free, prev.d_unit(D_GROUPS - 1, t))
                        act.dma_start(tile_dram(y_prompt, y_sample, TILE0[prev.p] + t - 1),
                                      h[0:prev.rows[t - 1], t - 1]).then_inc(y_stored[t - 1], 16)

            def slab_read(s, m, nb):
                unit_read(s, m, nb)
                next_weights(s, m, nb)

            def next_weights(s, m, nb):
                if nb == 1 and m + 2 < len(SLABS):
                    high1(s, m + 2)
                elif nb == 1 and m + 1 == len(SLABS):
                    high1(s, OUT_ID)
                    high1(s, OUT_ID + 1)

            def unit_read(s, m, nb):
                kind, j, _ = SLABS[m]
                zi, oi = s.z_unit(m, nb), s.oi(m, nb)
                z = ps[:, zi % 2, 0:s.NB]
                act.wait_ge(z_ready, zi + 1)
                if kind == "v":
                    nc.scalar.activation(vt_sb[:, 1, nb * s.NB:(nb + 1) * s.NB], z, ACT.Copy)\
                        .then_inc(z_free, 1)
                    return
                if kind == "u":
                    for a, e in s.cuts(nb):
                        last = nc.scalar.activation(ut_sb[:, j, s.ucol(a):s.ucol(a) + e - a],
                                                    z[:, a - nb * s.NB:e - nb * s.NB], ACT.Copy)
                    last.then_inc(z_free, 1)
                    return
                need(act, ss_ready, oi - 1)
                nc.scalar.activation(sq[:, oi % 2, 0:s.NB], z, ACT.Square).then_inc(sq_ready, 1)
                if kind == "k":
                    need(act, fin_done, oi - 1)
                    if j == 1:
                        nc.scalar.activation(vt_sb[:, 0, nb * s.NB:(nb + 1) * s.NB], z, ACT.Copy)
                    dst, scale = zs[:, oi % 2, 0:s.NB], kg[:, :]
                else:
                    g = j // 2
                    if g >= 2:
                        act.wait_ge(qk_ready, s.a0 + s.nt * (g - 1))
                    dst, scale = qt_sb[:, g % 2, j % 2, nb * s.NB:(nb + 1) * s.NB], qg[:, :]
                nc.scalar.activation(dst, z, ACT.Copy, scale=scale).then_inc(z_free, 1)
                if not s.whole(oi):
                    act.wait_ge(sq_ready, oi + 1)
                    need(act, ss_ready, oi)
                    nc.scalar.activation(sq_hi[:, 0:s.NB], sq[:, oi % 2, 0:s.NB], ACT.Copy).then_inc(sq_high, 1)

            def head_rstd(s, oi):
                act.wait_ge(ss_ready, oi + 1)
                need(act, fin_done, oi - 1)
                r = rr[:, oi % 2, 0:s.NB]
                nc.scalar.activation(r, ps[:, 2, 0:s.NB], ACT.Ln, bias=eps[:, :],
                                     scale=1.0 / HD).then_inc(ss_free, 1)
                act.wait_ge(ss_free, oi + 1)
                nc.scalar.activation(r, r, ACT.Exp, scale=-0.5).then_inc(r_ready, 1)

            def v_copy(s, t):
                tp_copy(v_sb[0:s.rows[t], s.slot(t), 0:KV_DIM // 2],
                        ps[0:s.rows[t], 4 + tp[0] % 4, HD:HD + KV_DIM // 2])

            def exps(s, n):
                ai, rows = s.a0 + n, s.rows[s.units[n][1]]
                c0, c1 = s.keys(s.units[n][1])
                act.wait_ge(nm_ready, ai + 1)
                for hh in range(GQA):
                    p = s_sb[0:rows, ai % 2, hh, c0:c1]
                    nc.scalar.activation(p, p, ACT.Exp, bias=negmax[0:rows, ai % 2, hh:hh + 1],
                                         accum_out=den[0:rows, ai % 2, hh:hh + 1])
                nc.scalar.activation(esink[0:rows, ai % 2, :], esink[0:rows, ai % 2, :],
                                     ACT.Exp).then_inc(e_ready, 1)

            def prob_copy(s, n):
                ai, rows = s.a0 + n, s.rows[s.units[n][1]]
                c0, c1 = s.keys(s.units[n][1])
                act.wait_ge(pt_ready, ai + 1)
                need(act, pv_ready, ai - 1)
                if c1 - c0 == 2 * PART:
                    pieces = [(slice(0, PART), slice(0, 2))]
                else:
                    pieces = [(slice(0, min(c1, PART * (half + 1)) - PART * half), slice(half, half + 1))
                              for half in range(2) if c0 < PART * (half + 1)]
                for keys, halves in pieces:
                    last = nc.scalar.activation(
                        pt_sb[keys, ai % 2, halves, 0:GQA * rows],
                        ps[keys, slice(6 + halves.start, 6 + halves.stop), 0:GQA * rows], ACT.Copy)
                last.then_inc(pt_done, 1)

            def pool_high(s, b):
                for nb in range(2):
                    mi = 4 * s.p + 2 * b + nb
                    act.wait_ge(m_ready, mi + 1)
                    nc.scalar.activation(xt_hi[:, b, nb * s.NB:(nb + 1) * s.NB], ps[:, mi % 2, 0:s.NB],
                                         ACT.Copy, scale=pscale[:, b:b + 1]).then_inc(m_hi, 1)

            def late_rstd(s, n):
                d = s.late_unit(n - 1)
                if d is not None:
                    head_rstd(s, s.o0 + 8 + d)

            def late_read(s, n):
                d = s.late_unit(n)
                if d is not None:
                    slab_read(s, EARLY + d // 2, d % 2)

            def attend(s):
                last = len(s.units) - 1
                late_read(s, -1)
                exps(s, 0)
                late_read(s, 0)
                head_rstd(s, s.o0 + 8)
                for n in range(last + 1):
                    if n == s.mix_at:
                        pool_high(s, 0)
                    if s.dense_first(n):
                        late_rstd(s, n)
                        exps(s, n + 1)
                        late_read(s, n)
                    if n == 1:
                        late_read(s, n)
                        late_rstd(s, n)
                    prob_copy(s, n)
                    t = n - s.out_at
                    if 0 <= t < s.nt:
                        act.wait_ge(group0_ready, s.x0 // 2 + t + 1)
                        tok = slice(PART * t, PART * t + s.rows[t])
                        nc.scalar.activation(xt_hi[:, 2:4, tok],
                                             ps[:, 2, 0:2 * s.rows[t]].rearrange("p (k t) -> p k t", k=2),
                                             ACT.Copy).then_inc(group0_hi, 1)
                    if n < last and not s.dense_first(n):
                        exps(s, n + 1)
                    if n >= s.mix_at:
                        late_rstd(s, n)
                    if n == s.mix_at:
                        pool_high(s, 1)
                    if t == s.nt - 1:
                        act.wait_ge(d_ready, s.d_unit(1, 0))
                        for c in range(2):
                            high1(s, OUT_ID + 2 + c)

            def gates(s, j, parity, begin=None, bank0=4):
                if begin != "first":
                    act.wait_ge(d_ready, s.d0 + s.d_of * (OUT_GROUPS - 1 + j))
                    high1_down(s, j - 1)
                for n in range(4):
                    gi = s.g0 + 4 * j + n
                    act.wait_ge(g_ready, gi + 1)
                    need(act, a_done, gi - 1)
                    nc.scalar.activation(sg[:, n % 2, 0:s.NB], ps[:, bank0 if n == 0 else 4 + n % 2, 0:s.NB],
                                         ACT.Silu).then_inc(silu_done, 1)
                    if n == 2:
                        high2(s, (0, 1), 1 + j + 1)
                    if n >= 1:
                        high_part(s, j, n - 1, parity)
                high_part(s, j, 3, parity)
                if begin != "last":
                    act.wait_ge(u_ready, s.g0 + 4 * j + 4)
                    high2(s, (2, 3), 1 + j + 1)

            def high_part(s, j, n, parity):
                act.wait_ge(a_done, s.g0 + 4 * j + n + 1)
                nc.scalar.activation(act_hi[:, parity, n // 2, (n % 2) * s.NB:(n % 2 + 1) * s.NB],
                                     aa[:, n % 2, 0:s.NB], ACT.Copy).then_inc(ah_done, 1)

            def state_copies(s):
                for n, rows in enumerate((PART, DEC)):
                    tp_copy(k_st[0:rows, KV_DIM * n:KV_DIM * n + 2 * HD].rearrange("p (g d) -> p g d", g=2),
                            ps[0:rows, 4 + tp[0] % 4, 0:2 * PART]
                            .rearrange("p (g d) -> p g d", g=2)[:, :, 0:HD])
                tp_copy(u_st[0:HIST, 0:POOL_DIM], ps[0:HIST, 4 + tp[0] % 4, 0:POOL_DIM])

            def store_states(s):
                act.wait_ge(tp_free, state_read(s))
                act.dma_start(nk_prompt[0, 0].rearrange("r g d -> r (g d)"), k_st[:, 0:KV_DIM])\
                    .then_inc(state_stored, 16)
                act.dma_start(nk_sample[0, 0, PART - DEC:PART].rearrange("r g d -> r (g d)"),
                              k_st[0:DEC, KV_DIM:2 * KV_DIM]).then_inc(state_stored, 16)
                act.dma_start(nk_sample[0, 0, 0:PART - DEC], cache_k[0, 0, DEC:PART])\
                    .then_inc(state_stored, 16)
                act.dma_start(nv_sample[0, 0, 0:PART - DEC], cache_v[0, 0, DEC:PART])\
                    .then_inc(state_stored, 16)
                act.dma_start(nv_prompt[0, 0].rearrange("r g d -> r (g d)"), v_tail[:, :])\
                    .then_inc(state_stored, 16)
                act.dma_start(nv_sample[0, 0, PART - DEC:PART].rearrange("r g d -> r (g d)"),
                              k_st[0:DEC, 2 * KV_DIM:3 * KV_DIM]).then_inc(state_stored, 16)
                act.dma_start(np_prompt[0, 0], u_st[0:HIST, 0:POOL_DIM]).then_inc(state_stored, 16)
                act.dma_start(np_sample[0, 0], u_st[0:HIST, POOL_DIM:2 * POOL_DIM])\
                    .then_inc(state_stored, 16)

            act.wait_ge(const_ready, 1)
            prev = None
            for s in shapes:
                boundary(prev, s)
                if s.p == 0:
                    act.wait_ge(const_ready, 3)
                    nc.scalar.activation(headsum_r[:, :], headsum[:, :], ACT.Copy).then_inc(headsum_ready, 1)
                for m, nb in FIRST_UNITS:
                    slab_read(s, m, nb)
                if s.has_sample:
                    c0 = PART * (s.slot(4) - 1)
                    for g in range(N_KV):
                        tp_copy(kt_sb[0:HD, g, c0:c0 + PART], ps[0:HD, 4 + tp[0] % 4, 0:PART])
                    u0 = s.ucol(s.T - DEC) - HIST
                    tp_copy(ut_sb[:, 0, u0:u0 + HIST], ps[:, 4 + tp[0] % 4, 0:HIST])
                for n, (m, nb) in enumerate(EARLY_UNITS):
                    unit_read(s, m, nb)
                    if n > 0 and EARLY_UNITS[n - 1][0] != V_SLAB:
                        head_rstd(s, s.oi(*EARLY_UNITS[n - 1]))
                    for t in s.v_tiles(m, nb):
                        v_copy(s, t)
                    if n + 1 < len(EARLY_UNITS):
                        next_weights(s, m, nb)
                head_rstd(s, s.o0 + 7)
                next_weights(s, *EARLY_UNITS[-1])
                attend(s)
                if s.has_sample:
                    state_copies(s)
                for t in range(s.nt):
                    tp_unit(4, 4, slice(PART * t, PART * t + s.rows[t]))
                    if t == 3:
                        high2(s, (0, 1), 0)
                high2(s, (2, 3), 0)
                if s.has_sample:
                    store_states(s)
                act.wait_ge(d_ready, s.d_unit(3, 0))
                high2(s, (0, 1), 1)
                tp_start = tp[0]
                for t in range(s.nt):
                    act.wait_ge(d_free, s.d_unit(3, t) + 2)
                    row_rstd(s, h[0:s.rows[t], t], s.x0 + s.nt + t, 8 + t, t, tp_start)
                    if t >= 1:
                        norm_copies(s, t - 1)
                high2(s, (2, 3), 1)
                norm_copies(s, s.nt - 1)
                nc.scalar.preload_act_table(ACT.Silu)
                if s.has_sample:
                    act.wait_ge(state_stored, 16 * 8)
                gates(s, 0, 0, "first", bank0=0)
                with act.Fori(0, LOOPS) as i:
                    gates(s, 2 * i + 1, 1)
                    gates(s, 2 * i + 2, 0)
                gates(s, GROUPS - 2, 1)
                gates(s, GROUPS - 1, 0, "last")
                prev = s
            boundary(prev, None)
            for t in range(6):
                act.wait_ge(y_stored[t], 16 * sum(t < n for n in NT))

        @block.vector
        def _(dve):
            steps, tp = [0], [0]

            def link(ins):
                steps[0] += 1
                ins.then_inc(dve_step, 1)
                dve.wait_ge(dve_step, steps[0])

            def tp_wait():
                tp[0] += 1
                dve.wait_ge(tp_hi, tp[0])
                return ps[:, 4 + (tp[0] - 1) % 4]

            def low(k0, nk, tok, bank, done, for_out=False):
                n = tok.stop - tok.start
                src = bank[:, 0:nk * n].rearrange("p (k t) -> p k t", k=nk)
                hi = xt_hi[:, k0:k0 + nk, tok].bitcast(F32)
                if for_out and n < PART:
                    nc.vector.tensor_tensor(xt_hi[:, k0:k0 + nk, tok.stop:tok.stop + n], src, hi, ALU.subtract)
                nc.vector.tensor_tensor(xt_lo[:, k0:k0 + nk, tok], src, hi, ALU.subtract).then_inc(done, 1)

            def tp_unit(k0, nk, tok, for_out=False):
                low(k0, nk, tok, tp_wait(), tp_free, for_out)

            def norm_low(s, t):
                for half in range(2):
                    tp_unit(4 * half, 4, slice(PART * t, PART * t + s.rows[t]))

            def normalise(s, src, xi, c, t, weight):
                rows = s.rows[t]
                dve.wait_ge(rstd_ready, xi + 1)
                nc.vector.scalar_tensor_tensor(xn[0:rows, xi % 2], src, rstd[0:rows, c:c + 1],
                                               weight[0:rows, :], ALU.mult, ALU.mult).then_inc(xn_ready, 1)

            def accumulate_unit(s, group, bank, t, nh):
                rows, cols = s.rows[t], slice(512 * nh, 512 * (nh + 1))
                dve.wait_ge(d_ready, s.d_unit(group, t, nh) + 1)
                out = h[0:rows, t, cols]
                if rows < PART:
                    nc.vector.tensor_tensor(out, ps[rows:2 * rows, bank, :], out, ALU.add).then_inc(half_sum, 1)
                    dve.wait_ge(half_sum, 2 * group + nh + 1)
                nc.vector.tensor_tensor(out, ps[0:rows, bank, :], out, ALU.add).then_inc(d_free, 1)

            def accumulate_tile(s, group, parity, t):
                for nh in range(2):
                    accumulate_unit(s, group, s.bank(parity, t, nh), t, nh)

            def out_sums(s, j, t):
                for nh in range(2):
                    accumulate_unit(s, j, nh, t, nh)

            def accumulate(s, group, parity):
                for t in range(s.nt):
                    accumulate_tile(s, group, parity, t)

            def boundary(prev, s):
                for t in range(max(prev.nt if prev else 0, s.nt if s else 0)):
                    if prev and t < prev.nt:
                        accumulate_tile(prev, D_GROUPS - 1, 0, t)
                    if s and t < s.nt:
                        norm_low(s, t)
                    if s and t + 2 < s.nt:
                        first_normalise(prev, s, t + 2)

            def first_normalise(prev, s, t):
                src = xload[0:s.rows[t], s.xi(t) % 2] if prev else h[0:s.rows[t], t]
                normalise(s, src, s.x0 + t, t, t, g_mix)

            def normed(s, m, nb):
                kind, j, _ = SLABS[m]
                oi = s.oi(m, nb)
                dve.wait_ge(r_ready, oi + 1)
                dve.wait_ge(z_free, s.z_unit(m, nb) + 1)
                r = rr[:, oi % 2, 0:s.NB]
                if kind == "q":
                    q = qt_sb[:, j // 2 % 2, j % 2, nb * s.NB:(nb + 1) * s.NB]
                    nc.vector.tensor_tensor(q, q, r, ALU.mult).then_inc(fin_done, 1)
                    return
                z = zs[:, oi % 2, 0:s.NB]
                for g in ((0, 1), (2,))[j]:
                    src = slice(HD * (g % 2), HD * (g % 2 + 1))
                    for e in range(2):
                        for a, b in s.cuts(nb):
                            cols = slice(a - nb * s.NB, b - nb * s.NB)
                            last = nc.vector.tensor_tensor(
                                kt_sb[HD * e:HD * (e + 1), g, s.kcol(a):s.kcol(a) + b - a],
                                z[src, cols], r[src, cols], ALU.mult)
                last.then_inc(fin_done, 1)

            def squares_low(s, m, nb):
                if s.whole(s.oi(m, nb)):
                    return
                oi = s.oi(m, nb)
                dve.wait_ge(sq_high, s.splits(oi) + 1)
                nc.vector.tensor_tensor(sq_lo[:, 0:s.NB], sq[:, oi % 2, 0:s.NB], sq_hi[:, 0:s.NB].bitcast(F32),
                                        ALU.subtract).then_inc(sq_low, 1)

            def restore_tails(s):
                if s.p == 0:
                    nc.vector.memset(ut_sb[:, :, 0:HALO], 0.0).then_inc(halo_ready, 1)
                    return
                nc.vector.tensor_copy(kt_sb[:, :, 0:PART], k_tail[:, :, :])
                nc.vector.tensor_copy(v_sb[:, 0, :], v_tail[:, :])
                nc.vector.tensor_copy(ut_sb[:, :, 0:HALO], u_tail[:, 0]).then_inc(halo_ready, 1)

            def save_tails(s):
                end = s.T - (DEC if s.has_sample else 0)
                dve.wait_ge(fin_done, s.o0 + 4)
                nc.vector.tensor_copy(k_tail[:, :, :], kt_sb[:, :, end:end + PART])
                nc.vector.tensor_copy(v_tail[:, :], v_sb[:, end // PART, :])
                if s.has_sample:
                    c = s.ucol(s.T - DEC) + DEC
                    nc.vector.tensor_copy(u_tail[:, 1], ut_sb[:, :, c - HALO:c])
                nc.vector.tensor_copy(u_tail[:, 0], ut_sb[:, :, end:end + HALO]).then_inc(tails_saved, 1)

            def pool_means(s, b):
                n = HALO + s.T + (HALO if s.has_sample else 0)
                dve.wait_ge(windows_ready, 2 * s.p + b + 1)
                dve.wait_ge(tails_saved, s.p + 1)
                for half in range(2):
                    rows = slice(HD * half, HD * (half + 1))
                    last = nc.vector.scalar_tensor_tensor(
                        ut_sb[rows, b, HALO:n], win[rows, half, HALO:n], 1.0 / POOL_WINDOWS[2 * b + half],
                        ut_sb[rows, b, HALO:n], ALU.mult, ALU.subtract)
                last.then_inc(windows_used, 1)

            def pool_low(s, b):
                for nb in range(2):
                    mi, tok = 4 * s.p + 2 * b + nb, slice(nb * s.NB, (nb + 1) * s.NB)
                    dve.wait_ge(m_hi, mi + 1)
                    if s.has_sample and nb == 1:
                        nc.vector.scalar_tensor_tensor(xt_hi[:, b, s.T:s.T + DEC], ps[:, mi % 2, s.NB - DEC:s.NB],
                                                       pscale[:, b:b + 1],
                                                       xt_hi[:, b, s.T - DEC:s.T].bitcast(F32), ALU.mult,
                                                       ALU.subtract)
                    nc.vector.scalar_tensor_tensor(xt_lo[:, b, tok], ps[:, mi % 2, 0:s.NB], pscale[:, b:b + 1],
                                                   xt_hi[:, b, tok].bitcast(F32), ALU.mult,
                                                   ALU.subtract).then_inc(m_free, 1)

            def softmax_top(s, n):
                g, t = s.units[n]
                ai, rows = s.a0 + n, s.rows[t]
                c0, c1 = s.keys(t)
                b = ai % 2
                dve.wait_ge(qk_ready, ai + 1)
                need(dve, pt_ready, ai - 1)
                need(dve, e_ready, ai - 1)
                for hh in range(GQA):
                    e, j = hh % 2, hh // 2
                    last = nc.vector.scalar_tensor_tensor(
                        s_sb[0:rows, b, hh, c0:c1], dist[0:rows, c0:c1], SLOPES[GQA * g + hh],
                        ps[0:rows, 4 + e, 256 * j + c0:256 * j + c1], ALU.mult, ALU.add)
                last.then_inc(sc_free, 1)
                dve.wait_ge(sc_free, ai + 1)
                link(nc.vector.tensor_reduce(negmax[0:rows, b, :], s_sb[0:rows, b, :, c0:c1], AX.X, ALU.max,
                                             negate=True))
                link(nc.vector.tensor_tensor(negmax[0:rows, b, :], negmax[0:rows, b, :],
                                             nsink[0:rows, GQA * g:GQA * (g + 1)], ALU.min))
                nc.vector.tensor_tensor(esink[0:rows, b, :], negmax[0:rows, b, :],
                                        sink[0:rows, GQA * g:GQA * (g + 1)], ALU.add).then_inc(nm_ready, 1)

            def denominators(s, n):
                ai, rows = s.a0 + n, s.rows[s.units[n][1]]
                b = ai % 2
                dve.wait_ge(e_ready, ai + 1)
                link(nc.vector.tensor_tensor(den[0:rows, b, :], den[0:rows, b, :], esink[0:rows, b, :], ALU.add))
                link(nc.vector.reciprocal(rden[0:rows, b, :], den[0:rows, b, :]))

            def outputs(s, n):
                g, t = s.units[n]
                ai, rows = s.a0 + n, s.rows[t]
                dve.wait_ge(pv_ready, ai + 1)
                cols = slice(GQA * HD * g, GQA * HD * (g + 1))
                nc.vector.tensor_tensor(atok[0:rows, t, cols].rearrange("p (h d) -> p h d", h=GQA),
                                        ps[0:rows, 3, 0:GQA * HD].rearrange("p (h d) -> p h d", h=GQA),
                                        rden[0:rows, ai % 2, :].unsqueeze(2).to_broadcast([rows, GQA, HD]),
                                        ALU.mult).then_inc(o_done, 1)

            def out1_low(s):
                for c in range(2):
                    dve.wait_ge(hi_done, HI_BLOCKS * s.p + order1(OUT_ID) + 2 + c + 1)
                    nc.vector.tensor_tensor(w1_lo[:, c], raw1[:, c], w1_hi[:, c].bitcast(F32), ALU.subtract)\
                        .then_inc(split1, 1)

            def group0_low(s, t):
                tok = slice(PART * t, PART * t + s.rows[t])
                dve.wait_ge(group0_hi, s.x0 // 2 + t + 1)
                low(2, 2, tok, ps[:, 2], group0_free, for_out=True)

            def late_normed(s, n):
                d = s.late_unit(n - 1)
                if d is not None:
                    normed(s, EARLY + d // 2, d % 2)

            def attend(s):
                last = len(s.units) - 1
                for n in range(last + 1):
                    if n < last:
                        softmax_top(s, n + 1)
                    if s.dense_first(n):
                        late_normed(s, n)
                    if n == s.mix_at:
                        pool_low(s, 0)
                    denominators(s, n)
                    t = n - s.out_at
                    if 0 <= t < s.nt:
                        group0_low(s, t)
                    if n >= 1:
                        outputs(s, n - 1)
                    if not s.dense_first(n):
                        late_normed(s, n)
                    if n == s.mix_at:
                        pool_low(s, 1)
                    if 0 <= t < s.nt:
                        dve.wait_ge(h_loaded[t], 16 * (s.p + 1))
                    if t >= 0:
                        out_sums(s, *divmod(t, s.nt))
                    if t == s.nt - 1:
                        out1_low(s)
                    if n in MEANS_AT:
                        pool_means(s, MEANS_AT.index(n))
                outputs(s, last)

            def activations(s, j, parity, bank0=6):
                for n in range(4):
                    gi = s.g0 + 4 * j + n
                    dve.wait_ge(silu_done, gi + 1)
                    dve.wait_ge(u_ready, gi + 1)
                    need(dve, ah_done, gi - 1)
                    need(dve, al_done, gi - 1)
                    nc.vector.tensor_tensor(aa[:, n % 2, 0:s.NB], ps[:, bank0 if n == 0 else 6 + n % 2, 0:s.NB],
                                            sg[:, n % 2, 0:s.NB], ALU.mult).then_inc(a_done, 1)
                    if n >= 1:
                        low_part(s, j, n - 1, parity)
                low_part(s, j, 3, parity)

            def low_part(s, j, n, parity):
                dve.wait_ge(ah_done, s.g0 + 4 * j + n + 1)
                at = (slice(None), parity, n // 2, slice((n % 2) * s.NB, (n % 2 + 1) * s.NB))
                if s.has_sample and n % 2 == 1:
                    nc.vector.tensor_tensor(act_hi[:, parity, n // 2, s.T:s.T + DEC], aa[:, 1, s.NB - DEC:s.NB],
                                            act_hi[:, parity, n // 2, s.T - DEC:s.T].bitcast(F32), ALU.subtract)
                nc.vector.tensor_tensor(act_lo[at], aa[:, n % 2, 0:s.NB], act_hi[at].bitcast(F32),
                                        ALU.subtract).then_inc(al_done, 1)

            nc.vector.memset(eps[:, :], EPS).then_inc(const_ready, 1)
            link(nc.vector.memset(u_tail[:, :, :, :], 0.0))
            dve.wait_ge(gmix_loaded, 16)
            prev = None
            for t in range(2):
                first_normalise(None, shapes[0], t)
            for s in shapes:
                boundary(prev, s)
                restore_tails(s)
                if s.p == 0:
                    dve.wait_ge(const_loaded, 16 * N_CONST)
                    nc.vector.tensor_scalar(nsink[:, :], sink[:, :], -1.0, None, ALU.mult)\
                        .then_inc(const_ready, 1)
                    nc.vector.tensor_scalar(qg[:, :], qg[:, :], HD ** -0.5, None, ALU.mult)\
                        .then_inc(const_ready, 1)
                if s.has_sample:
                    c0 = PART * (s.slot(4) - 1)
                    for g in range(N_KV):
                        bank = tp_wait()
                        nc.vector.tensor_copy(kt_sb[HD:PART, g, c0:c0 + PART], bank[HD:PART, 0:PART])\
                            .then_inc(tp_free, 1)
                    u0 = s.ucol(s.T - DEC) - HIST
                    nc.vector.memset(ut_sb[:, :, u0 - 1:u0], 0.0)
                    bank = tp_wait()
                    nc.vector.tensor_copy(ut_sb[:, 1, u0:u0 + HIST], bank[:, HALO:HALO + HIST])\
                        .then_inc(tp_free, 1)
                for n, (m, nb) in enumerate(EARLY_UNITS):
                    if m != V_SLAB:
                        squares_low(s, m, nb)
                    if n > 0 and EARLY_UNITS[n - 1][0] != V_SLAB:
                        normed(s, *EARLY_UNITS[n - 1])
                    for t in s.v_tiles(m, nb):
                        bank = tp_wait()
                        nc.vector.tensor_copy(v_sb[0:s.rows[t], s.slot(t), KV_DIM // 2:KV_DIM],
                                              bank[0:s.rows[t], HD + KV_DIM // 2:HD + KV_DIM])\
                            .then_inc(tp_free, 1)
                normed(s, *EARLY_UNITS[-1])
                softmax_top(s, 0)
                save_tails(s)
                attend(s)
                if s.has_sample:
                    nc.vector.tensor_copy(k_st[0:DEC, 2 * KV_DIM:3 * KV_DIM], v_sb[0:DEC, s.slot(4), :])
                    for n, rows in enumerate((PART, DEC)):
                        bank = tp_wait()
                        nc.vector.tensor_copy(k_st[0:rows, KV_DIM * n + 2 * HD:KV_DIM * (n + 1)],
                                              bank[0:rows, 2 * PART:2 * PART + HD]).then_inc(tp_free, 1)
                    bank = tp_wait()
                    nc.vector.tensor_copy(u_st[0:HIST, POOL_DIM:2 * POOL_DIM],
                                          bank[0:HIST, POOL_DIM:2 * POOL_DIM]).then_inc(tp_free, 1)
                for n in range(s.nt - s.out1_early):
                    for t in range(2 * n, min(2 * n + 2, s.nt)):
                        tp_unit(4, 4, slice(PART * t, PART * t + s.rows[t]), for_out=True)
                    out_sums(s, 1, s.out1_early + n)
                accumulate(s, 2, 0)
                for t in range(s.nt):
                    accumulate_unit(s, 3, s.bank(1, t, 0), t, 0)
                    if t >= 1:
                        normalise(s, h[0:s.rows[t - 1], t - 1], s.x0 + s.nt + t - 1, 8 + t - 1, t - 1, g_ffn)
                    if t == s.nt - 1:
                        norm_low(s, t - 2)
                    accumulate_unit(s, 3, s.bank(1, t, 1), t, 1)
                    if 2 <= t < s.nt - 1:
                        norm_low(s, t - 2)
                t = s.nt - 1
                normalise(s, h[0:s.rows[t], t], s.x0 + s.nt + t, 8 + t, t, g_ffn)
                norm_low(s, t - 1)
                norm_low(s, t)
                activations(s, 0, 0, bank0=1)
                with dve.Fori(0, LOOPS) as i:
                    activations(s, 2 * i + 1, 1)
                    accumulate(s, OUT_GROUPS + 2 * i, 0)
                    activations(s, 2 * i + 2, 0)
                    accumulate(s, OUT_GROUPS + 2 * i + 1, 1)
                activations(s, GROUPS - 2, 1)
                accumulate(s, D_GROUPS - 3, 0)
                activations(s, GROUPS - 1, 0)
                for t in range(s.nt):
                    accumulate_tile(s, D_GROUPS - 2, 1, t)
                    if t in (1, 3) and s.p + 1 < PARTS:
                        first_normalise(s, shapes[s.p + 1], t // 2)
                prev = s
            boundary(prev, None)


def constants():
    row, col = np.arange(PART)[:, None], np.arange(2 * PART)[None, :]
    chunk = (row // 64) * 64
    valid = (col >= chunk) & (col < chunk + PART + 64)
    dist = np.where(valid, -np.abs(row + PART - col), -1e30 / SLOPES[-1]).astype(np.float32)
    ident = np.eye(PART, dtype=np.float32)
    heads = np.kron(np.eye(2, dtype=np.float32), np.ones((HD, HD), np.float32))
    width = np.repeat(np.array(POOL_WINDOWS, np.float32), 64).reshape(2, PART).T[:, :, None]
    count = np.minimum(np.arange(1, HALO + 1, dtype=np.float32)[None, None, :], width)
    return {"c_dist": dist, "c_ident": ident, "c_ones": heads, "c_inv": (width / count).astype(np.float32)}


_INS = ['x_prompt', 'x_sample', 'cache_pool', 'cache_k', 'cache_v', 'norm_mix', 'w_in', 'w_pool', 'pool_scale',
        'q_norm', 'k_norm', 'sinks', 'w_out', 'norm_ffn', 'w_gate', 'w_up', 'w_down']
_OUTS = [(1, 2048, 1024), (1, 64, 1024), (1, 1, 15, 256), (1, 1, 128, 3, 64), (1, 1, 128, 3, 64),
         (1, 1, 15, 256), (1, 1, 128, 3, 64), (1, 1, 128, 3, 64)]


def kernel(**inputs):
    import concourse.bacc as bacc
    from concourse.bass_utils import run_bass_kernel_spmd

    nc = bacc.Bacc("TRN2", target_bir_lowering=False, num_devices=1)
    arrays, args = {}, []
    given = {name: np.ascontiguousarray(inputs[name]) for name in _INS} | constants()
    for name, a in given.items():
        arrays[f"in_{name}"] = a
        args.append(nc.dram_tensor(f"in_{name}", a.shape, mybir.dt.from_np(a.dtype), kind="ExternalInput").ap())
    for i, shape in enumerate(_OUTS):
        args.append(nc.dram_tensor(f"out_{i}", shape, F32, kind="ExternalOutput").ap())
    build(nc, *args)
    r = run_bass_kernel_spmd(nc, [arrays], core_ids=[0])
    return tuple(r.results[0][f"out_{i}"] for i in range(len(_OUTS)))
```
